# Optimizing a Trainium2 kernel written in Bass

```python
import jax, jax.numpy as jnp
from jax import lax
import numpy as np
import math

D_MODEL = 1024
BATCH = 1
SEQ = 512
DEPTH = 1

CHUNK = 64
N_MEM = 256
HEAD_DIM = 64
FOX_HEADS = 8
CHUNK_HEADS = 8
FOX_WIDTH = FOX_HEADS * HEAD_DIM
CHUNK_WIDTH = CHUNK_HEADS * HEAD_DIM
IN_COLS = 3 * FOX_WIDTH + FOX_HEADS + 3 * CHUNK_WIDTH
Q_BLOCK = 128
LEFT_CHUNKS = 8
REL_CLIP = 128
NUM_REL = CHUNK + REL_CLIP
MEM_HEADS = 4
MEM_HEAD_DIM = D_MODEL // MEM_HEADS
D_FF = -(-8 * D_MODEL // 768) * 256
EPS = 1e-6
NEG_INF = -1e30


def rms_norm(x, g):
    xf = x.astype(jnp.float32)
    y = xf * lax.rsqrt(jnp.mean(xf * xf, axis=-1, keepdims=True) + EPS)
    return (y * g.astype(jnp.float32)).astype(x.dtype)

def fox_attention(q, k, v, log_f):
    B, S, H, D = q.shape
    nb = S // Q_BLOCK
    scale = D ** -0.5
    c = lax.cumsum(log_f, axis=1)
    c_keys = jnp.transpose(c, (0, 2, 1))
    k_pos = jnp.arange(S)
    q_blocks = jnp.transpose(q.reshape(B, nb, Q_BLOCK, H, D), (1, 0, 2, 3, 4))
    c_blocks = jnp.transpose(c.reshape(B, nb, Q_BLOCK, H), (1, 0, 3, 2))

    def one_block(args):
        i, q_i, c_i = args
        q_pos = i * Q_BLOCK + jnp.arange(Q_BLOCK)
        s = jnp.einsum('bqhd,bkhd->bhqk', q_i, k).astype(jnp.float32) * scale
        s = s + c_i[..., :, None] - c_keys[:, :, None, :]
        s = jnp.where((k_pos[None, :] <= q_pos[:, None])[None, None], s, NEG_INF)
        p = jax.nn.softmax(s, axis=-1)
        return jnp.einsum('bhqk,bkhd->bqhd', p.astype(v.dtype), v)

    out = lax.map(one_block, (jnp.arange(nb), q_blocks, c_blocks))
    return jnp.transpose(out, (1, 0, 2, 3, 4)).reshape(B, S, H, D)

def chunked_rel_attention(q, k, v, rel_bias):
    B, S, H, D = q.shape
    nc = S // CHUNK
    band = (LEFT_CHUNKS + 1) * CHUNK
    pad = LEFT_CHUNKS * CHUNK
    scale = D ** -0.5
    kp = jnp.pad(k, ((0, 0), (pad, 0), (0, 0), (0, 0)))
    vp = jnp.pad(v, ((0, 0), (pad, 0), (0, 0), (0, 0)))
    idx = (jnp.arange(nc) * CHUNK)[:, None] + jnp.arange(band)[None, :]
    k_band = kp[:, idx]
    v_band = vp[:, idx]
    q_c = q.reshape(B, nc, CHUNK, H, D)
    s = jnp.einsum('bnqhd,bnkhd->bhnqk', q_c, k_band).astype(jnp.float32) * scale
    dist = jnp.arange(CHUNK)[:, None] + pad - jnp.arange(band)[None, :]
    rel_idx = jnp.clip(dist, -(CHUNK - 1), REL_CLIP) + (CHUNK - 1)
    bias = rel_bias.astype(jnp.float32)[:, rel_idx]
    s = s + bias[None, :, None]
    valid = (idx - pad) >= 0
    s = jnp.where(valid[None, None, :, None, :], s, NEG_INF)
    p = jax.nn.softmax(s, axis=-1)
    o = jnp.einsum('bhnqk,bnkhd->bnqhd', p.astype(v.dtype), v_band)
    return o.reshape(B, S, H, D)

def memory_cross_attention(h, m, w_q, w_kv, w_o):
    B, S, _ = h.shape
    q = (h @ w_q).reshape(B, S, MEM_HEADS, MEM_HEAD_DIM)
    k, v = jnp.split(m @ w_kv, 2, axis=-1)
    k = k.reshape(B, N_MEM, MEM_HEADS, MEM_HEAD_DIM)
    v = v.reshape(B, N_MEM, MEM_HEADS, MEM_HEAD_DIM)
    s = jnp.einsum('bshd,bmhd->bhsm', q, k).astype(jnp.float32) * (MEM_HEAD_DIM ** -0.5)
    p = jax.nn.softmax(s, axis=-1)
    o = jnp.einsum('bhsm,bmhd->bshd', p.astype(v.dtype), v).reshape(B, S, D_MODEL)
    return o @ w_o

def swiglu(h, w_gate_up, w_down):
    g, u = jnp.split(h @ w_gate_up, 2, axis=-1)
    return (jax.nn.silu(g) * u) @ w_down

def first_inputs(seed: int = 0) -> dict:
    key = jax.random.key(seed)
    ks = jax.random.split(key, 24)

    def nrm(k, shape, scale):
        return scale * jax.random.normal(k, shape, jnp.float32)

    def gain(k, n):
        return 1.0 + nrm(k, (DEPTH, n), 0.05)

    s_d = D_MODEL ** -0.5
    w_in = jnp.concatenate([
        nrm(ks[0], (DEPTH, D_MODEL, 3 * FOX_WIDTH), s_d),
        nrm(ks[1], (DEPTH, D_MODEL, FOX_HEADS), 0.1 * s_d),
        nrm(ks[2], (DEPTH, D_MODEL, 3 * CHUNK_WIDTH), s_d),
    ], axis=-1)
    b_fgate = jnp.linspace(3.0, 7.0, FOX_HEADS)[None, :] + nrm(ks[3], (DEPTH, FOX_HEADS), 0.3)
    return {
        "x": jax.random.normal(ks[4], (BATCH, SEQ, D_MODEL), jnp.float32),
        "mem": jax.random.normal(ks[5], (BATCH, N_MEM, D_MODEL), jnp.float32),
        "g_mix_pre": gain(ks[6], D_MODEL),
        "w_in": w_in,
        "b_fgate": b_fgate,
        "rel_bias": nrm(ks[7], (DEPTH, CHUNK_HEADS, NUM_REL), 0.5),
        "g_fox_out": gain(ks[8], FOX_WIDTH),
        "g_chunk_out": gain(ks[9], CHUNK_WIDTH),
        "w_out": nrm(ks[10], (DEPTH, D_MODEL, D_MODEL), s_d),
        "g_mix_post": gain(ks[11], D_MODEL),
        "g_mem_pre": gain(ks[12], D_MODEL),
        "g_mem_kv": gain(ks[13], D_MODEL),
        "w_mem_q": nrm(ks[14], (DEPTH, D_MODEL, D_MODEL), s_d),
        "w_mem_kv": nrm(ks[15], (DEPTH, D_MODEL, 2 * D_MODEL), s_d),
        "w_mem_o": nrm(ks[16], (DEPTH, D_MODEL, D_MODEL), s_d),
        "g_mem_post": gain(ks[17], D_MODEL),
        "g_ffn_pre": gain(ks[18], D_MODEL),
        "w_gate_up": nrm(ks[19], (DEPTH, D_MODEL, 2 * D_FF), s_d),
        "w_down": nrm(ks[20], (DEPTH, D_FF, D_MODEL), D_FF ** -0.5),
        "g_ffn_post": gain(ks[21], D_MODEL),
    }

def first_block(x, mem, g_mix_pre, w_in, b_fgate, rel_bias, g_fox_out, g_chunk_out, w_out,
              g_mix_post, g_mem_pre, g_mem_kv, w_mem_q, w_mem_kv, w_mem_o, g_mem_post,
              g_ffn_pre, w_gate_up, w_down, g_ffn_post):
    B, S, _ = x.shape
    splits = [FOX_WIDTH, 2 * FOX_WIDTH, 3 * FOX_WIDTH, 3 * FOX_WIDTH + FOX_HEADS,
              3 * FOX_WIDTH + FOX_HEADS + CHUNK_WIDTH, 3 * FOX_WIDTH + FOX_HEADS + 2 * CHUNK_WIDTH]
    for l in range(DEPTH):
        h = rms_norm(x, g_mix_pre[l])
        proj = h @ w_in[l]
        q_f, k_f, v_f, f_logit, q_c, k_c, v_c = jnp.split(proj, splits, axis=-1)
        log_f = jax.nn.log_sigmoid((f_logit + b_fgate[l]).astype(jnp.float32))
        o_f = fox_attention(q_f.reshape(B, S, FOX_HEADS, HEAD_DIM),
                            k_f.reshape(B, S, FOX_HEADS, HEAD_DIM),
                            v_f.reshape(B, S, FOX_HEADS, HEAD_DIM), log_f)
        o_c = chunked_rel_attention(q_c.reshape(B, S, CHUNK_HEADS, HEAD_DIM),
                                    k_c.reshape(B, S, CHUNK_HEADS, HEAD_DIM),
                                    v_c.reshape(B, S, CHUNK_HEADS, HEAD_DIM), rel_bias[l])
        o_f = rms_norm(o_f.reshape(B, S, FOX_WIDTH), g_fox_out[l])
        o_c = rms_norm(o_c.reshape(B, S, CHUNK_WIDTH), g_chunk_out[l])
        mix = jnp.concatenate([o_f, o_c], axis=-1) @ w_out[l]
        x = x + rms_norm(mix, g_mix_post[l])
        h = rms_norm(x, g_mem_pre[l])
        m = rms_norm(mem, g_mem_kv[l])
        ca = memory_cross_attention(h, m, w_mem_q[l], w_mem_kv[l], w_mem_o[l])
        x = x + rms_norm(ca, g_mem_post[l])
        h = rms_norm(x, g_ffn_pre[l])
        x = x + rms_norm(swiglu(h, w_gate_up[l], w_down[l]), g_ffn_post[l])
    return x


N_MIXERS = 3
ATTN_GROUPS = ((128, 1), (512, 4), (2048, 16))
ATTN_N_GROUPS = len(ATTN_GROUPS)
ATTN_HEADS_PER_GROUP = 8
ATTN_HEAD_DIM = 64
ATTN_BLOCK = 128
ATTN_GROUP_WIDTH = ATTN_HEADS_PER_GROUP * ATTN_HEAD_DIM
ATTN_IN_WIDTH = ATTN_N_GROUPS * 3 * ATTN_GROUP_WIDTH
CONV_CHANNELS = D_MODEL
CONV_WIDTH = 31
HGRN_EXPAND = 128
HGRN_HEADS = D_MODEL // HGRN_EXPAND
HGRN_KEY_DIM = HGRN_HEADS * HGRN_EXPAND
HGRN_HEAD_V = D_MODEL // HGRN_HEADS
HGRN_VALUE_DIM = HGRN_HEADS * HGRN_HEAD_V
HGRN_CHUNK = 64
FFN_HIDDEN = 2816
FFN_CONV_WIDTH = 3
N_ATTN_LAYERS = len(range(0, DEPTH, N_MIXERS))
N_CONV_LAYERS = len(range(1, DEPTH, N_MIXERS))
N_HGRN_LAYERS = len(range(2, DEPTH, N_MIXERS))


def rms_norm_2(x, gain):
    xf = x.astype(jnp.float32)
    y = xf * lax.rsqrt(jnp.mean(xf * xf, axis=-1, keepdims=True) + EPS)
    return (y * gain.astype(jnp.float32)).astype(x.dtype)

def layer_norm(x, gain, bias):
    xf = x.astype(jnp.float32)
    mu = jnp.mean(xf, axis=-1, keepdims=True)
    var = jnp.mean(jnp.square(xf - mu), axis=-1, keepdims=True)
    y = (xf - mu) * lax.rsqrt(var + EPS)
    return (y * gain.astype(jnp.float32) + bias.astype(jnp.float32)).astype(x.dtype)

def causal_depthwise_conv(x, w, b):
    K, C = w.shape
    y = lax.conv_general_dilated(
        x, w[:, None, :].astype(x.dtype), window_strides=(1,), padding=((K - 1, 0),),
        dimension_numbers=('NWC', 'WIO', 'NWC'), feature_group_count=C)
    return y + b.astype(x.dtype)

def dilated_window_attention(q, k, v, window, dilation):
    B, S, H, Dh = q.shape
    span = window // dilation
    unit = dilation * ATTN_BLOCK
    L = -(-S // unit) * unit
    n = L // dilation
    nb = n // ATTN_BLOCK

    def to_blocks(t):
        t = jnp.pad(t, ((0, 0), (0, L - S), (0, 0), (0, 0)))
        t = t.reshape(B, n, dilation, H, Dh).transpose(0, 2, 3, 1, 4)
        return t.reshape(B, dilation, H, nb, ATTN_BLOCK, Dh)

    def with_prev(t):
        prev = jnp.pad(t, ((0, 0), (0, 0), (0, 0), (1, 0), (0, 0), (0, 0)))[:, :, :, :-1]
        return jnp.concatenate([prev, t], axis=-2)

    qb = to_blocks(q)
    kw = with_prev(to_blocks(k))
    vw = with_prev(to_blocks(v))
    s = jnp.einsum('brhnqd,brhnkd->brhnqk', qb, kw).astype(jnp.float32)
    qi = jnp.arange(ATTN_BLOCK)[:, None]
    kj = jnp.arange(2 * ATTN_BLOCK)[None, :]
    dist = qi + ATTN_BLOCK - kj
    band = (dist >= 0) & (dist <= span)
    kpos = jnp.arange(nb)[:, None, None] * ATTN_BLOCK + kj[None] - ATTN_BLOCK
    mask = band[None] & (kpos >= 0)
    s = jnp.where(mask, s, -jnp.inf)
    lse = jax.nn.logsumexp(s, axis=-1)
    p = jnp.exp(s - lse[..., None])
    o = jnp.einsum('brhnqk,brhnkd->brhnqd', p.astype(v.dtype), vw)
    o = o.reshape(B, dilation, H, n, Dh).transpose(0, 3, 1, 2, 4).reshape(B, L, H, Dh)[:, :S]
    lse = lse.reshape(B, dilation, H, n).transpose(0, 3, 1, 2).reshape(B, L, H)[:, :S]
    return o, lse

def dilated_attention_mixer(h, w_in, q_gain, k_gain, w_out):
    B, S, _ = h.shape
    proj = (h @ w_in).reshape(B, S, ATTN_N_GROUPS, 3, ATTN_HEADS_PER_GROUP, ATTN_HEAD_DIM)
    scale = ATTN_HEAD_DIM ** -0.5
    outs, lses = [], []
    for g, (window, dilation) in enumerate(ATTN_GROUPS):
        q = rms_norm_2(proj[:, :, g, 0], q_gain[g]) * scale
        k = rms_norm_2(proj[:, :, g, 1], k_gain[g])
        o, lse = dilated_window_attention(q, k, proj[:, :, g, 2], window, dilation)
        outs.append(o)
        lses.append(lse)
    weights = jax.nn.softmax(jnp.stack(lses), axis=0)
    o = jnp.sum(weights[..., None] * jnp.stack(outs).astype(jnp.float32), axis=0)
    return o.astype(h.dtype).reshape(B, S, ATTN_GROUP_WIDTH) @ w_out

def conformer_conv_mixer(h, w_in, b_in, dw_w, dw_b, ln_g, ln_b, w_out, b_out):
    u = h @ w_in + b_in
    a, gate = jnp.split(u, 2, axis=-1)
    u = a * jax.nn.sigmoid(gate)
    u = causal_depthwise_conv(u, dw_w, dw_b)
    u = jax.nn.silu(layer_norm(u, ln_g, ln_b))
    return u @ w_out + b_out

def hgrn2_chunk_scan(q, k, v, log_f):
    B, S, H, K = q.shape
    V = v.shape[-1]
    C = HGRN_CHUNK
    n = S // C

    def chunks(t):
        return t.reshape(B, n, C, H, t.shape[-1]).transpose(1, 0, 3, 2, 4)

    qc, kc, vc = chunks(q), chunks(k), chunks(v)
    bc = jnp.cumsum(chunks(log_f), axis=-2)
    tri = jnp.tril(jnp.ones((C, C), dtype=bool))[:, :, None]

    def step(state, xs):
        q_, k_, v_, b_ = xs
        o_inter = jnp.einsum('bhtk,bhkv->bhtv', q_ * jnp.exp(b_), state)
        diff = b_[:, :, :, None, :] - b_[:, :, None, :, :]
        decay = jnp.where(tri, jnp.exp(jnp.where(tri, diff, 0.0)), 0.0)
        scores = jnp.einsum('bhtsk,bhsk->bhts', q_[:, :, :, None, :] * decay, k_)
        o_intra = jnp.einsum('bhts,bhsv->bhtv', scores, v_)
        b_last = b_[:, :, -1, :]
        k_dec = k_ * jnp.exp(b_last[:, :, None, :] - b_)
        state = state * jnp.exp(b_last)[..., None] + jnp.einsum('bhsk,bhsv->bhkv', k_dec, v_)
        return state, o_inter + o_intra

    state0 = jnp.zeros((B, H, K, V), jnp.float32)
    _, o = lax.scan(step, state0, (qc, kc, vc, bc))
    return o.transpose(1, 0, 3, 2, 4).reshape(B, S, H, V)

def hgrn2_mixer(h, w_in, lower_bound, norm_gain, w_out):
    B, S, _ = h.shape
    q, f, i, g = jnp.split(h @ w_in, [HGRN_KEY_DIM, 2 * HGRN_KEY_DIM,
                                      2 * HGRN_KEY_DIM + HGRN_VALUE_DIM], axis=-1)
    q = jax.nn.silu(q.astype(jnp.float32))
    lb = lower_bound.astype(jnp.float32)
    log_f = jnp.logaddexp(jnp.log(lb), jnp.log1p(-lb) + jax.nn.log_sigmoid(f.astype(jnp.float32)))
    k = -jnp.expm1(log_f)
    heads = lambda t, dim: t.reshape(B, S, HGRN_HEADS, dim)
    o = hgrn2_chunk_scan(heads(q, HGRN_EXPAND), heads(k, HGRN_EXPAND),
                         heads(i.astype(jnp.float32), HGRN_HEAD_V), heads(log_f, HGRN_EXPAND))
    o = rms_norm_2(o, norm_gain.reshape(HGRN_HEADS, HGRN_HEAD_V)) * \
        jax.nn.silu(heads(g.astype(jnp.float32), HGRN_HEAD_V))
    return o.reshape(B, S, HGRN_VALUE_DIM).astype(h.dtype) @ w_out

def conv_ffn(h, w_up, conv_w, conv_b, w_down):
    u = causal_depthwise_conv(h @ w_up, conv_w, conv_b)
    gate, up = jnp.split(u, 2, axis=-1)
    return (jax.nn.silu(gate) * up) @ w_down

def second_inputs(seed: int = 0) -> dict:
    key = jax.random.key(seed)
    ks = iter(jax.random.split(key, 32))
    D = D_MODEL
    F2 = 2 * FFN_HIDDEN

    def nrm(shape, scale):
        return scale * jax.random.normal(next(ks), shape, jnp.float32)

    def gain(shape):
        return 1.0 + nrm(shape, 0.02)

    return {
        "x": nrm((BATCH, SEQ, D), 1.0),
        "mixer_norm": gain((DEPTH, D)),
        "ffn_norm": gain((DEPTH, D)),
        "attn_w_in": nrm((N_ATTN_LAYERS, D, ATTN_IN_WIDTH), D ** -0.5),
        "attn_q_gain": gain((N_ATTN_LAYERS, ATTN_N_GROUPS, ATTN_HEAD_DIM)),
        "attn_k_gain": gain((N_ATTN_LAYERS, ATTN_N_GROUPS, ATTN_HEAD_DIM)),
        "attn_w_out": nrm((N_ATTN_LAYERS, ATTN_GROUP_WIDTH, D), ATTN_GROUP_WIDTH ** -0.5),
        "conv_w_in": nrm((N_CONV_LAYERS, D, 2 * CONV_CHANNELS), D ** -0.5),
        "conv_b_in": nrm((N_CONV_LAYERS, 2 * CONV_CHANNELS), 0.02),
        "conv_dw_w": nrm((N_CONV_LAYERS, CONV_WIDTH, CONV_CHANNELS), CONV_WIDTH ** -0.5),
        "conv_dw_b": nrm((N_CONV_LAYERS, CONV_CHANNELS), 0.02),
        "conv_ln_g": gain((N_CONV_LAYERS, CONV_CHANNELS)),
        "conv_ln_b": nrm((N_CONV_LAYERS, CONV_CHANNELS), 0.02),
        "conv_w_out": nrm((N_CONV_LAYERS, CONV_CHANNELS, D), CONV_CHANNELS ** -0.5),
        "conv_b_out": nrm((N_CONV_LAYERS, D), 0.02),
        "hgrn_w_in": nrm((N_HGRN_LAYERS, D, 2 * HGRN_KEY_DIM + 2 * HGRN_VALUE_DIM), D ** -0.5),
        "hgrn_lb_logits": nrm((DEPTH, HGRN_KEY_DIM), 1.0),
        "hgrn_norm_g": gain((N_HGRN_LAYERS, HGRN_VALUE_DIM)),
        "hgrn_w_out": nrm((N_HGRN_LAYERS, HGRN_VALUE_DIM, D), HGRN_VALUE_DIM ** -0.5),
        "ffn_w_up": nrm((DEPTH, D, F2), D ** -0.5),
        "ffn_conv_w": nrm((DEPTH, FFN_CONV_WIDTH, F2), FFN_CONV_WIDTH ** -0.5),
        "ffn_conv_b": nrm((DEPTH, F2), 0.02),
        "ffn_w_down": nrm((DEPTH, FFN_HIDDEN, D), FFN_HIDDEN ** -0.5),
    }

def second_block(x, mixer_norm, ffn_norm, attn_w_in, attn_q_gain, attn_k_gain, attn_w_out,
              conv_w_in, conv_b_in, conv_dw_w, conv_dw_b, conv_ln_g, conv_ln_b, conv_w_out,
              conv_b_out, hgrn_w_in, hgrn_lb_logits, hgrn_norm_g, hgrn_w_out,
              ffn_w_up, ffn_conv_w, ffn_conv_b, ffn_w_down):
    lb_cum = jnp.cumsum(jax.nn.softmax(hgrn_lb_logits.astype(jnp.float32), axis=0), axis=0)
    lower_bounds = lb_cum - lb_cum[0]
    for layer in range(DEPTH):
        kind = layer % N_MIXERS
        j = layer // N_MIXERS
        h = rms_norm_2(x, mixer_norm[layer])
        if kind == 0:
            mix = dilated_attention_mixer(h, attn_w_in[j], attn_q_gain[j], attn_k_gain[j],
                                          attn_w_out[j])
        elif kind == 1:
            mix = conformer_conv_mixer(h, conv_w_in[j], conv_b_in[j], conv_dw_w[j], conv_dw_b[j],
                                       conv_ln_g[j], conv_ln_b[j], conv_w_out[j], conv_b_out[j])
        else:
            mix = hgrn2_mixer(h, hgrn_w_in[j], lower_bounds[layer], hgrn_norm_g[j], hgrn_w_out[j])
        x = x + mix
        x = x + conv_ffn(rms_norm_2(x, ffn_norm[layer]), ffn_w_up[layer], ffn_conv_w[layer],
                         ffn_conv_b[layer], ffn_w_down[layer])
    return x


def setup_inputs(seed=0):
    out = dict(first_inputs(seed))
    for name, value in second_inputs(seed + 1).items():
        if name != "x":
            out[name + "_2"] = value
    return out


def reference(
    x, mem, g_mix_pre, w_in, b_fgate, rel_bias, g_fox_out, g_chunk_out, w_out, g_mix_post,
    g_mem_pre, g_mem_kv, w_mem_q, w_mem_kv, w_mem_o, g_mem_post, g_ffn_pre, w_gate_up, w_down,
    g_ffn_post, mixer_norm_2, ffn_norm_2, attn_w_in_2, attn_q_gain_2, attn_k_gain_2,
    attn_w_out_2, conv_w_in_2, conv_b_in_2, conv_dw_w_2, conv_dw_b_2, conv_ln_g_2, conv_ln_b_2,
    conv_w_out_2, conv_b_out_2, hgrn_w_in_2, hgrn_lb_logits_2, hgrn_norm_g_2, hgrn_w_out_2,
    ffn_w_up_2, ffn_conv_w_2, ffn_conv_b_2, ffn_w_down_2,
):
    x = first_block(
        x, mem, g_mix_pre, w_in, b_fgate, rel_bias, g_fox_out, g_chunk_out, w_out, g_mix_post,
        g_mem_pre, g_mem_kv, w_mem_q, w_mem_kv, w_mem_o, g_mem_post, g_ffn_pre, w_gate_up,
        w_down, g_ffn_post,
    )
    return second_block(
        x, mixer_norm_2, ffn_norm_2, attn_w_in_2, attn_q_gain_2, attn_k_gain_2, attn_w_out_2,
        conv_w_in_2, conv_b_in_2, conv_dw_w_2, conv_dw_b_2, conv_ln_g_2, conv_ln_b_2,
        conv_w_out_2, conv_b_out_2, hgrn_w_in_2, hgrn_lb_logits_2, hgrn_norm_g_2, hgrn_w_out_2,
        ffn_w_up_2, ffn_conv_w_2, ffn_conv_b_2, ffn_w_down_2,
    )


_drawn_inputs = setup_inputs


def setup_inputs(seed=0):
    import zlib

    import numpy as np

    out = dict(_drawn_inputs(seed))
    spreads = {}
    factors = {'mixer_norm_2': 8.0,
     'ffn_norm_2': 6.859,
     'attn_q_gain_2': 8.0,
     'attn_k_gain_2': 8.0,
     'ffn_conv_b_2': 7.098}
    for name, (base, spread) in spreads.items():
        noise = np.random.default_rng([zlib.crc32(name.encode()), seed]).standard_normal(out[name].shape)
        drawn = base * np.exp(spread * noise) if base else spread * noise
        out[name] = __import__('jax').numpy.asarray(drawn.astype(out[name].dtype))
    for name, factor in factors.items():
        out[name] = (out[name] * factor).astype(out[name].dtype)
    return out
```

```python
import concourse.bass as bass
from concourse import mybir
from contextlib import ExitStack

S = 512
D = 1024
KT = D // 128
N_MEM = 256
HEADS = 8
HW = 512
N_REL = 192
D_FF = 2816
FT = D_FF // 128
IN_COLS = 3080
EPS = 1e-6
NEG = -1e30
CHUNK = 2048
CREDIT = 4

GEMMS = [
    ("forget", 1, 1, 1, "act"),
    ("fox_qk", 4, 2, 2, "act"), ("fox_v", 2, 2, 2, "act"),
    ("chunk_qk", 4, 2, 2, "act"), ("chunk_v", 2, 2, 2, "act"),
    ("mix_out", 4, 2, 2, "act"),
    ("mem_k", 4, 2, 2, "act"), ("mem_v", 4, 2, 2, "act"),
    ("mem_q", 4, 2, 2, "act"), ("mem_o", 4, 2, 2, "act"),
    ("ffn_up", 22, 2, 2, "dve"), ("ffn_down", 11, 1, 0, ""),
    ("dil_in", 18, 2, 2, "dve"), ("dil_out", 2, 4, 4, "dve"),
    ("conv_up", 22, 2, 2, "dve"), ("conv_down", 11, 1, 0, ""),
]


class Gemm:

    def __init__(self, name, chunks, signals, tiles, freed_by, chunk0, signal0, freed0):
        self.name, self.chunks, self.signals, self.tiles = name, chunks, signals, tiles
        self.freed_by, self.chunk0, self.signal0, self.freed0 = freed_by, chunk0, signal0, freed0
        self.signal_end = signal0 + chunks * signals
        self.freed_end = freed0 + chunks * tiles


def plan():
    gemms, chunk, signal, freed = {}, 0, 0, {"act": 0, "dve": 0, "": 0}
    for name, n, signals, tiles, by in GEMMS:
        gemms[name] = Gemm(name, n, signals, tiles, by, chunk, signal, freed[by])
        chunk, signal, freed[by] = chunk + n, signal + n * signals, freed[by] + n * tiles
    return gemms, chunk


class Chunk:

    def __init__(self, gemm, i, per, o):
        at = gemm.chunk0 + o
        self.gemm, self.o = gemm, o
        self.c, self.g = i * per + o, i * per + at
        self.slot, self.next_slot = at % 2, (at + 1) % 2
        self.next_loads = i * (per // 2 * 32) + ((at + 1) // 2 * 32 + 32)
        self.before = i * (per * gemm.signals) + (gemm.signal0 + o * gemm.signals)
        self.freed = i * (per * gemm.tiles) + (gemm.freed0 + o * gemm.tiles)
        self.first = isinstance(i, int) and self.g == 0
        self.last_of_gemm = isinstance(i, int) and self.c == gemm.chunks - 1
        self.last = self.last_of_gemm and gemm.name == GEMMS[-1][0]


def over_chunks(eng, gemm, body):
    odd = gemm.chunks % 2
    if odd:
        body(Chunk(gemm, 0, 2, 0))
    turns = gemm.chunks // 2 - odd
    if turns > 0:
        with eng.Fori(0, turns) as i:
            for s in range(2):
                body(Chunk(gemm, i, 2, s + odd))
    if odd and gemm.chunks > 1:
        for s in range(2):
            body(Chunk(gemm, turns, 2, s + odd))


def two_blocks_kernel(nc, A, out):
    F, R = mybir.dt.float32, mybir.dt.float32r
    ALU, ACT, AX = mybir.AluOpType, mybir.ActivationFunctionType, mybir.AxisListType
    ds = bass.ds
    G, TOTAL = plan()

    def by_columns(w, width=256):
        return w.rearrange("(k p) (c n) -> c p k n", p=128, n=width)

    def by_rows(w):
        return w.rearrange("(c k p) n -> c p k n", p=128, k=2)

    def gate_and_up(w):
        return w.rearrange("(k p) (h c n) -> c p k h n", p=128, h=2, n=128)

    w_in, w_kv = A["w_in"][0], A["w_mem_kv"][0]
    fox_end = 3 * HW
    views = {
        "forget": by_columns(w_in[:, fox_end:fox_end + 256]),
        "fox_qk": by_columns(w_in[:, 0:2 * HW]),
        "fox_v": by_columns(w_in[:, 2 * HW:3 * HW]),
        "chunk_qk": by_columns(w_in[:, fox_end + HEADS:fox_end + HEADS + 2 * HW]),
        "chunk_v": by_columns(w_in[:, fox_end + HEADS + 2 * HW:IN_COLS]),
        "mix_out": by_columns(A["w_out"][0]),
        "mem_k": by_columns(w_kv[:, 0:D]), "mem_v": by_columns(w_kv[:, D:2 * D]),
        "mem_q": by_columns(A["w_mem_q"][0]), "mem_o": by_columns(A["w_mem_o"][0]),
        "ffn_up": gate_and_up(A["w_gate_up"][0]), "ffn_down": by_rows(A["w_down"][0]),
        "dil_in": by_columns(A["attn_w_in_2"][0]), "dil_out": by_columns(A["attn_w_out_2"][0], 512),
        "conv_up": gate_and_up(A["ffn_w_up_2"][0]), "conv_down": by_rows(A["ffn_w_down_2"][0]),
    }

    ctx = ExitStack()
    with ctx:
        def sb(name, shape, dt=F):
            return ctx.enter_context(nc.sbuf_tensor(name, shape, dt))

        def sem(name):
            return ctx.enter_context(nc.semaphore(name))

        raw = sb("raw", [128, 2, CHUNK])
        w_hi = sb("w_hi", [128, 2, CHUNK], R)
        w_lo = sb("w_lo", [128, 2, CHUNK], R)
        a_hi = sb("a_hi", [128, KT, S], R)
        a_lo = sb("a_lo", [128, KT, S], R)
        x_t = sb("x_t", [128, KT, S])
        arena = sb("arena", [128, 21504])
        probs = sb("probs", [128, 2, 768])
        probs_t = sb("probs_t", [128, 2, 768])
        masks = sb("masks", [128, 1152], R)
        ident = sb("ident", [128, 128])
        ident_r = sb("ident_r", [128, 128], R)
        sel_col = sb("sel_col", [128, HEADS])
        mean_d = sb("mean_d", [128, 128])
        mean_head = sb("mean_head", [128, 128])
        std = sb("std", [128, S])
        rstd = sb("rstd", [128, S])
        vec = sb("vec", [128, 3 * 128])
        gate_bias = sb("gate_bias", [8, 1])
        eps = sb("eps", [128, 1])
        row_sq = sb("row_sq", [128, 8])
        row_std = sb("row_std", [128, 8])
        row_rstd = sb("row_rstd", [128, 8])
        neg_max = sb("neg_max", [128, 4])
        row_sum = sb("row_sum", [128, 4])
        row_recip = sb("row_recip", [128, 4])
        mod4 = sb("mod4", [128, 4])
        ps = ctx.enter_context(nc.psum_tensor("ps", [128, 8, 512], F))
        rel_dram = nc.dram_tensor("rel_dram", [HEADS, 640], F, kind="Internal").ap()

        def region(start, *shape):
            n = 1
            for d in shape:
                n *= d
            ap = arena[:, start:start + n]
            if len(shape) == 2:
                ap = ap.rearrange("p (a b) -> p a b", b=shape[1])
            return ap

        def flat(start, n):
            return arena[:, ds(start, n)]

        def pair_of_hidden(c):
            return flat(c * (2 * S), 2 * S).rearrange("p (a n) -> p a n", a=2)

        QK_1, V_1, REL, HEADS_1, Y_1, MEM_K, MEM_V, MEM_Q, V_2 = (
            0, 8192, 12288, 16384, 0, 8192, 10240, 0, 12288)
        qk_1 = region(0, 16, S)
        v_1 = region(8192, 8, HW)
        rel = region(12288, HEADS, S)
        rel_rows = arena[0:HEADS, 12288:12288 + 640]
        rel_back = region(16384, HEADS, S)
        rel_pad = region(0, 2, S)
        causal_made = region(20864, 128)
        heads_1 = region(16384, 4, D)
        q_pad_1 = region(20480, 2, S)
        x_tok = region(16384, 4, D)
        y_1 = region(0, KT, S)
        mem_tok = region(4096, 2, D)
        mem_t = region(6144, KT, N_MEM)
        mem_k = region(8192, KT, N_MEM)
        mem_v = region(10240, 2, D)
        mem_q = region(0, KT, S)
        mem_q_pad = region(12288, 4, S)
        hidden = region(0, FT, S)
        y_ffn = region(12288, KT, S)
        gate_act = region(16384, 2, S)
        conv = region(17408, 4, S)
        qk_2 = region(0, 24, S)
        v_2 = region(12288, 12, HW)
        q_pad_2 = region(18432, 6, S)
        heads_2 = region(0, 4, S)
        out_tok = region(12288, 2, D)
        decay = masks[:, 0:512]
        causal = masks[:, 512:640]
        sel_pad = masks[:, 640:896].rearrange("p (a n) -> p a n", a=2)
        decay_made = probs[0:8, 0, 0:S]
        band = masks[:, 0:896]
        stride_masks = masks[:, 896:1152]
        masks_made = region(14336, 1152)
        band_made, stride_made = masks_made[:, 0:896], masks_made[:, 896:1152]
        squares = probs[:, :, 0:S]
        normed = probs_t[:, :, 0:S]
        vec_rows = region(20480, 3, 128)
        x_flat = x_t[:, :, :].rearrange("p k n -> p (k n)")

        raw_loaded = [sem("raw_loaded_0"), sem("raw_loaded_1")]
        weights_hi = sem("weights_hi")
        weights_split = sem("weights_split")
        tile_done = sem("tile_done")
        freed = {"act": sem("freed_by_act"), "dve": sem("freed_by_dve")}
        x_loaded, mem_loaded, vec_loaded = sem("x_loaded"), sem("mem_loaded"), sem("vec_loaded")
        rel_loaded, rel_stored, rel_spread = sem("rel_loaded"), sem("rel_stored"), sem("rel_spread")
        out_stored = [sem("out_stored_0"), sem("out_stored_1")]
        const_step, const_ready, mask_step, mask_ready = (
            sem("const_step"), sem("const_ready"), sem("mask_step"), sem("mask_ready"))
        vec_cleared, vec_turned, vec_ready = sem("vec_cleared"), sem("vec_turned"), sem("vec_ready")
        gate_step, decay_ready = sem("gate_step"), sem("decay_ready")
        rel_row, rel_ready, rel_padded = sem("rel_row"), sem("rel_ready"), sem("rel_padded")
        bias_open = sem("bias_open")
        scores_done, max_done, probs_done, turned, turned_read, values_done, recip_done, heads_done = (
            sem(n) for n in ("scores_done", "max_done", "probs_done", "turned", "turned_read",
                             "values_done", "recip_done", "heads_done"))
        q_padded = sem("q_padded")
        pad_cleared = sem("pad_cleared")
        row_step, heads_scaled = sem("row_step"), sem("heads_scaled")
        silu_done = sem("silu_done")
        hidden_written, hidden_hi, hidden_split = sem("hidden_written"), sem("hidden_hi"), sem("hidden_split")
        conv_base, conv_tap = sem("conv_base"), sem("conv_tap")
        dil_sq, dil_mean, dil_std, dil_rstd, dil_written = (
            sem(n) for n in ("dil_sq", "dil_mean", "dil_std", "dil_rstd", "dil_written"))
        x_block2, x_final = sem("x_block2"), sem("x_final")
        freed_down = sem("freed_down")
        out_turned, out_copied = sem("out_turned"), sem("out_copied")

        class Norm:

            def __init__(self, n):
                self.sq, self.mean, self.std, self.rstd, self.value, self.hi, self.ready = (
                    sem(f"{n}_{s}") for s in ("sq", "mean", "std", "rstd", "value", "hi", "ready"))

        norms = {n: Norm(n) for n in ("mix_pre", "mix_post", "mem_kv_pre", "mem_pre", "mem_post",
                                      "ffn_pre", "ffn_post", "mixer_2", "ffn_2")}

        class Turn:

            def __init__(self, n):
                self.turned, self.hi, self.read = sem(f"{n}_turned"), sem(f"{n}_hi"), sem(f"{n}_read")

        turns = {n: Turn(n) for n in ("x", "mem", "mix", "memo", "dil")}

        VEC = {"mix_pre": 0, "mix_post": 8, "mem_pre": 16, "mem_kv_pre": 24, "mem_post": 32, "ffn_pre": 40,
               "ffn_post": 48, "mixer_2": 56, "ffn_2": 64, "fox_out": 72, "chunk_out": 76, "conv_b": 80,
               "tap0": 128, "tap1": 172, "tap2": 256, "q_gain": 300, "k_gain": 303}

        def vcol(name, k):
            return vec[:, ds(k + VEC[name], 1)]

        class Units:

            def __init__(self, base, pads0, pads, pairs, width):
                self.base, self.pads0, self.pads, self.pairs, self.width = base, pads0, pads, pairs, width

            def number(self, p, u):
                return p * 8 + (self.base + u)

            def last(self, p):
                return isinstance(p, int) and p == self.pairs - 1

            def padded(self, p, half):
                return p * (2 * self.pads) + (self.pads0 + (half + 1) * self.pads)

            def keys(self, u):
                return (u % 4 + 1) * 128

            def scores(self, u):
                return ps[:, 4 + u % 2, 0:self.keys(u)]

            def turned(self, u):
                return ps[:, 6 + u % 2, 0:self.keys(u)]

            def turn_free(self, n):
                return n - 1

            def pipeline(self, eng, lead, turn=None, values=None):
                def step(p, t, leads=True):
                    if leads:
                        lead(p + (t + 1) // 8, (t + 1) % 8)
                    if turn:
                        turn(p + t // 8, t % 8)
                    if values and t:
                        values(p + (t - 1) // 8, (t - 1) % 8)

                lead(0, 0)
                step(0, 0)
                with eng.Fori(0, self.pairs - 1) as p:
                    for t in range(1, 9):
                        step(p, t)
                for t in range(1, 8):
                    step(self.pairs - 1, t, t < 7)
                if values:
                    values(self.pairs - 1, 7)

        class Heads64(Units):

            def __init__(self, base, pads0, pads, q, v, out):
                super().__init__(base, pads0, pads, 4, 64)
                self.q, self.v, self.to = q, v, out

            def pad(self, dve, p, half):
                rows = slice(64 * half, 64 * half + 64)
                dve.tensor_scalar(q_pad_1[rows, half, :], arena[rows, ds(p * S + (QK_1 + self.q * S), S)], 0.125, None,
                                  ALU.mult).then_inc(q_padded, 1)
                if self.pads == 2:
                    dve.tensor_copy(sel_pad[:, half, :], sel_col[:, ds(p * 2 + half, 1)].to_broadcast([128, 128]))\
                       .then_inc(q_padded, 1)

            def score(self, pe, p, u):
                half, i, n = u // 4, u % 4, self.keys(u)
                last = pe.matmul(self.scores(u), q_pad_1[:, half, i * 128:(i + 1) * 128],
                          flat(p * S + (QK_1 + (self.q + 4) * S), n), start=True, stop=self.pads == 1)
                if self.pads == 1:
                    return last
                pe.matmul(self.scores(u), sel_pad[:, half, :], decay[:, 0:n], start=False, stop=False)
                return pe.matmul(self.scores(u)[:, n - 128:n], ident_r[:, :], causal, start=False, stop=True)

            def bias(self, u):
                return rel_pad[:, u // 4, (3 - u % 4) * 128:S]

            def value(self, p, u, b):
                return flat(p * 128 + (V_1 + (self.v + b) * HW + u // 4 * 64), 64)

            def out(self, p, u):
                return flat(p * 128 + (HEADS_1 + u % 4 * D + self.to + u // 4 * 64), 64)

        class MemoryHeads(Units):

            def keys(self, u):
                return N_MEM

            def pad(self, dve, p, half):
                dve.tensor_scalar(mem_q_pad[:, 2 * half:2 * half + 2, :],
                                  flat(p * (4 * S) + (MEM_Q + half * 2 * S), 2 * S).rearrange("p (a n) -> p a n", a=2),
                                  0.0625, None, ALU.mult).then_inc(q_padded, 1)

            def score(self, pe, p, u):
                half, i = u // 4, u % 4
                for k in range(2):
                    last = pe.matmul(self.scores(u), mem_q_pad[:, 2 * half + k, i * 128:(i + 1) * 128],
                                     flat(p * (4 * N_MEM) + (MEM_K + (2 * half + k) * N_MEM), N_MEM),
                                     start=k == 0, stop=k == 1)
                return last

            def value(self, p, u, b):
                return flat(p * 512 + (MEM_V + b * D + u // 4 * 256), 256)

            def out(self, p, u):
                return flat(p * 512 + (HEADS_1 + u % 4 * D + u // 4 * 256), 256)

        class DilatedHeads(Units):

            def keys(self, u):
                return 768

            def scores(self, u):
                b = 4 * (1 - u % 2)
                return ps[:, b:b + 2, :].rearrange("p b n -> p (b n)")[:, 0:768]

            def turned(self, u):
                return ps[:, 6:8, :].rearrange("p b n -> p (b n)")[:, 0:768]

            def turn_free(self, n):
                return n

            def pad(self, dve, p, half):
                rows = slice(64 * half, 64 * half + 64)
                for g in range(3):
                    dve.tensor_scalar(q_pad_2[rows, 3 * half + g, :], arena[rows, ds(p * S + 8 * g * S, S)], 0.125, None,
                                      ALU.mult).then_inc(q_padded, 1)

            def score(self, pe, p, u):
                half, r = u // 4, u % 4
                out, own = self.scores(u), slice(r * 128, (r + 1) * 128)
                pe.matmul(out[:, S:768], ident_r[:, :], stride_masks, start=True, stop=False)
                for g in (1, 2):
                    at = S + (g - 1) * 128
                    pe.matmul(out[:, at:at + 128], q_pad_2[:, 3 * half + g, own],
                              flat(p * S + ((8 * g + 4) * S + r * 128), 128), start=False, stop=g == 2)
                pe.matmul(out[:, 0:S], q_pad_2[:, 3 * half, own], flat(p * S + 4 * S, S), start=True, stop=False)
                return pe.matmul(out[:, 0:S], ident_r[:, :], band[:, (3 - r) * 128:(7 - r) * 128], start=False, stop=True)

            def value(self, p, u, b):
                tile = b if b < 4 else 4 * (b - 3) + u % 4
                return flat(p * 128 + (V_2 + tile * HW + u // 4 * 64), 64)

            def out(self, p, u):
                return flat(p * S + (u % 4 * 128 + u // 4 * 64), 64)

        FOX = Heads64(CREDIT, 0, 2, 0, 0, 0)
        CHUNKED = Heads64(CREDIT + 32, 16, 1, 8, 4, HW)
        MEMORY = MemoryHeads(CREDIT + 64, 24, 1, 2, 256)
        DILATED = DilatedHeads(CREDIT + 80, 28, 3, 4, 64)

        block = ctx.enter_context(nc.Block())

        @block.sync
        def _(sp):
            def load_chunk(ch):
                sp.wait_ge(weights_split, ch.g + (CREDIT - 1))
                src = views[ch.gemm.name][ch.c]
                dst = raw[:, ch.slot, :]
                if len(src.shape) == 4:
                    dst = dst.rearrange("p (k h n) -> p k h n", k=KT, h=2)
                    halves = [(dst[:, :, h, :], src[:, :, h, :]) for h in range(2)]
                else:
                    k = src.shape[1]
                    dst = dst.rearrange("p (k n) -> p k n", k=k)
                    halves = [(dst[:, h * k // 2:(h + 1) * k // 2, :], src[:, h * k // 2:(h + 1) * k // 2, :])
                              for h in range(2)]
                for to, of in halves:
                    sp.dma_start(to, of).then_inc(raw_loaded[ch.slot], 16)

            for b in range(4):
                sp.dma_start(x_tok[:, b, :], A["x"][0, b * 128:(b + 1) * 128, :]).then_inc(x_loaded, 16)
            for name, *_ in GEMMS:
                over_chunks(sp, G[name], load_chunk)
            for b in range(4):
                sp.wait_ge(out_copied, b + 1)
                sp.dma_start(out[0, b * 128:(b + 1) * 128, :], out_tok[:, b % 2, :]).then_inc(out_stored[b % 2], 16)
            for b in range(2):
                sp.wait_ge(out_stored[b], 32)

        @block.gpsimd
        def _(pool):
            pool.memset(ident[:, :], 0.0).then_inc(const_step, 1)
            pool.memset(causal_made, 0.0).then_inc(const_step, 1)
            pool.memset(sel_col[:, :], 0.0).then_inc(const_step, 1)
            pool.memset(mean_d[:, :], 1.0 / D).then_inc(const_ready, 1)
            pool.memset(decay.bitcast(F), 0.0).then_inc(const_ready, 1)
            pool.wait_ge(const_step, 3)
            pool.affine_select(out=ident[:, :], in_=ident[:, :], compare_op=ALU.not_equal, fill=1.0,
                               base=0, pattern=[[-1, 128]], channel_multiplier=1).then_inc(const_ready, 1)
            pool.affine_select(out=causal_made, in_=causal_made, compare_op=ALU.is_ge, fill=NEG,
                               base=0, pattern=[[-1, 128]], channel_multiplier=1).then_inc(const_ready, 1)
            pool.affine_select(out=sel_col[:, :], in_=sel_col[:, :], compare_op=ALU.not_equal, fill=-1.0,
                               base=0, pattern=[[-1, HEADS]], channel_multiplier=1).then_inc(const_step, 1)
            pool.wait_ge(const_step, 4)
            pool.affine_select(out=sel_col[:, :], in_=sel_col[:, :], compare_op=ALU.not_equal, fill=-1.0,
                               base=-32, pattern=[[-1, HEADS]], channel_multiplier=1).then_inc(const_ready, 1)
            pool.wait_ge(rel_row, 2)
            pool.dma_start(rel_dram, rel_rows).then_inc(rel_stored, 16)
            pool.wait_ge(rel_stored, 16)
            pool.wait_ge(turns["x"].read, KT)
            pool.dma_start(rel_back, bass.AP(rel_dram.tensor, 0, [[1, 128], [640, HEADS], [1, S]]))\
                .then_inc(rel_spread, 16)
            pool.wait_ge(rel_spread, 16)
            pool.tensor_copy(rel, rel_back[:, :, ::-1]).then_inc(rel_row, 1)
            pool.wait_ge(rel_row, 3)
            pool.memset(rel[0:64, :, S - 64:S], NEG).then_inc(rel_ready, 1)
            pool.wait_ge(rel_ready, 1)
            pool.wait_ge(scores_done, CREDIT + 32)
            with pool.Fori(0, HEADS // 2) as p:
                for half in range(2):
                    pool.wait_ge(max_done, p * 8 + (CHUNKED.base + 4 * half - 4))
                    pool.tensor_copy(rel_pad[:, half, :], flat(p * (2 * S) + (REL + half * S), S))\
                        .then_inc(rel_padded, 1)
            pool.wait_ge(scores_done, CREDIT + 64)
            pool.dma_start(mem_tok, A["mem"][0].rearrange("(b p) n -> p b n", p=128)).then_inc(mem_loaded, 16)
            pool.wait_ge(max_done, CREDIT + 64)
            pool.memset(masks_made, 0.0).then_inc(mask_step, 1)
            pool.wait_ge(mask_step, 1)
            pool.affine_select(out=band_made, in_=band_made, compare_op=ALU.is_ge, fill=NEG, base=3,
                               pattern=[[-1, 7], [-4, 128]], channel_multiplier=4).then_inc(mask_step, 1)
            pool.wait_ge(mask_step, 2)
            pool.affine_select(out=band_made, in_=band_made, compare_op=ALU.is_ge, fill=NEG, base=125,
                               pattern=[[1, 7], [4, 128]], channel_multiplier=-4).then_inc(mask_ready, 1)
            pool.affine_select(out=stride_made, in_=stride_made, compare_op=ALU.is_ge, fill=NEG, base=0,
                               pattern=[[0, 2], [-1, 128]], channel_multiplier=1).then_inc(mask_ready, 1)

        @block.scalar
        def _(act):
            def load_vectors():
                def rows(name, v):
                    n, at = v.shape[0] // 128, VEC[name]
                    act.dma_start(vec_rows[at % 128:at % 128 + n, at // 128, :],
                                  v.rearrange("(a n) -> a n", n=128)).then_inc(vec_loaded, 16)

                act.wait_ge(vec_cleared, 1)
                for name, key in (("mix_pre", "g_mix_pre"), ("mix_post", "g_mix_post"), ("mem_pre", "g_mem_pre"),
                                  ("mem_kv_pre", "g_mem_kv"), ("mem_post", "g_mem_post"), ("ffn_pre", "g_ffn_pre"),
                                  ("ffn_post", "g_ffn_post"), ("mixer_2", "mixer_norm_2"), ("ffn_2", "ffn_norm_2"),
                                  ("fox_out", "g_fox_out"), ("chunk_out", "g_chunk_out"), ("conv_b", "ffn_conv_b_2")):
                    rows(name, A[key][0])
                for tap in range(3):
                    rows(f"tap{tap}", A["ffn_conv_w_2"][0, tap])
                for name, key in (("q_gain", "attn_q_gain_2"), ("k_gain", "attn_k_gain_2")):
                    for half in range(2):
                        at = VEC[name]
                        act.dma_start(vec_rows[at % 128:at % 128 + 3, at // 128, half * 64:half * 64 + 64],
                                      A[key][0]).then_inc(vec_loaded, 16)
                act.dma_start(rel_rows[:, 64:256], A["rel_bias"][0]).then_inc(rel_loaded, 16)
                act.dma_start(gate_bias[:, :], A["b_fgate"][0].rearrange("(h a) -> h a", a=1),
                              allow_slow_non_contiguous=True).then_inc(vec_loaded, 16)

            def split_hi(ch):
                act.wait_ge(raw_loaded[ch.next_slot], ch.next_loads)
                if not ch.first:
                    act.wait_ge(tile_done, ch.before)
                act.activation(w_hi[:, ch.next_slot, :], raw[:, ch.next_slot, :], ACT.Copy).then_inc(weights_hi, 1)

            def squares_of(norm, src, tokens=S, ready=None):
                for k in range(KT):
                    if ready is not None:
                        act.wait_ge(ready[0], ready[1] + k)
                    if k >= 2:
                        act.wait_ge(norm.mean, k - 1)
                    act.activation(squares[:, k % 2, 0:tokens], src[:, k, :], ACT.Square).then_inc(norm.sq, 1)

            def std_of(norm, tokens=S):
                act.wait_ge(norm.mean, KT)
                act.activation(std[:, 0:tokens], ps[:, 4, 0:tokens], ACT.Sqrt, bias=eps[:, :]).then_inc(norm.std, 1)

            def operand_hi(norm, tokens=S):
                for k in range(KT):
                    act.wait_ge(norm.value, k + 1)
                    act.activation(a_hi[:, k, 0:tokens], normed[:, k % 2, 0:tokens], ACT.Copy).then_inc(norm.hi, 1)

            def turned_hi(turn, tiles, gain, columns):
                for f in range(tiles):
                    act.wait_ge(turn.turned, f + 1)
                    act.activation(columns(a_hi, f), ps[:, 4 + f % 4, :].rearrange("p (r j) -> p r j", r=4),
                                   ACT.Identity, scale=1.0 if gain is None else gain(f)).then_inc(turn.hi, 1)

            def tiles_out(name, write):
                def body(ch):
                    split_hi(ch)
                    for j in range(2):
                        act.wait_ge(tile_done, ch.before + (j + 1))
                        write(ch, j, ps[:, (ch.o * 2 + j) % 4, :]).then_inc(freed["act"], 1)
                over_chunks(act, G[name], body)

            def feature_tiles(dst, first=0, tokens=S):
                return lambda ch, j, src: act.activation(
                    arena[:, ds(ch.c * (2 * tokens) + (dst + (first + j) * tokens), tokens)], src[:, 0:tokens], ACT.Copy)

            def token_tiles(dst, first):
                return lambda ch, j, src: act.activation(
                    dst[:, first + 2 * j:first + 2 * j + 2, ds(ch.c * 256, 256)],
                    src.rearrange("p (b n) -> p b n", b=2), ACT.Copy)

            def exps(units, p, u):
                n, U = units.number(p, u), units.keys(u)
                act.wait_ge(max_done, n + 1)
                if units is CHUNKED:
                    act.wait_ge(recip_done, n - 3)
                    act.activation(probs[:, u % 2, 0:U], probs[:, u % 2, 0:U], ACT.Exp, scale=-1.0,
                                   bias=neg_max[:, u % 4:u % 4 + 1],
                                   accum_out=row_sum[:, u % 4:u % 4 + 1]).then_inc(probs_done, 1)
                    return
                act.wait_ge(turned, n - 1)
                act.wait_ge(recip_done, n - 3)
                act.activation(probs[:, u % 2, 0:U], units.scores(u), ACT.Exp, bias=neg_max[:, u % 4:u % 4 + 1],
                               accum_out=row_sum[:, u % 4:u % 4 + 1]).then_inc(probs_done, 1)

            def attention(units):
                units.pipeline(act, lead=lambda p, u: exps(units, p, u))

            act.sem_inc(freed["act"], CREDIT)
            act.sem_inc(probs_done, CREDIT)
            load_vectors()

            squares_of(norms["mix_pre"], x_t, ready=(turns["x"].read, 1))
            std_of(norms["mix_pre"])
            act.wait_ge(raw_loaded[0], 32)
            act.activation(w_hi[:, 0, :], raw[:, 0, :], ACT.Copy).then_inc(weights_hi, 1)
            operand_hi(norms["mix_pre"])

            z, e, u_ = probs[0:8, 0, 0:S], probs[0:8, 1, 0:S], probs_t[0:8, 0, 0:S]
            first = Chunk(G["forget"], 0, 2, 0)
            split_hi(first)
            act.wait_ge(tile_done, 1)
            act.wait_ge(const_ready, 6)
            act.activation(ident_r[:, :], ident[:, :], ACT.Copy).then_inc(decay_ready, 1)
            act.activation(causal, causal_made, ACT.Copy).then_inc(decay_ready, 1)
            act.activation(z, ps[0:8, 0, :], ACT.Identity, bias=gate_bias[:, :]).then_inc(freed["act"], 1)
            act.wait_ge(freed["act"], CREDIT + 1)
            act.activation(e, z, ACT.Abs).then_inc(gate_step, 1)
            act.wait_ge(gate_step, 1)
            act.activation(e, e, ACT.Exp, scale=-1.0).then_inc(gate_step, 1)
            act.wait_ge(gate_step, 3)
            act.activation(probs_t[0:8, 1, 0:S], u_, ACT.Ln).then_inc(gate_step, 1)

            act.wait_ge(gate_step, 12)
            act.activation(decay[0:8, :], decay_made, ACT.Copy).then_inc(decay_ready, 1)

            tiles_out("fox_qk", feature_tiles(QK_1))
            tiles_out("fox_v", token_tiles(v_1, 0))
            tiles_out("chunk_qk", feature_tiles(QK_1, 8))
            tiles_out("chunk_v", token_tiles(v_1, 4))
            attention(FOX)
            attention(CHUNKED)

            squares_of(norms["mem_kv_pre"], mem_t, N_MEM, ready=(turns["mem"].read, 1))
            std_of(norms["mem_kv_pre"], N_MEM)
            act.wait_ge(heads_done, CREDIT + 64)
            for b in range(4):
                for half in range(2):
                    n = 2 * b + half
                    if n >= 2:
                        act.wait_ge(row_step, n - 1)
                    act.activation(squares[:, n % 2, :], heads_1[:, b, half * HW:(half + 1) * HW], ACT.Square,
                                   accum_out=row_sq[:, n:n + 1]).then_inc(row_step, 1)
            act.wait_ge(row_step, 8)
            act.activation(row_std[:, :], row_sq[:, :], ACT.Sqrt, scale=1.0 / HW, bias=eps[:, :]).then_inc(row_step, 1)
            straight = lambda a, f: a[:, f, :].rearrange("p (r j) -> p r j", r=4)
            turned_hi(turns["mix"], KT, lambda f: vcol("fox_out", f), straight)
            tiles_out("mix_out", feature_tiles(Y_1))
            for k in range(KT):
                act.wait_ge(norms["mem_kv_pre"].value, k + 1)
                act.activation(a_hi[:, k, 0:N_MEM], mem_t[:, k, :], ACT.Copy).then_inc(norms["mem_kv_pre"].hi, 1)
            squares_of(norms["mix_post"], y_1, ready=(freed["act"], CREDIT + G["mix_out"].freed0 + 1))
            std_of(norms["mix_post"])
            tiles_out("mem_k", feature_tiles(MEM_K, tokens=N_MEM))
            tiles_out("mem_v", lambda ch, j, src: act.activation(mem_v[:, j, ds(ch.c * 256, 256)],
                                                                 src[:, 0:256], ACT.Copy))
            squares_of(norms["mem_pre"], x_t, ready=(norms["mix_post"].ready, 1))
            std_of(norms["mem_pre"])
            operand_hi(norms["mem_pre"])
            tiles_out("mem_q", feature_tiles(MEM_Q))
            attention(MEMORY)
            turned_hi(turns["memo"], KT, None, straight)
            tiles_out("mem_o", feature_tiles(Y_1))
            squares_of(norms["mem_post"], y_1, ready=(freed["act"], CREDIT + G["mem_o"].freed0 + 1))
            std_of(norms["mem_post"])
            squares_of(norms["ffn_pre"], x_t, ready=(norms["mem_post"].ready, 1))
            std_of(norms["ffn_pre"])
            operand_hi(norms["ffn_pre"])

            def gate(ch):
                split_hi(ch)
                act.wait_ge(tile_done, ch.before + 1)
                act.wait_ge(hidden_written, ch.c + (CREDIT - 1))
                act.activation(gate_act[:, ch.o, :], ps[:, 2 * ch.o, :], ACT.Silu).then_inc(silu_done, 1)

            def rows_hi(ch):
                if not ch.last:
                    split_hi(ch)
                if not ch.last_of_gemm:
                    to = 2 * ((ch.o + 1) % 2)
                    act.activation(a_hi[:, to:to + 2, :], pair_of_hidden(ch.c + 1), ACT.Copy).then_inc(hidden_hi, 1)

            def first_rows_hi(gemm, written):
                act.wait_ge(hidden_written, written)
                act.wait_ge(tile_done, gemm.signal0)
                act.activation(a_hi[:, 0:2, :], hidden[:, 0:2, :], ACT.Copy).then_inc(hidden_hi, 1)

            act.wait_ge(mask_ready, 8)
            act.activation(masks[:, :], masks_made, ACT.Copy).then_inc(mask_ready, 1)
            over_chunks(act, G["ffn_up"], gate)
            first_rows_hi(G["ffn_down"], CREDIT + FT)
            over_chunks(act, G["ffn_down"], rows_hi)
            act.wait_ge(mask_ready, 9)
            act.wait_ge(tile_done, G["ffn_down"].signal_end)
            for k in range(KT):
                act.activation(y_ffn[:, k, :], ps[:, k, :], ACT.Copy).then_inc(freed_down, 1)
            squares_of(norms["ffn_post"], y_ffn, ready=(freed_down, 1))
            std_of(norms["ffn_post"])

            squares_of(norms["mixer_2"], x_t, ready=(norms["ffn_post"].ready, 1))
            std_of(norms["mixer_2"])
            operand_hi(norms["mixer_2"])
            with act.Fori(0, 3) as grp:
                for c in range(6):
                    ch = Chunk(G["dil_in"], grp, 6, c)
                    split_hi(ch)
                    if c < 4:
                        for j in range(2):
                            t, n = 2 * c + j, 8 * grp + (2 * c + j)
                            act.wait_ge(tile_done, ch.before + (j + 1))
                            act.wait_ge(dil_mean, n - 1 + CREDIT)
                            act.activation(squares[:, t % 2, :], ps[:, t % 4, :], ACT.Square).then_inc(dil_sq, 1)
                            act.wait_ge(dil_mean, n + 1 + CREDIT)
                            act.wait_ge(dil_rstd, n + CREDIT)
                            act.activation(std[:, :], ps[:, 4 + t % 2, :], ACT.Sqrt, bias=eps[:, :]).then_inc(dil_std, 1)
            attention(DILATED)
            strided = lambda a, f: a[:, f, :].rearrange("p (j r) -> p r j", r=4)
            turned_hi(turns["dil"], 4, None, strided)

            def wide(ch):
                split_hi(ch)
            over_chunks(act, G["dil_out"], wide)
            squares_of(norms["ffn_2"], x_t, ready=(x_block2, 1))
            std_of(norms["ffn_2"])
            operand_hi(norms["ffn_2"])

            def conv_gate(ch):
                split_hi(ch)
                for j in range(2):
                    act.wait_ge(tile_done, ch.before + (j + 1))
                    act.wait_ge(hidden_written, ch.c + (2 * CREDIT + FT - 1))
                    act.activation(conv[:, 2 * ch.o + j, :], ps[:, (ch.o * 2 + j) % 4, :], ACT.Identity,
                                   bias=vcol("conv_b", ch.c + j * FT), scale=vcol("tap2", ch.c + j * FT))\
                       .then_inc(conv_base, 1)
                act.wait_ge(conv_tap, 4 * ch.c + 2)
                act.activation(gate_act[:, ch.o, :], conv[:, 2 * ch.o, :], ACT.Silu).then_inc(silu_done, 1)

            over_chunks(act, G["conv_up"], conv_gate)
            first_rows_hi(G["conv_down"], 2 * CREDIT + 2 * FT)
            over_chunks(act, G["conv_down"], rows_hi)

        @block.vector
        def _(dve):
            def split_lo(ch):
                dve.wait_ge(weights_hi, ch.g + 2)
                dve.tensor_tensor(w_lo[:, ch.next_slot, :], raw[:, ch.next_slot, :],
                                  w_hi[:, ch.next_slot, :].bitcast(F), ALU.subtract).then_inc(weights_split, 1)

            def rstd_of(norm, tokens=S):
                dve.wait_ge(norm.std, 1)
                dve.reciprocal(rstd[:, 0:tokens], std[:, 0:tokens]).then_inc(norm.rstd, 1)
                dve.wait_ge(norm.rstd, 1)

            def operand(name, src, used, permute=False):
                norm = norms[name]
                if used:
                    dve.wait_ge(tile_done, used)

                def value(k):
                    if k >= 2:
                        dve.wait_ge(norm.ready, k - 1)
                    dst, a, b = normed[:, k % 2, :], src[:, k, :], rstd[:, :]
                    if permute:
                        dst = dst.rearrange("p (r j) -> p j r", r=4)
                        a, b = (v.rearrange("p (j r) -> p j r", r=4) for v in (a, b))
                    dve.scalar_tensor_tensor(out=dst, in0=a, scalar=vcol(name, k), in1=b,
                                             op0=ALU.mult, op1=ALU.mult).then_inc(norm.value, 1)
                value(0)
                for k in range(KT):
                    if k + 1 < KT:
                        value(k + 1)
                    dve.wait_ge(norm.hi, k + 1)
                    dve.tensor_tensor(a_lo[:, k, :], normed[:, k % 2, :], a_hi[:, k, :].bitcast(F),
                                      ALU.subtract).then_inc(norm.ready, 1)

            def residual(name, y):
                norm = norms[name]

                def value(k):
                    dve.scalar_tensor_tensor(out=y[:, k, :], in0=y[:, k, :], scalar=vcol(name, k), in1=rstd[:, :],
                                             op0=ALU.mult, op1=ALU.mult).then_inc(norm.value, 1)
                value(0)
                for k in range(KT):
                    if k + 1 < KT:
                        value(k + 1)
                    dve.wait_ge(norm.value, k + 1)
                    dve.tensor_tensor(x_t[:, k, :], x_t[:, k, :], y[:, k, :], ALU.add).then_inc(norm.ready, 1)

            def turned_lo(turn, tiles, gain, columns):
                for f in range(tiles):
                    dve.wait_ge(turn.hi, f + 1)
                    src = ps[:, 4 + f % 4, :].rearrange("p (r j) -> p r j", r=4)
                    hi = columns(a_hi, f).bitcast(F)
                    if gain is None:
                        dve.tensor_tensor(columns(a_lo, f), src, hi, ALU.subtract).then_inc(turn.read, 1)
                    else:
                        dve.scalar_tensor_tensor(out=columns(a_lo, f), in0=src, scalar=gain(f), in1=hi,
                                                 op0=ALU.mult, op1=ALU.subtract).then_inc(turn.read, 1)

            def splits(name):
                over_chunks(dve, G[name], split_lo)

            def pad(units, p, half):
                units.pad(dve, p, half)

            def lead(units):
                def f(p, u):
                    n = units.number(p, u)
                    dve.wait_ge(scores_done, n + 1)
                    dve.wait_ge(probs_done, n - 3)
                    if units is CHUNKED:
                        dve.wait_ge(turned, n - 1)
                        if u % 4 == 0:
                            dve.wait_ge(rel_padded, p * 2 + (u // 4 + 1))
                        dve.sem_inc(bias_open, 1)
                        dve.tensor_tensor_reduce(out=probs[:, u % 2, 0:units.keys(u)], in0=units.scores(u),
                                                 in1=units.bias(u), scale=-1.0, scalar=3e38, op0=ALU.add,
                                                 op1=ALU.min, accum_out=neg_max[:, u % 4:u % 4 + 1])\
                           .then_inc(max_done, 1)
                        if u in (3, 7) and not units.last(p):
                            pad(units, p + 1, u // 4)
                        return
                    dve.tensor_reduce(neg_max[:, u % 4:u % 4 + 1], units.scores(u), axis=AX.X, op=ALU.max,
                                      negate=True).then_inc(max_done, 1)
                    if u in (3, 7) and not units.last(p):
                        pad(units, p + 1, u // 4)
                return f

            def turned_out(units):
                def f(p, u):
                    n = units.number(p, u)
                    dve.wait_ge(turned, n + 1)
                    dve.wait_ge(values_done, n - 1)
                    dve.tensor_copy(probs_t[:, u % 2, 0:units.keys(u)], units.turned(u)).then_inc(turned_read, 1)
                return f

            def heads_out(units):
                def f(p, u):
                    n = units.number(p, u)
                    dve.wait_ge(probs_done, n + 1)
                    dve.reciprocal(row_recip[:, u % 4:u % 4 + 1], row_sum[:, u % 4:u % 4 + 1]).then_inc(recip_done, 1)
                    dve.wait_ge(recip_done, n + 1)
                    dve.wait_ge(values_done, n + 1)
                    dve.tensor_scalar(units.out(p, u), ps[:, 2 + u % 2, 0:units.width], row_recip[:, u % 4:u % 4 + 1],
                                      None, ALU.mult).then_inc(heads_done, 1)
                return f

            def attention(units):
                for half in range(2):
                    pad(units, 0, half)
                units.pipeline(dve, lead=lead(units), turn=turned_out(units), values=heads_out(units))

            dve.memset(vec_rows, 0.0).then_inc(vec_cleared, 1)
            dve.memset(eps[:, :], EPS).then_inc(const_ready, 1)
            dve.memset(mean_head[:, :], 0.0).then_inc(pad_cleared, 1)
            dve.wait_ge(pad_cleared, 1)
            dve.memset(mean_head[0:64, 0:64], 1.0 / 64).then_inc(pad_cleared, 1)
            dve.memset(mean_head[64:128, 64:128], 1.0 / 64).then_inc(pad_cleared, 1)
            dve.sem_inc(weights_split, CREDIT)
            dve.sem_inc(freed["dve"], CREDIT)
            dve.sem_inc(hidden_written, CREDIT)
            dve.sem_inc(dil_rstd, CREDIT)
            for s in (max_done, turned_read, recip_done, heads_done):
                dve.sem_inc(s, CREDIT)

            for f in range(KT):
                dve.wait_ge(turns["x"].turned, f + 1)
                dve.tensor_copy(x_t[:, f, :], ps[:, 4 + f % 4, :]).then_inc(turns["x"].read, 1)
            dve.wait_ge(vec_turned, 3)
            dve.tensor_copy(vec[:, :], ps[:, 0, 0:384]).then_inc(vec_ready, 1)
            dve.wait_ge(vec_ready, 1)
            rstd_of(norms["mix_pre"])
            dve.wait_ge(weights_hi, 1)
            dve.tensor_tensor(w_lo[:, 0, :], raw[:, 0, :], w_hi[:, 0, :].bitcast(F), ALU.subtract)\
               .then_inc(weights_split, 1)
            operand("mix_pre", x_t, 0)
            split_lo(Chunk(G["forget"], 0, 2, 0))

            z, e, u_, ln = probs[0:8, 0, 0:S], probs[0:8, 1, 0:S], probs_t[0:8, 0, 0:S], probs_t[0:8, 1, 0:S]
            r, w = std[0:8, :], rstd[0:8, :]
            dve.wait_ge(gate_step, 2)
            dve.tensor_scalar(u_, e, 1.0, None, ALU.add).then_inc(gate_step, 1)
            dve.wait_ge(gate_step, 4)
            dve.tensor_scalar(r, u_, -1.0, None, ALU.add).then_inc(gate_step, 1)
            dve.wait_ge(gate_step, 5)
            dve.tensor_tensor(r, e, r, ALU.subtract).then_inc(gate_step, 1)
            dve.reciprocal(w, u_).then_inc(gate_step, 1)
            dve.wait_ge(gate_step, 7)
            dve.tensor_tensor(r, r, w, ALU.mult).then_inc(gate_step, 1)
            dve.wait_ge(gate_step, 8)
            dve.tensor_tensor(r, r, ln, ALU.add).then_inc(gate_step, 1)
            dve.wait_ge(gate_step, 9)
            dve.scalar_tensor_tensor(out=r, in0=z, scalar=0.0, in1=r, op0=ALU.min, op1=ALU.subtract)\
               .then_inc(gate_step, 1)
            dve.memset(w, 1.0).then_inc(gate_step, 1)
            dve.wait_ge(gate_step, 11)
            dve.tensor_tensor_scan(decay_made, w, r, 0.0, ALU.mult, ALU.add).then_inc(gate_step, 1)
            dve.wait_ge(decay_ready, 3)
            dve.tensor_tensor(decay[32:40, :], decay_made, decay[0:8, :].bitcast(F), ALU.subtract)\
               .then_inc(decay_ready, 1)

            dve.wait_ge(rel_loaded, 16)
            dve.tensor_copy(rel_rows[:, 0:64], rel_rows[:, 64:65].to_broadcast([HEADS, 64])).then_inc(rel_row, 1)
            dve.tensor_copy(rel_rows[:, 256:640], rel_rows[:, 255:256].to_broadcast([HEADS, 384])).then_inc(rel_row, 1)

            for name in ("fox_qk", "fox_v", "chunk_qk", "chunk_v"):
                splits(name)
            dve.memset(q_pad_1, 0.0).then_inc(pad_cleared, 1)
            dve.wait_ge(pad_cleared, 4)
            dve.wait_ge(freed["act"], CREDIT + G["chunk_v"].freed_end)
            dve.wait_ge(rel_ready, 1)
            attention(FOX)
            attention(CHUNKED)

            for f in range(KT):
                dve.wait_ge(turns["mem"].turned, f + 1)
                dve.tensor_copy(mem_t[:, f, :], ps[:, 4 + f % 4, 0:N_MEM]).then_inc(turns["mem"].read, 1)
            rstd_of(norms["mem_kv_pre"], N_MEM)
            for k in range(KT):
                dve.scalar_tensor_tensor(out=mem_t[:, k, :], in0=mem_t[:, k, :], scalar=vcol("mem_kv_pre", k),
                                         in1=rstd[:, 0:N_MEM], op0=ALU.mult, op1=ALU.mult)\
                   .then_inc(norms["mem_kv_pre"].value, 1)
            dve.wait_ge(row_step, 9)
            dve.reciprocal(row_rstd[:, :], row_std[:, :]).then_inc(row_step, 1)
            dve.wait_ge(row_step, 10)
            for b in range(4):
                for half in range(2):
                    n = 2 * b + half
                    part = heads_1[:, b, half * HW:(half + 1) * HW]
                    dve.tensor_scalar(part, part, row_rstd[:, n:n + 1], None, ALU.mult).then_inc(heads_scaled, 1)
            straight = lambda a, f: a[:, f, :].rearrange("p (r j) -> p r j", r=4)
            turned_lo(turns["mix"], KT, lambda f: vcol("fox_out", f), straight)
            splits("mix_out")
            dve.wait_ge(tile_done, G["mix_out"].signal_end)
            for k in range(KT):
                dve.wait_ge(norms["mem_kv_pre"].hi, k + 1)
                dve.tensor_tensor(a_lo[:, k, 0:N_MEM], mem_t[:, k, :], a_hi[:, k, 0:N_MEM].bitcast(F),
                                  ALU.subtract).then_inc(norms["mem_kv_pre"].ready, 1)
            rstd_of(norms["mix_post"])
            residual("mix_post", y_1)
            splits("mem_k")
            splits("mem_v")
            dve.wait_ge(mask_ready, 2)
            dve.tensor_reduce(mod4[:, :], ident[:, :].rearrange("p (a b) -> p b a", b=4), axis=AX.X, op=ALU.add)\
               .then_inc(mask_ready, 1)
            dve.wait_ge(mask_ready, 3)
            dve.tensor_scalar(mod4[:, :], mod4[:, :], -1.0, -NEG, ALU.add, ALU.mult).then_inc(mask_ready, 1)
            dve.wait_ge(mask_ready, 4)
            for b in range(4):
                part = stride_made[:, 128:256].rearrange("p (a b) -> p b a", b=4)[:, b, :]
                dve.tensor_scalar(part, part, mod4[:, b:b + 1], None, ALU.add).then_inc(mask_ready, 1)
            rstd_of(norms["mem_pre"])
            operand("mem_pre", x_t, G["mem_v"].signal_end)
            splits("mem_q")
            dve.wait_ge(freed["act"], CREDIT + G["mem_q"].freed_end)
            attention(MEMORY)
            turned_lo(turns["memo"], KT, None, straight)
            splits("mem_o")
            rstd_of(norms["mem_post"])
            residual("mem_post", y_1)
            rstd_of(norms["ffn_pre"])
            operand("ffn_pre", x_t, G["mem_o"].signal_end)

            def gated(ch):
                split_lo(ch)
                dve.wait_ge(silu_done, ch.c + 1)
                dve.wait_ge(tile_done, ch.before + 2)
                dve.tensor_tensor(arena[:, ds(ch.c * S, S)], gate_act[:, ch.o, :],
                                  ps[:, 2 * ch.o + 1, :], ALU.mult).then_inc(hidden_written, 1)
                dve.wait_ge(hidden_written, ch.c + (CREDIT + 1))
                dve.sem_inc(freed["dve"], 2)

            def rows_lo(ch, base):
                if not ch.last:
                    split_lo(ch)
                if not ch.last_of_gemm:
                    to = 2 * ((ch.o + 1) % 2)
                    dve.wait_ge(hidden_hi, ch.c + (base + 2))
                    dve.tensor_tensor(a_lo[:, to:to + 2, :], pair_of_hidden(ch.c + 1),
                                      a_hi[:, to:to + 2, :].bitcast(F), ALU.subtract).then_inc(hidden_split, 1)

            def first_rows_lo(base):
                dve.wait_ge(hidden_hi, base + 1)
                dve.tensor_tensor(a_lo[:, 0:2, :], hidden[:, 0:2, :], a_hi[:, 0:2, :].bitcast(F),
                                  ALU.subtract).then_inc(hidden_split, 1)

            over_chunks(dve, G["ffn_up"], gated)
            first_rows_lo(0)
            over_chunks(dve, G["ffn_down"], lambda ch: rows_lo(ch, 0))
            rstd_of(norms["ffn_post"])
            residual("ffn_post", y_ffn)

            rstd_of(norms["mixer_2"])
            operand("mixer_2", x_t, G["ffn_down"].signal_end, permute=True)
            with dve.Fori(0, 3) as grp:
                for c in range(6):
                    ch = Chunk(G["dil_in"], grp, 6, c)
                    split_lo(ch)
                    for j in range(2):
                        if c < 4:
                            t, n = 2 * c + j, 8 * grp + (2 * c + j)
                            dve.wait_ge(dil_std, n + 1)
                            dve.wait_ge(freed["dve"], ch.freed + (j + CREDIT))
                            dve.reciprocal(rstd[:, :], std[:, :]).then_inc(dil_rstd, 1)
                            dve.wait_ge(dil_rstd, n + 1 + CREDIT)
                            dve.scalar_tensor_tensor(
                                out=arena[:, ds(n * S, S)], in0=ps[:, t % 4, :],
                                scalar=vcol("q_gain" if c < 2 else "k_gain", grp), in1=rstd[:, :],
                                op0=ALU.mult, op1=ALU.mult).then_inc(freed["dve"], 1)
                        else:
                            t = 2 * c + j
                            dve.wait_ge(tile_done, ch.before + (j + 1))
                            dve.tensor_copy(v_2[:, ds(4 * grp + 2 * j, 2), (c - 4) * 256:(c - 3) * 256],
                                            ps[:, t % 4, :].rearrange("p (b n) -> p b n", b=2))\
                               .then_inc(freed["dve"], 1)
            dve.wait_ge(freed["dve"], CREDIT + G["dil_in"].freed_end)
            dve.memset(q_pad_2, 0.0).then_inc(pad_cleared, 1)
            dve.wait_ge(pad_cleared, 5)
            attention(DILATED)
            turned_lo(turns["dil"], 4, None, lambda a, f: a[:, f, :].rearrange("p (j r) -> p r j", r=4))

            def wide(ch):
                split_lo(ch)
                for j in range(4):
                    dve.wait_ge(tile_done, ch.before + (j + 1))
                    xt = x_flat[:, ds(ch.c * (4 * S) + j * S, S)]
                    dve.tensor_tensor(xt, xt, ps[:, j, :], ALU.add).then_inc(x_block2, 1)
                dve.wait_ge(x_block2, 4 * ch.c + 4)
                dve.sem_inc(freed["dve"], 4)
            over_chunks(dve, G["dil_out"], wide)
            rstd_of(norms["ffn_2"])
            operand("ffn_2", x_t, G["dil_out"].signal_end)

            def convolved(ch):
                split_lo(ch)
                for j in range(2):
                    u, src = conv[:, 2 * ch.o + j, :], ps[:, (ch.o * 2 + j) % 4, :]
                    for tap in (1, 2):
                        if tap == 1:
                            dve.wait_ge(conv_base, 2 * ch.c + (j + 1))
                        else:
                            dve.wait_ge(conv_tap, 4 * ch.c + (2 * j + 1))
                        dve.scalar_tensor_tensor(out=u[:, tap:S], in0=src[:, 0:S - tap],
                                                 scalar=vcol(f"tap{2 - tap}", ch.c + j * FT), in1=u[:, tap:S],
                                                 op0=ALU.mult, op1=ALU.add).then_inc(conv_tap, 1)
                dve.wait_ge(conv_tap, 4 * ch.c + 4)
                dve.sem_inc(freed["dve"], 2)
                dve.wait_ge(silu_done, ch.c + (FT + 1))
                dve.tensor_tensor(arena[:, ds(ch.c * S, S)], gate_act[:, ch.o, :],
                                  conv[:, 2 * ch.o + 1, :], ALU.mult).then_inc(hidden_written, 1)

            dve.wait_ge(hidden_written, CREDIT + FT)
            dve.sem_inc(hidden_written, CREDIT)
            over_chunks(dve, G["conv_up"], convolved)
            first_rows_lo(11)
            over_chunks(dve, G["conv_down"], lambda ch: rows_lo(ch, 11))
            dve.wait_ge(tile_done, G["conv_down"].signal_end)
            for k in range(KT):
                dve.tensor_tensor(x_t[:, k, :], x_t[:, k, :], ps[:, k, :], ALU.add).then_inc(x_final, 1)
            for b in range(4):
                dve.wait_ge(out_turned, b + 1)
                if b >= 2:
                    dve.wait_ge(out_stored[b % 2], 16)
                dve.tensor_copy(out_tok[:, b % 2, :].rearrange("p (a n) -> p a n", a=2),
                                ps[:, 2 * (b % 2):2 * (b % 2) + 2, :]).then_inc(out_copied, 1)

        @block.tensor
        def _(pe):
            def three(dst, stationary, moving, start, stop, across=False):
                (s_hi, s_lo), (m_hi, m_lo) = stationary, moving
                pe.matmul(dst, s_hi, m_hi, start=start, stop=False, skip_group_check=across)
                pe.matmul(dst, s_hi, m_lo, start=False, stop=False, skip_group_check=across)
                return pe.matmul(dst, s_lo, m_hi, start=False, stop=stop, skip_group_check=across)

            def weights(slot, k_tiles):
                return tuple(w[:, slot, :].rearrange("p (k n) -> p k n", k=k_tiles) for w in (w_hi, w_lo))

            def enter(name, previous):
                if previous and G[previous].freed_by:
                    pe.wait_ge(freed[G[previous].freed_by], CREDIT + G[previous].freed_end)

            def chunk_ready(ch):
                pe.wait_ge(weights_split, ch.g + 1 + CREDIT)

            def feature_major(name, previous, tokens=S, tiles=2, k_tiles=KT):
                enter(name, previous)
                by = G[name].freed_by

                def body(ch):
                    chunk_ready(ch)
                    whi, wlo = weights(ch.slot, k_tiles)
                    for j in range(tiles):
                        pe.wait_ge(freed[by], ch.freed + (j + 1))
                        bank = (ch.o * tiles + j) % 4
                        cols = slice(j * 128, j * 128 + 128)
                        for k in range(k_tiles):
                            last = three(ps[:, bank, 0:tokens], (whi[:, k, cols], wlo[:, k, cols]),
                                         (a_hi[:, k, 0:tokens], a_lo[:, k, 0:tokens]), k == 0, k == k_tiles - 1)
                        last.then_inc(tile_done, 1)
                over_chunks(pe, G[name], body)

            def token_chunk(ch, by, bank0, blocks):
                chunk_ready(ch)
                whi, wlo = weights(ch.slot, KT)
                for j in range(2):
                    pe.wait_ge(freed[by], ch.freed + (j + 1))
                    for h in range(blocks):
                        b = blocks * j + h
                        tok = slice(b * 128, b * 128 + 128)
                        for k in range(KT):
                            last = three(ps[:, (bank0 + j) % 4, h * 256:h * 256 + 256],
                                         (a_hi[:, k, tok], a_lo[:, k, tok]), (whi[:, k, :], wlo[:, k, :]),
                                         k == 0, k == KT - 1)
                    last.then_inc(tile_done, 1)

            def token_major(name, previous, blocks=2):
                enter(name, previous)
                over_chunks(pe, G[name], lambda ch: token_chunk(ch, G[name].freed_by, 2 * ch.o, blocks))

            def down(name, previous, base):
                enter(name, previous)

                def body(ch):
                    chunk_ready(ch)
                    pe.wait_ge(hidden_split, ch.c + (base + 1))
                    whi, wlo = weights(ch.slot, 2)
                    for k in range(2):
                        for j in range(8):
                            cols = slice(j * 128, j * 128 + 128)
                            at = 2 * (ch.o % 2) + k
                            last = three(ps[:, j, :], (whi[:, k, cols], wlo[:, k, cols]),
                                         (a_hi[:, at, :], a_lo[:, at, :]), isinstance(ch.c, int) and ch.c == 0 and k == 0,
                                         k == 1, across=True)
                    last.then_inc(tile_done, 1)
                over_chunks(pe, G[name], body)

            def means(norm, tokens=S):
                for k in range(KT):
                    pe.wait_ge(norm.sq, k + 1)
                    pe.matmul(ps[:, 4, 0:tokens], mean_d[:, :], squares[:, k % 2, 0:tokens],
                              start=k == 0, stop=k == KT - 1).then_inc(norm.mean, 1)

            def turn(t, tiles, src, blocks=4):
                for f in range(tiles):
                    if f >= 4:
                        pe.wait_ge(t.read, f - 3)
                    for b in range(blocks):
                        last = pe.transpose(ps[:, 4 + f % 4, b * 128:(b + 1) * 128], src(f, b), ident[:, :])
                    last.then_inc(t.turned, 1)

            def lead(units):
                def f(p, u):
                    n = units.number(p, u)
                    if u % 4 == 0:
                        pe.wait_ge(q_padded, units.padded(p, u // 4))
                    pe.wait_ge(probs_done, n - 1)
                    units.score(pe, p, u).then_inc(scores_done, 1)
                return f

            def turn_probs(units):
                def f(p, u):
                    n = units.number(p, u)
                    pe.wait_ge(probs_done, n + 1)
                    pe.wait_ge(turned_read, units.turn_free(n))
                    for b in range(units.keys(u) // 128):
                        last = pe.transpose(units.turned(u)[:, b * 128:(b + 1) * 128],
                                            probs[:, u % 2, b * 128:(b + 1) * 128], ident[:, :])
                    last.then_inc(turned, 1)
                return f

            def values(units):
                def f(p, u):
                    n = units.number(p, u)
                    pe.wait_ge(turned_read, n + 1)
                    pe.wait_ge(heads_done, n - 1)
                    blocks = units.keys(u) // 128
                    for b in range(blocks):
                        last = pe.matmul(ps[:, 2 + u % 2, 0:units.width], probs_t[:, u % 2, b * 128:(b + 1) * 128],
                                         units.value(p, u, b), start=b == 0, stop=b == blocks - 1)
                    last.then_inc(values_done, 1)
                return f

            def attention(units):
                units.pipeline(pe, lead=lead(units), turn=turn_probs(units), values=values(units))

            for s in (scores_done, turned, values_done, dil_mean):
                pe.sem_inc(s, CREDIT)
            pe.wait_ge(const_ready, 6)
            for f in range(KT):
                if f >= 4:
                    pe.wait_ge(turns["x"].read, f - 3)
                for b in range(4):
                    if f == 0:
                        pe.wait_ge(x_loaded, 64)
                    last = pe.transpose(ps[:, 4 + f % 4, b * 128:(b + 1) * 128], x_tok[:, b, f * 128:(f + 1) * 128],
                                        ident[:, :])
                last.then_inc(turns["x"].turned, 1)
            pe.wait_ge(vec_loaded, 20 * 16)
            for t in range(3):
                pe.transpose(ps[:, 0, t * 128:(t + 1) * 128], vec_rows[:, t, :], ident[:, :]).then_inc(vec_turned, 1)
            pe.wait_ge(turns["x"].read, KT)
            means(norms["mix_pre"])

            pe.wait_ge(norms["mix_pre"].ready, KT)
            first = Chunk(G["forget"], 0, 2, 0)
            chunk_ready(first)
            pe.wait_ge(vec_ready, 1)
            whi, wlo = weights(0, KT)
            for k in range(KT):
                last = three(ps[:, 0, :], (whi[:, k, 0:128], wlo[:, k, 0:128]), (a_hi[:, k, :], a_lo[:, k, :]),
                             k == 0, k == KT - 1)
            last.then_inc(tile_done, 1)
            feature_major("fox_qk", "forget")
            token_major("fox_v", "fox_qk")
            feature_major("chunk_qk", "fox_v")
            token_major("chunk_v", "chunk_qk")
            enter("", "chunk_v")
            pe.wait_ge(decay_ready, 4)
            attention(FOX)
            attention(CHUNKED)

            pe.wait_ge(mem_loaded, 16)
            turn(turns["mem"], KT, lambda f, b: mem_tok[:, b, f * 128:(f + 1) * 128], 2)
            pe.wait_ge(turns["mem"].read, KT)
            means(norms["mem_kv_pre"], N_MEM)
            pe.wait_ge(norms["mem_kv_pre"].std, 1)
            pe.wait_ge(heads_scaled, 8)
            turn(turns["mix"], KT, lambda f, b: heads_1[:, b, f * 128:(f + 1) * 128])
            pe.wait_ge(turns["mix"].read, KT)
            feature_major("mix_out", "chunk_v")
            means(norms["mix_post"])
            pe.wait_ge(norms["mem_kv_pre"].ready, KT)
            feature_major("mem_k", "mix_out", N_MEM)
            token_major("mem_v", "mem_k", 1)
            pe.wait_ge(norms["mix_post"].std, 1)
            means(norms["mem_pre"])
            pe.wait_ge(norms["mem_pre"].ready, KT)
            feature_major("mem_q", "mem_v")
            enter("", "mem_q")
            attention(MEMORY)
            pe.wait_ge(heads_done, CREDIT + 80)
            turn(turns["memo"], KT, lambda f, b: heads_1[:, b, f * 128:(f + 1) * 128])
            pe.wait_ge(turns["memo"].read, KT)
            feature_major("mem_o", "mem_q")
            means(norms["mem_post"])
            pe.wait_ge(norms["mem_post"].std, 1)
            means(norms["ffn_pre"])
            pe.wait_ge(norms["ffn_pre"].ready, KT)
            feature_major("ffn_up", "mem_o")
            down("ffn_down", "ffn_up", 0)
            pe.wait_ge(freed_down, KT)
            means(norms["ffn_post"])
            pe.wait_ge(norms["ffn_post"].std, 1)
            means(norms["mixer_2"])
            pe.wait_ge(norms["mixer_2"].ready, KT)

            def head_mean(n, t):
                pe.wait_ge(dil_sq, n + 1)
                pe.matmul(ps[:, 4 + t % 2, :], mean_head[:, :], squares[:, t % 2, :], start=True, stop=True)\
                  .then_inc(dil_mean, 1)

            with pe.Fori(0, 3) as grp:
                for c in range(6):
                    ch = Chunk(G["dil_in"], grp, 6, c)
                    if c >= 4:
                        token_chunk(ch, "dve", 2 * c, 2)
                        continue
                    chunk_ready(ch)
                    whi, wlo = weights(ch.slot, KT)
                    for j in range(2):
                        t = 2 * c + j
                        pe.wait_ge(freed["dve"], ch.freed + (j + 1))
                        cols = slice(j * 128, j * 128 + 128)
                        for k in range(KT):
                            last = three(ps[:, t % 4, :], (whi[:, k, cols], wlo[:, k, cols]),
                                         (a_hi[:, k, :], a_lo[:, k, :]), k == 0, k == KT - 1)
                        last.then_inc(tile_done, 1)
                        if t >= 1:
                            head_mean(8 * grp + (t - 1), t - 1)
                    if c == 3:
                        head_mean(8 * grp + 7, 7)
            enter("", "dil_in")
            pe.wait_ge(mask_ready, 9)
            attention(DILATED)
            pe.wait_ge(heads_done, CREDIT + 112)
            turn(turns["dil"], 4, lambda f, b: heads_2[:, f, b * 128:(b + 1) * 128])
            pe.wait_ge(turns["dil"].read, 4)
            feature_major("dil_out", "dil_in", tiles=4, k_tiles=4)
            means(norms["ffn_2"])
            pe.wait_ge(norms["ffn_2"].ready, KT)
            feature_major("conv_up", "dil_out")
            down("conv_down", "conv_up", 11)
            for b in range(4):
                if b == 0:
                    pe.wait_ge(x_final, KT)
                if b >= 2:
                    pe.wait_ge(out_copied, b - 1)
                for f in range(KT):
                    last = pe.transpose(ps[:, 2 * (b % 2) + f // 4, (f % 4) * 128:(f % 4 + 1) * 128],
                                        x_t[:, f, b * 128:(b + 1) * 128], ident[:, :])
                last.then_inc(out_turned, 1)


_INS = ["x", "mem", "g_mix_pre", "w_in", "b_fgate", "rel_bias", "g_fox_out", "g_chunk_out", "w_out", "g_mix_post",
        "g_mem_pre", "g_mem_kv", "w_mem_q", "w_mem_kv", "w_mem_o", "g_mem_post", "g_ffn_pre", "w_gate_up", "w_down",
        "g_ffn_post", "mixer_norm_2", "ffn_norm_2", "attn_w_in_2", "attn_q_gain_2", "attn_k_gain_2",
        "attn_w_out_2", "ffn_w_up_2", "ffn_conv_w_2", "ffn_conv_b_2", "ffn_w_down_2"]


def kernel(**inputs):
    import numpy as _np
    import concourse.bacc as _bacc
    from concourse import mybir as _mybir
    from concourse.bass_utils import run_bass_kernel_spmd as _run

    nc = _bacc.Bacc("TRN2", target_bir_lowering=False, num_devices=1)
    arrays, aps = {}, {}
    for name in _INS:
        a = _np.ascontiguousarray(inputs[name])
        arrays[f"in_{name}"] = a
        aps[name] = nc.dram_tensor(f"in_{name}", a.shape, _mybir.dt.from_np(a.dtype), kind="ExternalInput").ap()
    out = nc.dram_tensor("out_x", (1, S, D), _mybir.dt.float32, kind="ExternalOutput").ap()
    two_blocks_kernel(nc, aps, out)
    r = _run(nc, [arrays], core_ids=[0])
    return r.results[0]["out_x"]
```

```python
import concourse.bass as bass
from concourse import mybir
from contextlib import ExitStack

S = 512
D = 1024
KT = D // 128
N_MEM = 256
HEADS = 8
HW = 512
N_REL = 192
D_FF = 2816
FT = D_FF // 128
IN_COLS = 3080
EPS = 1e-6
NEG = -1e30
CHUNK = 2048
CREDIT = 4

GEMMS = [
    ("forget", 1, 1, 1, "act"),
    ("fox_qk", 4, 2, 2, "act"), ("fox_v", 2, 2, 2, "act"),
    ("chunk_qk", 4, 2, 2, "act"), ("chunk_v", 2, 2, 2, "act"),
    ("mem_k", 4, 2, 2, "act"), ("mem_v", 4, 2, 2, "act"),
    ("mix_out", 4, 2, 2, "act"),
    ("mem_q", 4, 2, 2, "dve"), ("mem_o", 4, 2, 2, "act"),
    ("ffn_up", 22, 2, 2, "dve"), ("ffn_down", 11, 1, 0, ""),
    ("dil_in", 18, 2, 2, "dve"), ("dil_out", 2, 4, 4, "dve"),
    ("conv_up", 22, 2, 2, "dve"), ("conv_down", 11, 1, 0, ""),
]


class Gemm:

    def __init__(self, name, chunks, signals, tiles, freed_by, chunk0, signal0, freed0):
        self.name, self.chunks, self.signals, self.tiles = name, chunks, signals, tiles
        self.freed_by, self.chunk0, self.signal0, self.freed0 = freed_by, chunk0, signal0, freed0
        self.signal_end = signal0 + chunks * signals
        self.freed_end = freed0 + chunks * tiles


def plan():
    gemms, chunk, signal, freed = {}, 0, 0, {"act": 0, "dve": 0, "": 0}
    for name, n, signals, tiles, by in GEMMS:
        gemms[name] = Gemm(name, n, signals, tiles, by, chunk, signal, freed[by])
        chunk, signal, freed[by] = chunk + n, signal + n * signals, freed[by] + n * tiles
    return gemms, chunk


class Chunk:

    def __init__(self, gemm, i, per, o):
        at = gemm.chunk0 + o
        self.gemm, self.o, self.slot_o = gemm, o, o % 2
        self.c, self.g = i * per + o, i * per + at
        self.slot, self.next_slot = at % 2, (at + 1) % 2
        self.next_loads = i * (per // 2 * 32) + ((at + 1) // 2 * 32 + 32)
        self.before = i * (per * gemm.signals) + (gemm.signal0 + o * gemm.signals)
        self.freed = i * (per * gemm.tiles) + (gemm.freed0 + o * gemm.tiles)
        self.first = isinstance(i, int) and self.g == 0
        self.first_of_gemm = isinstance(i, int) and self.c == 0
        self.second_of_gemm = isinstance(i, int) and self.c == 1
        self.last_of_gemm = isinstance(i, int) and self.c == gemm.chunks - 1
        self.last = self.last_of_gemm and gemm.name == GEMMS[-1][0]


def over_chunks(eng, gemm, body, peel=0, tail=0):
    odd = gemm.chunks % 2
    tail = tail or (odd and gemm.chunks > 1)
    if odd:
        body(Chunk(gemm, 0, 2, 0))
    for t in range(peel):
        for s in range(2):
            body(Chunk(gemm, t, 2, s + odd))
    turns = gemm.chunks // 2 - peel - tail
    if turns > 0:
        with eng.Fori(0, turns) as i:
            for s in range(2):
                body(Chunk(gemm, i, 2, s + odd + 2 * peel))
    for t in range(tail):
        for s in range(2):
            body(Chunk(gemm, turns + peel + t, 2, s + odd))


def pool_splits(ch):
    return ch.gemm.name == "dil_in" or (
        ch.gemm.name in ("mem_q", "ffn_up", "conv_up") and (ch.first_of_gemm or ch.second_of_gemm))


def two_blocks_kernel(nc, A, out):
    F, R = mybir.dt.float32, mybir.dt.float32r
    ALU, ACT, AX = mybir.AluOpType, mybir.ActivationFunctionType, mybir.AxisListType
    ds = bass.ds
    G, TOTAL = plan()

    def by_columns(w, width=256):
        return w.rearrange("(k p) (c n) -> c p k n", p=128, n=width)

    def by_rows(w):
        return w.rearrange("(c k p) n -> c p k n", p=128, k=2)

    def gate_and_up(w):
        return w.rearrange("(k p) (h c n) -> c p k h n", p=128, h=2, n=128)

    w_in, w_kv = A["w_in"][0], A["w_mem_kv"][0]
    fox_end = 3 * HW
    views = {
        "forget": by_columns(w_in[:, fox_end:fox_end + HEADS], HEADS),
        "fox_qk": by_columns(w_in[:, 0:2 * HW]),
        "fox_v": by_columns(w_in[:, 2 * HW:3 * HW]),
        "chunk_qk": by_columns(w_in[:, fox_end + HEADS:fox_end + HEADS + 2 * HW]),
        "chunk_v": by_columns(w_in[:, fox_end + HEADS + 2 * HW:IN_COLS]),
        "mix_out": by_columns(A["w_out"][0]),
        "mem_k": by_columns(w_kv[:, 0:D]), "mem_v": by_columns(w_kv[:, D:2 * D]),
        "mem_q": by_columns(A["w_mem_q"][0]), "mem_o": by_columns(A["w_mem_o"][0]),
        "ffn_up": gate_and_up(A["w_gate_up"][0]), "ffn_down": by_rows(A["w_down"][0]),
        "dil_in": by_columns(A["attn_w_in_2"][0]), "dil_out": by_columns(A["attn_w_out_2"][0], 512),
        "conv_up": gate_and_up(A["ffn_w_up_2"][0]), "conv_down": by_rows(A["ffn_w_down_2"][0]),
    }

    ctx = ExitStack()
    with ctx:
        def sb(name, shape, dt=F):
            return ctx.enter_context(nc.sbuf_tensor(name, shape, dt))

        def sem(name):
            return ctx.enter_context(nc.semaphore(name))

        raw = sb("raw", [128, 2, CHUNK])
        w_hi = sb("w_hi", [128, 2, CHUNK], R)
        w_lo = sb("w_lo", [128, 2, CHUNK], R)
        a_hi = sb("a_hi", [128, KT, S], R)
        a_lo = sb("a_lo", [128, KT, S], R)
        x_t = sb("x_t", [128, KT, S])
        arena = sb("arena", [128, 21504])
        work = sb("work", [128, 3072])
        masks = sb("masks", [128, 1152], R)
        ident = sb("ident", [128, 128])
        ident_r = sb("ident_r", [128, 128], R)
        sel_col = sb("sel_col", [128, HEADS])
        ones = sb("ones", [128, 128])
        mean_head = sb("mean_head", [128, 128])
        std = sb("std", [128, S])
        tok_std = sb("tok_std", [128, 4])
        tok_rstd = sb("tok_rstd", [128, 4])
        rstd = sb("rstd", [128, S])
        vec = sb("vec", [128, 3 * 128])
        gate_bias = sb("gate_bias", [8, 1])
        eps = sb("eps", [128, 1])
        x_sq = sb("x_sq", [128, 4])
        x_std = sb("x_std", [128, 4])
        x_rstd = sb("x_rstd", [128, 4])
        mem_sq = sb("mem_sq", [128, 4])
        mem_std = sb("mem_std", [128, 2])
        mem_rstd = sb("mem_rstd", [128, 2])
        row_sq = sb("row_sq", [128, 8])
        row_std = sb("row_std", [128, 8])
        row_rstd = sb("row_rstd", [128, 8])
        neg_max = sb("neg_max", [128, 4])
        row_sum = sb("row_sum", [128, 4])
        row_recip = sb("row_recip", [128, 4])
        mod4 = sb("mod4", [128, 4])
        ps = ctx.enter_context(nc.psum_tensor("ps", [128, 8, 512], F))
        rel_dram = nc.dram_tensor("rel_dram", [HEADS, 640], F, kind="Internal").ap()

        def region(start, *shape):
            n = 1
            for d in shape:
                n *= d
            ap = arena[:, start:start + n]
            if len(shape) == 2:
                ap = ap.rearrange("p (a b) -> p a b", b=shape[1])
            return ap

        def slots(start, n, width):
            return work[:, start:start + n * width].rearrange("p (a b) -> p a b", b=width)

        def flat(start, n):
            return arena[:, ds(start, n)]

        def pair_of_hidden(c):
            return flat(c * (2 * S), 2 * S).rearrange("p (a n) -> p a n", a=2)

        QK_1, V_1, REL, HEADS_1, Y_1, MEM_K, MEM_V, MEM_Q, V_2 = (
            0, 8192, 12288, 16384, 4096, 0, 2048, 8192, 12288)
        qk_1 = region(0, 16, S)
        v_1 = region(8192, 8, HW)
        rel = region(12288, HEADS, S)
        rel_rows = arena[0:HEADS, 12288:12288 + 640]
        rel_back = region(16384, HEADS, S)
        rel_pad = region(0, 2, S)
        causal_made = region(20864, 128)
        heads_1 = region(16384, 4, D)
        q_pad_1 = region(20480, 2, S)
        x_tok = region(16384, 4, D)
        x_scaled = region(0, 4, D)
        mem_tok = heads_1[:, :, HW:D]
        y_1 = region(4096, KT, S)
        mem_k = region(0, KT, N_MEM)
        mem_v = region(2048, 2, D)
        mem_q_pad = region(12288, 4, S)
        hidden = region(0, FT, S)
        y_ffn = region(12288, KT, S)
        gate_act = region(16384, 2, S)
        conv = region(17408, 4, S)
        up = region(19456, 4, S)
        qk_2 = region(0, 24, S)
        v_2 = region(12288, 12, HW)
        q_pad_2 = region(18432, 6, S)
        heads_2 = region(0, 4, S)
        out_tok = region(12288, KT, S)
        decay = masks[:, 0:512]
        causal = masks[:, 512:640]
        sel_pad = masks[:, 640:896].rearrange("p (a n) -> p a n", a=2)
        decay_made = work[0:8, 0:S]
        band = masks[:, 0:896]
        stride_masks = masks[:, 896:1152]
        masks_made = region(14336, 1152)
        band_made, stride_made = masks_made[:, 0:896], masks_made[:, 896:1152]
        squares = slots(0, 4, S)
        square_sum = slots(4 * S, 1, S)[:, 0, :]
        diagonal = slots(5 * S, 1, S)[:, 0, :]
        normed = slots(4 * S, 2, S)
        x_squares = {"mem_pre": y_1, "ffn_pre": y_1, "ffn_2": y_ffn}
        vec_rows = region(20480, 3, 128)
        x_flat = x_t[:, :, :].rearrange("p k n -> p (k n)")

        raw_loaded = [sem("raw_loaded_0"), sem("raw_loaded_1")]
        weights_hi = sem("weights_hi")
        weights_split = sem("weights_split")
        tile_done = sem("tile_done")
        freed = {"act": sem("freed_by_act"), "dve": sem("freed_by_dve")}
        x_loaded = [sem(f"x_loaded_{b}") for b in range(4)]
        x_squared, x_rooted, x_inverted, x_ready = (
            sem(n) for n in ("x_squared", "x_rooted", "x_inverted", "x_ready"))
        mem_loaded, vec_loaded, mem_step, mem_scaled = (
            sem(n) for n in ("mem_loaded", "vec_loaded", "mem_step", "mem_scaled"))
        rel_loaded, rel_stored, rel_spread = sem("rel_loaded"), sem("rel_stored"), sem("rel_spread")
        out_stored = sem("out_stored")
        const_step, const_ready, mask_step, mask_ready = (
            sem("const_step"), sem("const_ready"), sem("mask_step"), sem("mask_ready"))
        vec_cleared, vec_turned, vec_ready = sem("vec_cleared"), sem("vec_turned"), sem("vec_ready")
        gate_step, decay_ready = sem("gate_step"), sem("decay_ready")
        rel_row, rel_ready, rel_padded = sem("rel_row"), sem("rel_ready"), sem("rel_padded")
        bias_open = sem("bias_open")
        scores_done, max_done, probs_done, turned, turned_read, values_done, recip_done, heads_done = (
            sem(n) for n in ("scores_done", "max_done", "probs_done", "turned", "turned_read",
                             "values_done", "recip_done", "heads_done"))
        q_padded = sem("q_padded")
        pad_cleared = sem("pad_cleared")
        row_step, heads_scaled = sem("row_step"), sem("heads_scaled")
        silu_done, gate_scaled, up_scaled = sem("silu_done"), sem("gate_scaled"), sem("up_scaled")
        rows_free = {n: sem(f"rows_free_{n}") for n in ("ffn_up", "conv_up")}
        x_added = {n: sem(f"x_added_{n}") for n in ("mix_post", "mem_post", "ffn_post")}
        hidden_written, hidden_hi, hidden_split = sem("hidden_written"), sem("hidden_hi"), sem("hidden_split")
        conv_base, conv_tap = sem("conv_base"), sem("conv_tap")
        dil_sq, dil_mean, dil_std, dil_rstd, dil_written = (
            sem(n) for n in ("dil_sq", "dil_mean", "dil_std", "dil_rstd", "dil_written"))
        x_block2, x_final = sem("x_block2"), sem("x_final")
        freed_down, down_done = sem("freed_down"), [sem("down_done_1"), sem("down_done_2")]
        out_turned, out_copied = sem("out_turned"), sem("out_copied")

        class Norm:

            def __init__(self, n, more):
                self.sq, self.added, self.sum, self.std, self.inverse, self.diagonal, self.spread = (
                    sem(f"{n}_{s}") for s in ("sq", "added", "sum", "std", "inverse", "diagonal", "spread"))
                self.value, self.rstd, self.hi, self.ready = (
                    sem(f"{n}_{s}") if s in more else None for s in ("value", "rstd", "hi", "ready"))

        norms = {n: Norm(n, ("value",)) for n in ("mix_post", "mem_post", "ffn_post")}
        norms.update({n: Norm(n, ("rstd", "hi", "ready")) for n in ("mem_pre", "ffn_pre", "ffn_2")})
        norms["mixer_2"] = Norm("mixer_2", ("value", "rstd", "hi", "ready"))

        class Turn:

            def __init__(self, n):
                self.turned, self.hi, self.read = sem(f"{n}_turned"), sem(f"{n}_hi"), sem(f"{n}_read")

        turns = {n: Turn(n) for n in ("x", "xs", "mem", "mix", "memo", "dil")}

        VEC = {"mix_pre": 0, "mix_post": 8, "mem_pre": 16, "mem_kv_pre": 24, "mem_post": 32, "ffn_pre": 40,
               "ffn_post": 48, "mixer_2": 56, "ffn_2": 64, "fox_out": 72, "chunk_out": 76, "conv_b": 80,
               "tap0": 128, "tap1": 172, "tap2": 256, "q_gain": 300, "k_gain": 303}

        def vcol(name, k):
            return vec[:, ds(k + VEC[name], 1)]

        class Units:

            def __init__(self, base, pads0, pads, pairs, width):
                self.base, self.pads0, self.pads, self.pairs, self.width = base, pads0, pads, pairs, width

            def number(self, p, u):
                return p * 8 + (self.base + u)

            def last(self, p):
                return isinstance(p, int) and p == self.pairs - 1

            def padded(self, p, half):
                return p * (2 * self.pads) + (self.pads0 + (half + 1) * self.pads)

            def keys(self, u):
                return (u % 4 + 1) * 128

            ahead, deep = 2, 4

            def scores(self, u):
                return ps[:, (4, 5, 0, 1)[u % 4], 0:self.keys(u)]

            def probs(self, u):
                return slots(0, 4, S)[:, u % 4, 0:self.keys(u)]

            def turned(self, u):
                return ps[:, 6 + u % 2, 0:self.keys(u)]

            def probs_t(self, u):
                return slots(4 * S, 2, S)[:, u % 2, 0:self.keys(u)]

            def turn_free(self, n):
                return n - 1

            def pipeline(self, eng, lead, turn=None, values=None):
                ahead = self.ahead

                def step(p, t, leads=True):
                    if leads:
                        lead(p + (t + ahead) // 8, (t + ahead) % 8)
                    if turn:
                        turn(p + t // 8, t % 8)
                    if values and t:
                        values(p + (t - 1) // 8, (t - 1) % 8)

                for u in range(ahead):
                    lead(0, u)
                step(0, 0)
                with eng.Fori(0, self.pairs - 1) as p:
                    for t in range(1, 9):
                        step(p, t)
                for t in range(1, 8):
                    step(self.pairs - 1, t, t < 8 - ahead)
                if values:
                    values(self.pairs - 1, 7)

        class Heads64(Units):

            def __init__(self, base, pads0, pads, q, v, out):
                super().__init__(base, pads0, pads, 4, 64)
                self.q, self.v, self.to = q, v, out

            def pad(self, dve, p, half):
                rows = slice(64 * half, 64 * half + 64)
                dve.tensor_scalar(q_pad_1[rows, half, :], arena[rows, ds(p * S + (QK_1 + self.q * S), S)], 0.125, None,
                                  ALU.mult).then_inc(q_padded, 1)
                if self.pads == 2:
                    dve.tensor_copy(sel_pad[:, half, :], sel_col[:, ds(p * 2 + half, 1)].to_broadcast([128, 128]))\
                       .then_inc(q_padded, 1)

            def score(self, pe, p, u):
                half, i, n = u // 4, u % 4, self.keys(u)
                last = pe.matmul(self.scores(u), q_pad_1[:, half, i * 128:(i + 1) * 128],
                          flat(p * S + (QK_1 + (self.q + 4) * S), n), start=True, stop=self.pads == 1)
                if self.pads == 1:
                    return last
                pe.matmul(self.scores(u), sel_pad[:, half, :], decay[:, 0:n], start=False, stop=False)
                return pe.matmul(self.scores(u)[:, n - 128:n], ident_r[:, :], causal, start=False, stop=True)

            def bias(self, u):
                return rel_pad[:, u // 4, (3 - u % 4) * 128:S]

            def value(self, p, u, b):
                return flat(p * 128 + (V_1 + (self.v + b) * HW + u // 4 * 64), 64)

            def out(self, p, u):
                return flat(p * 128 + (HEADS_1 + u % 4 * D + self.to + u // 4 * 64), 64)

        class MemoryHeads(Units):

            def keys(self, u):
                return N_MEM

            def pad(self, dve, p, half):
                dve.tensor_scalar(mem_q_pad[:, 2 * half:2 * half + 2, :],
                                  flat(p * (4 * S) + (MEM_Q + half * 2 * S), 2 * S).rearrange("p (a n) -> p a n", a=2),
                                  0.0625, None, ALU.mult).then_inc(q_padded, 1)

            def score(self, pe, p, u):
                half, i = u // 4, u % 4
                for k in range(2):
                    last = pe.matmul(self.scores(u), mem_q_pad[:, 2 * half + k, i * 128:(i + 1) * 128],
                                     flat(p * (4 * N_MEM) + (MEM_K + (2 * half + k) * N_MEM), N_MEM),
                                     start=k == 0, stop=k == 1)
                return last

            def value(self, p, u, b):
                return flat(p * 512 + (MEM_V + b * D + u // 4 * 256), 256)

            def out(self, p, u):
                return flat(p * 512 + (HEADS_1 + u % 4 * D + u // 4 * 256), 256)

        class DilatedHeads(Units):

            ahead, deep = 1, 2

            def keys(self, u):
                return 768

            def probs(self, u):
                return slots(0, 2, 768)[:, u % 2, :]

            def probs_t(self, u):
                return slots(1536, 2, 768)[:, u % 2, :]

            def scores(self, u):
                b = 4 * (1 - u % 2)
                return ps[:, b:b + 2, :].rearrange("p b n -> p (b n)")[:, 0:768]

            def turned(self, u):
                return ps[:, 6:8, :].rearrange("p b n -> p (b n)")[:, 0:768]

            def turn_free(self, n):
                return n

            def pad(self, dve, p, half):
                rows = slice(64 * half, 64 * half + 64)
                for g in range(3):
                    dve.tensor_scalar(q_pad_2[rows, 3 * half + g, :], arena[rows, ds(p * S + 8 * g * S, S)], 0.125, None,
                                      ALU.mult).then_inc(q_padded, 1)

            def score(self, pe, p, u):
                half, r = u // 4, u % 4
                out, own = self.scores(u), slice(r * 128, (r + 1) * 128)
                pe.matmul(out[:, S:768], ident_r[:, :], stride_masks, start=True, stop=False)
                for g in (1, 2):
                    at = S + (g - 1) * 128
                    pe.matmul(out[:, at:at + 128], q_pad_2[:, 3 * half + g, own],
                              flat(p * S + ((8 * g + 4) * S + r * 128), 128), start=False, stop=g == 2)
                pe.matmul(out[:, 0:S], q_pad_2[:, 3 * half, own], flat(p * S + 4 * S, S), start=True, stop=False)
                return pe.matmul(out[:, 0:S], ident_r[:, :], band[:, (3 - r) * 128:(7 - r) * 128], start=False, stop=True)

            def value(self, p, u, b):
                tile = b if b < 4 else 4 * (b - 3) + u % 4
                return flat(p * 128 + (V_2 + tile * HW + u // 4 * 64), 64)

            def out(self, p, u):
                return flat(p * S + (u % 4 * 128 + u // 4 * 64), 64)

        FOX = Heads64(CREDIT, 0, 2, 0, 0, 0)
        CHUNKED = Heads64(CREDIT + 32, 16, 1, 8, 4, HW)
        MEMORY = MemoryHeads(CREDIT + 64, 24, 1, 2, 256)
        DILATED = DilatedHeads(CREDIT + 80, 28, 3, 4, 64)

        def dil_groups(eng, body):
            for c in range(6):
                body(0, c)
            with eng.Fori(1, 3) as grp:
                for c in range(6):
                    body(grp, c)

        block = ctx.enter_context(nc.Block())

        @block.sync
        def _(sp):
            def load_chunk(ch):
                sp.wait_ge(weights_split, ch.g + (CREDIT - 1))
                src = views[ch.gemm.name][ch.c]
                dst = raw[:, ch.slot, 0:HEADS * KT if ch.first else CHUNK]
                if len(src.shape) == 4:
                    dst = dst.rearrange("p (k h n) -> p k h n", k=KT, h=2)
                    halves = [(dst[:, :, h, :], src[:, :, h, :]) for h in range(2)]
                else:
                    k = src.shape[1]
                    dst = dst.rearrange("p (k n) -> p k n", k=k)
                    halves = [(dst[:, h * k // 2:(h + 1) * k // 2, :], src[:, h * k // 2:(h + 1) * k // 2, :])
                              for h in range(2)]
                for to, of in halves:
                    sp.dma_start(to, of).then_inc(raw_loaded[ch.slot], 16)

            for b in range(4):
                sp.dma_start(x_tok[:, b, :], A["x"][0, b * 128:(b + 1) * 128, :]).then_inc(x_loaded[b], 16)
            for name, *_ in GEMMS:
                over_chunks(sp, G[name], load_chunk)
            by_tile = out[0].rearrange("(b p) n -> p b n", p=128)
            for f in range(KT):
                sp.wait_ge(out_copied, f + 1)
                sp.dma_start(by_tile[:, :, f * 128:(f + 1) * 128],
                             out_tok[:, f, :].rearrange("p (b n) -> p b n", b=4)).then_inc(out_stored, 16)
            sp.wait_ge(out_stored, KT * 16)

        @block.gpsimd
        def _(pool):
            pool.memset(ident[:, :], 0.0).then_inc(const_step, 1)
            pool.memset(causal_made, 0.0).then_inc(const_step, 1)
            pool.memset(sel_col[:, :], 0.0).then_inc(const_step, 1)
            pool.memset(ones[:, :], 1.0).then_inc(const_ready, 1)
            for n in ("mix_post", "mem_post", "ffn_post"):
                pool.sem_inc(norms[n].added, CREDIT)
            pool.memset(decay.bitcast(F), 0.0).then_inc(const_ready, 1)
            pool.wait_ge(const_step, 3)
            pool.affine_select(out=ident[:, :], in_=ident[:, :], compare_op=ALU.not_equal, fill=1.0,
                               base=0, pattern=[[-1, 128]], channel_multiplier=1).then_inc(const_ready, 1)
            pool.affine_select(out=causal_made, in_=causal_made, compare_op=ALU.is_ge, fill=NEG,
                               base=0, pattern=[[-1, 128]], channel_multiplier=1).then_inc(const_ready, 1)
            pool.affine_select(out=sel_col[:, :], in_=sel_col[:, :], compare_op=ALU.not_equal, fill=-1.0,
                               base=0, pattern=[[-1, HEADS]], channel_multiplier=1).then_inc(const_step, 1)
            pool.wait_ge(const_step, 4)
            pool.affine_select(out=sel_col[:, :], in_=sel_col[:, :], compare_op=ALU.not_equal, fill=-1.0,
                               base=-32, pattern=[[-1, HEADS]], channel_multiplier=1).then_inc(const_ready, 1)
            pool.wait_ge(rel_row, 2)
            pool.dma_start(rel_dram, rel_rows).then_inc(rel_stored, 16)
            pool.wait_ge(rel_stored, 16)
            pool.wait_ge(turns["x"].turned, KT)
            pool.dma_start(rel_back, bass.AP(rel_dram.tensor, 0, [[1, 128], [640, HEADS], [1, S]]))\
                .then_inc(rel_spread, 16)
            pool.wait_ge(rel_spread, 16)
            pool.tensor_copy(rel, rel_back[:, :, ::-1]).then_inc(rel_row, 1)
            pool.wait_ge(rel_row, 3)
            pool.memset(rel[0:64, :, S - 64:S], NEG).then_inc(rel_ready, 1)
            pool.wait_ge(rel_ready, 1)
            for b in range(2):
                pool.dma_start(mem_tok[:, 2 * b:2 * b + 2, :],
                               A["mem"][0, b * 128:(b + 1) * 128, :].rearrange("p (h n) -> p h n", h=2))\
                    .then_inc(mem_loaded, 16)
            pool.wait_ge(scores_done, CREDIT + 32)
            with pool.Fori(0, HEADS // 2) as p:
                for half in range(2):
                    pool.wait_ge(max_done, p * 8 + (CHUNKED.base + 4 * half - 4))
                    pool.tensor_copy(rel_pad[:, half, :], flat(p * (2 * S) + (REL + half * S), S))\
                        .then_inc(rel_padded, 1)
            pool.wait_ge(max_done, CREDIT + 64)
            pool.memset(masks_made, 0.0).then_inc(mask_step, 1)
            pool.wait_ge(mask_step, 1)
            pool.affine_select(out=band_made, in_=band_made, compare_op=ALU.is_ge, fill=NEG, base=3,
                               pattern=[[-1, 7], [-4, 128]], channel_multiplier=4).then_inc(mask_step, 1)
            pool.wait_ge(mask_step, 2)
            pool.affine_select(out=band_made, in_=band_made, compare_op=ALU.is_ge, fill=NEG, base=125,
                               pattern=[[1, 7], [4, 128]], channel_multiplier=-4).then_inc(mask_ready, 1)
            pool.affine_select(out=stride_made, in_=stride_made, compare_op=ALU.is_ge, fill=NEG, base=0,
                               pattern=[[0, 2], [-1, 128]], channel_multiplier=1).then_inc(mask_ready, 1)

            def sum_squares(norm):
                for k in range(KT):
                    pool.wait_ge(norm.sq, k + 1)
                    if k == 0:
                        pool.tensor_copy(square_sum, squares[:, 0, :]).then_inc(norm.added, 1)
                    else:
                        pool.wait_ge(norm.added, CREDIT + k)
                        pool.tensor_tensor(square_sum, square_sum, squares[:, k % 4, :], ALU.add)\
                            .then_inc(norm.added, 1)

            def add_residual(name, y):
                for k in range(KT):
                    pool.wait_ge(norms[name].value, k + 1)
                    pool.tensor_tensor(x_t[:, k, :], x_t[:, k, :], y[:, k, :], ALU.add).then_inc(x_added[name], 1)

            def split_lo(ch):
                pool.wait_ge(weights_split, ch.g + (1 + CREDIT))
                pool.wait_ge(weights_hi, ch.g + 2)
                pool.tensor_tensor(w_lo[:, ch.next_slot, :], raw[:, ch.next_slot, :],
                                   w_hi[:, ch.next_slot, :].bitcast(F), ALU.subtract).then_inc(weights_split, 1)

            pool.wait_ge(mask_ready, 2)
            for name, y, gemm in (("mix_post", y_1, "mem_q"), ("mem_post", y_1, "ffn_up")):
                sum_squares(norms[name])
                split_lo(Chunk(G[gemm], 0, 2, 0))
                add_residual(name, y)
                split_lo(Chunk(G[gemm], 0, 2, 1))
            sum_squares(norms["ffn_post"])
            split_lo(Chunk(G["dil_in"], 0, 6, 0))
            add_residual("ffn_post", y_ffn)
            for c in range(1, 6):
                split_lo(Chunk(G["dil_in"], 0, 6, c))
            with pool.Fori(1, 3) as grp:
                for c in range(6):
                    split_lo(Chunk(G["dil_in"], grp, 6, c))
            for c in range(2):
                split_lo(Chunk(G["conv_up"], 0, 2, c))

        @block.scalar
        def _(act):
            def load_vectors():
                def rows(name, v):
                    n, at = v.shape[0] // 128, VEC[name]
                    act.dma_start(vec_rows[at % 128:at % 128 + n, at // 128, :],
                                  v.rearrange("(a n) -> a n", n=128)).then_inc(vec_loaded, 16)

                act.wait_ge(vec_cleared, 1)
                for name, key in (("mix_pre", "g_mix_pre"), ("mix_post", "g_mix_post"), ("mem_pre", "g_mem_pre"),
                                  ("mem_kv_pre", "g_mem_kv"), ("mem_post", "g_mem_post"), ("ffn_pre", "g_ffn_pre"),
                                  ("ffn_post", "g_ffn_post"), ("mixer_2", "mixer_norm_2"), ("ffn_2", "ffn_norm_2"),
                                  ("fox_out", "g_fox_out"), ("chunk_out", "g_chunk_out"), ("conv_b", "ffn_conv_b_2")):
                    rows(name, A[key][0])
                for tap in range(3):
                    rows(f"tap{tap}", A["ffn_conv_w_2"][0, tap])
                for name, key in (("q_gain", "attn_q_gain_2"), ("k_gain", "attn_k_gain_2")):
                    for half in range(2):
                        at = VEC[name]
                        act.dma_start(vec_rows[at % 128:at % 128 + 3, at // 128, half * 64:half * 64 + 64],
                                      A[key][0]).then_inc(vec_loaded, 16)
                act.dma_start(rel_rows[:, 64:256], A["rel_bias"][0]).then_inc(rel_loaded, 16)
                act.dma_start(gate_bias[:, :], A["b_fgate"][0].rearrange("(h a) -> h a", a=1),
                              allow_slow_non_contiguous=True).then_inc(vec_loaded, 16)

            def split_hi(ch):
                act.wait_ge(raw_loaded[ch.next_slot], ch.next_loads)
                if not ch.first:
                    act.wait_ge(tile_done, ch.before)
                act.activation(w_hi[:, ch.next_slot, :], raw[:, ch.next_slot, :], ACT.Copy).then_inc(weights_hi, 1)

            def root_of(norm, src, scale=1.0 / D):
                act.wait_ge(norm.sum, 1)
                act.activation(tok_std[:, :], src, ACT.Sqrt, bias=eps[:, :], scale=scale).then_inc(norm.std, 1)

            def keep_rstd(norm):
                act.wait_ge(norm.spread, 1)
                act.activation(rstd[:, :], ps[:, 5, :], ACT.Copy).then_inc(norm.rstd, 1)

            def gained_hi(name, ready):
                norm = norms[name]
                for k in range(KT):
                    act.wait_ge(ready, k + 1)
                    act.activation(a_hi[:, k, :], x_t[:, k, :], ACT.Identity, scale=vcol(name, k)).then_inc(norm.hi, 1)
                    act.activation(x_squares[name][:, k, :], x_t[:, k, :], ACT.Square).then_inc(norm.sq, 1)

            def rstd_out(name, gemm):
                split_hi(Chunk(G[gemm], 0, 2, 1))
                root_of(norms[name], ps[:, 4, 0:4])
                keep_rstd(norms[name])

            def squared(norm, k):
                if k >= 4:
                    act.wait_ge(norm.added, k - 3)
                act.activation(squares[:, k % 4, :], x_t[:, k, :], ACT.Square).then_inc(norm.sq, 1)

            def later_split_hi(ch):
                if not (ch.first_of_gemm or ch.second_of_gemm):
                    split_hi(ch)

            def turned_hi(turn, tiles, gain, columns):
                for f in range(tiles):
                    act.wait_ge(turn.turned, f + 1)
                    act.activation(columns(a_hi, f), ps[:, 4 + f % 4, :].rearrange("p (r j) -> p r j", r=4),
                                   ACT.Identity, scale=1.0 if gain is None else gain(f)).then_inc(turn.hi, 1)

            def gained_tiles(name):
                return lambda ch, j, src: act.activation(flat(ch.c * (2 * S) + (Y_1 + j * S), S), src, ACT.Identity,
                                                         scale=vcol(name, ch.c * 2 + j))

            def tiles_out(name, write, norm=None):
                def body(ch):
                    split_hi(ch)
                    for j in range(2):
                        act.wait_ge(tile_done, ch.before + (j + 1))
                        if norm is not None:
                            tile = 2 * ch.c + j
                            act.wait_ge(norm.added, tile + (CREDIT - 3))
                            act.activation(squares[:, 2 * ch.o + j, :], ps[:, 2 * ch.o + j, :], ACT.Square)\
                               .then_inc(norm.sq, 1)
                        write(ch, j, ps[:, (ch.o * 2 + j) % 4, :]).then_inc(freed["act"], 1)
                over_chunks(act, G[name], body)

            def feature_tiles(dst, first=0, tokens=S):
                return lambda ch, j, src: act.activation(
                    arena[:, ds(ch.c * (2 * tokens) + (dst + (first + j) * tokens), tokens)], src[:, 0:tokens], ACT.Copy)

            def token_tiles(dst, first):
                return lambda ch, j, src: act.activation(
                    dst[:, first + 2 * j:first + 2 * j + 2, ds(ch.c * 256, 256)],
                    src.rearrange("p (b n) -> p b n", b=2), ACT.Copy)

            def exps(units, p, u):
                n = units.number(p, u)
                act.wait_ge(max_done, n + 1)
                if units is CHUNKED:
                    act.wait_ge(recip_done, n - 3)
                    act.activation(units.probs(u), units.probs(u), ACT.Exp, scale=-1.0,
                                   bias=neg_max[:, u % 4:u % 4 + 1],
                                   accum_out=row_sum[:, u % 4:u % 4 + 1]).then_inc(probs_done, 1)
                    return
                act.wait_ge(turned, n + 1 - units.deep)
                act.wait_ge(recip_done, n - 3)
                act.activation(units.probs(u), units.scores(u), ACT.Exp, bias=neg_max[:, u % 4:u % 4 + 1],
                               accum_out=row_sum[:, u % 4:u % 4 + 1]).then_inc(probs_done, 1)

            def attention(units):
                units.pipeline(act, lead=lambda p, u: exps(units, p, u))

            act.sem_inc(freed["act"], CREDIT)
            act.sem_inc(probs_done, CREDIT)
            load_vectors()

            for b in range(4):
                act.wait_ge(x_squared, b + 1)
                act.activation(x_std[:, b:b + 1], x_sq[:, b:b + 1], ACT.Sqrt, scale=1.0 / D, bias=eps[:, :])\
                   .then_inc(x_rooted, 1)
                act.wait_ge(x_inverted, b + 1)
                act.activation(x_scaled[:, b, :], x_tok[:, b, :], ACT.Copy, scale=x_rstd[:, b:b + 1]).then_inc(x_ready, 1)
            act.wait_ge(raw_loaded[0], 32)
            act.activation(w_hi[:, 0, 0:HEADS * KT], raw[:, 0, 0:HEADS * KT], ACT.Copy).then_inc(weights_hi, 1)
            straight = lambda a, f: a[:, f, :].rearrange("p (r j) -> p r j", r=4)
            act.wait_ge(vec_ready, 1)
            turned_hi(turns["xs"], KT, lambda f: vcol("mix_pre", f), straight)

            z, e, u_, ln = (work[0:8, a * S:(a + 1) * S] for a in range(4))
            first = Chunk(G["forget"], 0, 2, 0)
            split_hi(first)
            act.wait_ge(tile_done, 1)
            act.wait_ge(const_ready, 6)
            act.activation(ident_r[:, :], ident[:, :], ACT.Copy).then_inc(decay_ready, 1)
            act.activation(causal, causal_made, ACT.Copy).then_inc(decay_ready, 1)
            act.activation(z, ps[0:8, 0, :], ACT.Identity, bias=gate_bias[:, :]).then_inc(freed["act"], 1)
            act.wait_ge(freed["act"], CREDIT + 1)
            act.activation(e, z, ACT.Abs).then_inc(gate_step, 1)
            act.wait_ge(gate_step, 1)
            act.activation(e, e, ACT.Exp, scale=-1.0).then_inc(gate_step, 1)
            act.wait_ge(gate_step, 3)
            act.activation(ln, u_, ACT.Ln).then_inc(gate_step, 1)

            act.wait_ge(gate_step, 12)
            act.activation(decay[0:8, :], decay_made, ACT.Copy).then_inc(decay_ready, 1)

            def x_out(tiles):
                for f in tiles:
                    act.wait_ge(turns["x"].turned, f + 1)
                    act.activation(x_t[:, f, :], ps[:, 4 + f % 4, :], ACT.Copy).then_inc(turns["x"].read, 1)

            x_out(range(4))
            tiles_out("fox_qk", feature_tiles(QK_1))
            x_out(range(4, KT))
            tiles_out("fox_v", token_tiles(v_1, 0))
            tiles_out("chunk_qk", feature_tiles(QK_1, 8))
            act.wait_ge(mem_step, 5)
            act.activation(mem_std[:, :], mem_sq[:, 0:2], ACT.Sqrt, scale=1.0 / D, bias=eps[:, :]).then_inc(mem_step, 1)
            tiles_out("chunk_v", token_tiles(v_1, 4))
            for f in range(KT):
                act.wait_ge(turns["mem"].turned, f + 1)
                act.activation(a_hi[:, f, 0:N_MEM], ps[:, 4 + f % 4, 0:N_MEM], ACT.Identity,
                               scale=vcol("mem_kv_pre", f)).then_inc(turns["mem"].hi, 1)
            attention(FOX)
            attention(CHUNKED)

            tiles_out("mem_k", feature_tiles(MEM_K, tokens=N_MEM))
            act.wait_ge(heads_done, CREDIT + 64)
            for b in range(4):
                for half in range(2):
                    n = 2 * b + half
                    if n >= 4:
                        act.wait_ge(row_step, n - 3)
                    act.activation(squares[:, n % 4, :], heads_1[:, b, half * HW:(half + 1) * HW], ACT.Square,
                                   accum_out=row_sq[:, n:n + 1]).then_inc(row_step, 1)
            act.wait_ge(row_step, 8)
            act.activation(row_std[:, :], row_sq[:, :], ACT.Sqrt, scale=1.0 / HW, bias=eps[:, :]).then_inc(row_step, 1)
            tiles_out("mem_v", lambda ch, j, src: act.activation(mem_v[:, j, ds(ch.c * 256, 256)],
                                                                 src[:, 0:256], ACT.Copy))
            turned_hi(turns["mix"], KT, lambda f: vcol("fox_out", f), straight)
            tiles_out("mix_out", gained_tiles("mix_post"), norms["mix_post"])
            split_hi(Chunk(G["mem_q"], 0, 2, 0))
            root_of(norms["mix_post"], ps[:, 4, 0:4])
            gained_hi("mem_pre", x_added["mix_post"])
            rstd_out("mem_pre", "mem_q")
            over_chunks(act, G["mem_q"], later_split_hi, peel=1)
            attention(MEMORY)
            turned_hi(turns["memo"], KT, None, straight)
            tiles_out("mem_o", gained_tiles("mem_post"), norms["mem_post"])
            split_hi(Chunk(G["ffn_up"], 0, 2, 0))
            root_of(norms["mem_post"], ps[:, 4, 0:4])
            gained_hi("ffn_pre", x_added["mem_post"])
            rstd_out("ffn_pre", "ffn_up")

            def gate(ch):
                later_split_hi(ch)
                if ch.last_of_gemm:
                    first_rows_hi("ffn_up", CREDIT)
                act.wait_ge(gate_scaled, ch.c + 1)
                act.wait_ge(hidden_written, ch.c + (CREDIT - 1))
                act.activation(gate_act[:, ch.slot_o, :], up[:, 2 * ch.slot_o, :], ACT.Silu).then_inc(silu_done, 1)

            def rows_hi(ch):
                if not ch.last:
                    split_hi(ch)
                if not ch.last_of_gemm:
                    to = 2 * ((ch.o + 1) % 2)
                    act.activation(a_hi[:, to:to + 2, :], pair_of_hidden(ch.c + 1), ACT.Copy).then_inc(hidden_hi, 1)

            def first_rows_hi(gemm, written):
                act.wait_ge(hidden_written, written + 2)
                act.wait_ge(rows_free[gemm], 1)
                act.activation(a_hi[:, 0:2, :], hidden[:, 0:2, :], ACT.Copy).then_inc(hidden_hi, 1)

            act.wait_ge(mask_ready, 8)
            act.activation(masks[:, :], masks_made, ACT.Copy).then_inc(mask_ready, 1)
            over_chunks(act, G["ffn_up"], gate, peel=1, tail=1)
            act.wait_ge(hidden_written, CREDIT + FT)
            over_chunks(act, G["ffn_down"], rows_hi)
            act.wait_ge(mask_ready, 9)
            for k in range(KT):
                norm = norms["ffn_post"]
                act.wait_ge(down_done[0], k + 1)
                if k >= 4:
                    act.wait_ge(norm.added, CREDIT + k - 3)
                act.activation(squares[:, k % 4, :], ps[:, k, :], ACT.Square).then_inc(norm.sq, 1)
                act.activation(y_ffn[:, k, :], ps[:, k, :], ACT.Identity, scale=vcol("ffn_post", k)).then_inc(freed_down, 1)
            split_hi(Chunk(G["dil_in"], 0, 6, 0))
            root_of(norms["ffn_post"], ps[:, 4, 0:4])

            for k in range(KT):
                act.wait_ge(x_added["ffn_post"], k + 1)
                squared(norms["mixer_2"], k)
            root_of(norms["mixer_2"], ps[:, 4, 0:4])
            keep_rstd(norms["mixer_2"])
            for k in range(KT):
                act.wait_ge(norms["mixer_2"].value, k + 1)
                act.activation(a_hi[:, k, :], normed[:, k % 2, :], ACT.Copy).then_inc(norms["mixer_2"].hi, 1)

            def dil_tiles(grp, c):
                ch = Chunk(G["dil_in"], grp, 6, c)
                if not ch.first_of_gemm:
                    split_hi(ch)
                if c < 4:
                    for j in range(2):
                        t, n = 2 * c + j, 8 * grp + (2 * c + j)
                        act.wait_ge(tile_done, ch.before + (j + 1))
                        act.wait_ge(dil_mean, n - 1 + CREDIT)
                        act.activation(squares[:, t % 2, :], ps[:, t % 4, :], ACT.Square).then_inc(dil_sq, 1)
                        act.wait_ge(dil_mean, n + 1 + CREDIT)
                        act.wait_ge(dil_rstd, n + CREDIT)
                        act.activation(std[:, :], ps[:, 4 + t % 2, :], ACT.Sqrt, bias=eps[:, :]).then_inc(dil_std, 1)

            dil_groups(act, dil_tiles)
            attention(DILATED)
            strided = lambda a, f: a[:, f, :].rearrange("p (j r) -> p r j", r=4)
            turned_hi(turns["dil"], 4, None, strided)

            over_chunks(act, G["dil_out"], split_hi)
            split_hi(Chunk(G["conv_up"], 0, 2, 0))
            gained_hi("ffn_2", x_block2)
            rstd_out("ffn_2", "conv_up")

            def conv_gate(ch):
                later_split_hi(ch)
                if ch.last_of_gemm:
                    first_rows_hi("conv_up", 2 * CREDIT + FT)
                for j in range(2):
                    act.wait_ge(up_scaled, 2 * ch.c + (j + 1 + FT))
                    act.wait_ge(hidden_written, ch.c + (2 * CREDIT + FT - 1))
                    act.activation(conv[:, 2 * ch.slot_o + j, :], up[:, 2 * ch.slot_o + j, :], ACT.Identity,
                                   bias=vcol("conv_b", ch.c + j * FT), scale=vcol("tap2", ch.c + j * FT))\
                       .then_inc(conv_base, 1)
                act.wait_ge(conv_tap, 4 * ch.c + 2)
                act.activation(gate_act[:, ch.slot_o, :], conv[:, 2 * ch.slot_o, :], ACT.Silu).then_inc(silu_done, 1)

            over_chunks(act, G["conv_up"], conv_gate, peel=1, tail=1)
            act.wait_ge(hidden_written, 2 * CREDIT + 2 * FT)
            over_chunks(act, G["conv_down"], rows_hi)
            for f in range(KT):
                act.wait_ge(out_turned, f + 1)
                act.activation(out_tok[:, f, :], ps[:, f, :], ACT.Copy).then_inc(out_copied, 1)

        @block.vector
        def _(dve):
            def split_lo(ch):
                if pool_splits(ch):
                    return
                if ch.gemm.name in ("mem_q", "ffn_up", "dil_out", "conv_up"):
                    dve.wait_ge(weights_split, ch.g + (1 + CREDIT))
                dve.wait_ge(weights_hi, ch.g + 2)
                dve.tensor_tensor(w_lo[:, ch.next_slot, :], raw[:, ch.next_slot, :],
                                  w_hi[:, ch.next_slot, :].bitcast(F), ALU.subtract).then_inc(weights_split, 1)

            def invert(norm):
                dve.wait_ge(norm.std, 1)
                dve.reciprocal(tok_rstd[:, :], tok_std[:, :]).then_inc(norm.inverse, 1)
                dve.wait_ge(norm.inverse, 1)
                dve.tensor_tensor(diagonal.rearrange("p (b n) -> p b n", b=4),
                                  ident[:, :].rearrange("p (b n) -> p b n", b=1).to_broadcast([128, 4, 128]),
                                  tok_rstd[:, :].rearrange("p (b n) -> p b n", n=1).to_broadcast([128, 4, 128]),
                                  ALU.mult).then_inc(norm.diagonal, 1)

            def operand(name, src):
                norm = norms[name]

                def value(k):
                    if k >= 2:
                        dve.wait_ge(norm.ready, k - 1)
                    dst = normed[:, k % 2, :].rearrange("p (r j) -> p j r", r=4)
                    a, b = (v.rearrange("p (j r) -> p j r", r=4) for v in (src[:, k, :], rstd[:, :]))
                    dve.scalar_tensor_tensor(out=dst, in0=a, scalar=vcol(name, k), in1=b,
                                             op0=ALU.mult, op1=ALU.mult).then_inc(norm.value, 1)
                value(0)
                for k in range(KT):
                    if k + 1 < KT:
                        value(k + 1)
                    dve.wait_ge(norm.hi, k + 1)
                    dve.tensor_tensor(a_lo[:, k, :], normed[:, k % 2, :], a_hi[:, k, :].bitcast(F),
                                      ALU.subtract).then_inc(norm.ready, 1)

            def invert_pre(name):
                dve.wait_ge(norms[name].sq, KT)
                dve.tensor_reduce(square_sum, x_squares[name].rearrange("p k n -> p n k"), axis=AX.X, op=ALU.add)\
                   .then_inc(norms[name].added, 1)
                invert(norms[name])

            def gained_lo(name, k):
                dve.wait_ge(norms[name].hi, k + 1)
                dve.scalar_tensor_tensor(out=a_lo[:, k, :], in0=x_t[:, k, :], scalar=vcol(name, k),
                                         in1=a_hi[:, k, :].bitcast(F), op0=ALU.mult, op1=ALU.subtract)\
                   .then_inc(norms[name].ready, 1)

            def residual(name, y, after=None):
                norm = norms[name]
                invert(norm)
                dve.wait_ge(norm.spread, 1)
                for k in range(KT + 2):
                    if k < KT:
                        dve.tensor_tensor(y[:, k, :], y[:, k, :], ps[:, 5, :], ALU.mult).then_inc(norm.value, 1)
                    if after and k >= 2:
                        gained_lo(after, k - 2)

            def turned_lo(turn, tiles, gain, columns):
                for f in range(tiles):
                    dve.wait_ge(turn.hi, f + 1)
                    src = ps[:, 4 + f % 4, :].rearrange("p (r j) -> p r j", r=4)
                    hi = columns(a_hi, f).bitcast(F)
                    if gain is None:
                        dve.tensor_tensor(columns(a_lo, f), src, hi, ALU.subtract).then_inc(turn.read, 1)
                    else:
                        dve.scalar_tensor_tensor(out=columns(a_lo, f), in0=src, scalar=gain(f), in1=hi,
                                                 op0=ALU.mult, op1=ALU.subtract).then_inc(turn.read, 1)

            def splits(name):
                over_chunks(dve, G[name], split_lo)

            def pad(units, p, half):
                units.pad(dve, p, half)

            def lead(units):
                def f(p, u):
                    n = units.number(p, u)
                    dve.wait_ge(scores_done, n + 1)
                    dve.wait_ge(probs_done, n - 3)
                    if units is CHUNKED:
                        dve.wait_ge(turned, n + 1 - units.deep)
                        if u % 4 == 0:
                            dve.wait_ge(rel_padded, p * 2 + (u // 4 + 1))
                        dve.sem_inc(bias_open, 1)
                        dve.tensor_tensor_reduce(out=units.probs(u), in0=units.scores(u),
                                                 in1=units.bias(u), scale=-1.0, scalar=3e38, op0=ALU.add,
                                                 op1=ALU.min, accum_out=neg_max[:, u % 4:u % 4 + 1])\
                           .then_inc(max_done, 1)
                        if u in (3, 7) and not units.last(p):
                            pad(units, p + 1, u // 4)
                        return
                    dve.tensor_reduce(neg_max[:, u % 4:u % 4 + 1], units.scores(u), axis=AX.X, op=ALU.max,
                                      negate=True).then_inc(max_done, 1)
                    if u in (3, 7) and not units.last(p):
                        pad(units, p + 1, u // 4)
                return f

            def turned_out(units):
                def f(p, u):
                    n = units.number(p, u)
                    dve.wait_ge(turned, n + 1)
                    dve.wait_ge(values_done, n - 1)
                    dve.tensor_copy(units.probs_t(u), units.turned(u)).then_inc(turned_read, 1)
                return f

            def heads_out(units):
                def f(p, u):
                    n = units.number(p, u)
                    dve.wait_ge(probs_done, n + 1)
                    dve.reciprocal(row_recip[:, u % 4:u % 4 + 1], row_sum[:, u % 4:u % 4 + 1]).then_inc(recip_done, 1)
                    dve.wait_ge(recip_done, n + 1)
                    dve.wait_ge(values_done, n + 1)
                    dve.tensor_scalar(units.out(p, u), ps[:, 2 + u % 2, 0:units.width], row_recip[:, u % 4:u % 4 + 1],
                                      None, ALU.mult).then_inc(heads_done, 1)
                return f

            def attention(units):
                for half in range(2):
                    pad(units, 0, half)
                units.pipeline(dve, lead=lead(units), turn=turned_out(units), values=heads_out(units))

            dve.memset(vec_rows, 0.0).then_inc(vec_cleared, 1)
            dve.memset(eps[:, :], EPS).then_inc(const_ready, 1)
            dve.memset(mean_head[:, :], 0.0).then_inc(pad_cleared, 1)
            dve.wait_ge(pad_cleared, 1)
            dve.memset(mean_head[0:64, 0:64], 1.0 / 64).then_inc(pad_cleared, 1)
            dve.memset(mean_head[64:128, 64:128], 1.0 / 64).then_inc(pad_cleared, 1)
            dve.sem_inc(weights_split, CREDIT)
            dve.sem_inc(freed["dve"], CREDIT)
            dve.sem_inc(hidden_written, CREDIT)
            dve.sem_inc(dil_rstd, CREDIT)
            for s in (max_done, turned_read, recip_done, heads_done):
                dve.sem_inc(s, CREDIT)

            for b in range(4):
                dve.wait_ge(x_loaded[b], 16)
                dve.tensor_tensor_reduce(out=work[:, (b % 2) * D:(b % 2 + 1) * D], in0=x_tok[:, b, :], in1=x_tok[:, b, :],
                                         scale=1.0, scalar=0.0, op0=ALU.mult, op1=ALU.add,
                                         accum_out=x_sq[:, b:b + 1]).then_inc(x_squared, 1)
                dve.wait_ge(x_rooted, b + 1)
                dve.reciprocal(x_rstd[:, b:b + 1], x_std[:, b:b + 1]).then_inc(x_inverted, 1)
            dve.wait_ge(vec_turned, 3)
            dve.tensor_copy(vec[:, :], ps[:, 0, 0:384]).then_inc(vec_ready, 1)
            dve.wait_ge(vec_ready, 1)
            dve.wait_ge(weights_hi, 1)
            dve.tensor_tensor(w_lo[:, 0, 0:HEADS * KT], raw[:, 0, 0:HEADS * KT], w_hi[:, 0, 0:HEADS * KT].bitcast(F),
                              ALU.subtract).then_inc(weights_split, 1)
            straight = lambda a, f: a[:, f, :].rearrange("p (r j) -> p r j", r=4)
            turned_lo(turns["xs"], KT, lambda f: vcol("mix_pre", f), straight)
            split_lo(Chunk(G["forget"], 0, 2, 0))

            z, e, u_, ln = (work[0:8, a * S:(a + 1) * S] for a in range(4))
            r, w = std[0:8, :], rstd[0:8, :]
            dve.wait_ge(gate_step, 2)
            dve.tensor_scalar(u_, e, 1.0, None, ALU.add).then_inc(gate_step, 1)
            dve.wait_ge(gate_step, 4)
            dve.tensor_scalar(r, u_, -1.0, None, ALU.add).then_inc(gate_step, 1)
            dve.wait_ge(gate_step, 5)
            dve.tensor_tensor(r, e, r, ALU.subtract).then_inc(gate_step, 1)
            dve.reciprocal(w, u_).then_inc(gate_step, 1)
            dve.wait_ge(gate_step, 7)
            dve.tensor_tensor(r, r, w, ALU.mult).then_inc(gate_step, 1)
            dve.wait_ge(gate_step, 8)
            dve.tensor_tensor(r, r, ln, ALU.add).then_inc(gate_step, 1)
            dve.wait_ge(gate_step, 9)
            dve.scalar_tensor_tensor(out=r, in0=z, scalar=0.0, in1=r, op0=ALU.min, op1=ALU.subtract)\
               .then_inc(gate_step, 1)
            dve.memset(w, 1.0).then_inc(gate_step, 1)
            dve.wait_ge(gate_step, 11)
            dve.tensor_tensor_scan(decay_made, w, r, 0.0, ALU.mult, ALU.add).then_inc(gate_step, 1)
            dve.wait_ge(decay_ready, 3)
            dve.tensor_tensor(decay[32:40, :], decay_made, decay[0:8, :].bitcast(F), ALU.subtract)\
               .then_inc(decay_ready, 1)

            dve.wait_ge(rel_loaded, 16)
            dve.tensor_copy(rel_rows[:, 0:64], rel_rows[:, 64:65].to_broadcast([HEADS, 64])).then_inc(rel_row, 1)
            dve.tensor_copy(rel_rows[:, 256:640], rel_rows[:, 255:256].to_broadcast([HEADS, 384])).then_inc(rel_row, 1)

            for name in ("fox_qk", "fox_v", "chunk_qk"):
                splits(name)
            dve.wait_ge(mem_loaded, 32)
            for n in range(4):
                dve.tensor_tensor_reduce(out=slots(0, 4, S)[:, n, :], in0=mem_tok[:, n, :], in1=mem_tok[:, n, :],
                                         scale=1.0, scalar=0.0, op0=ALU.mult, op1=ALU.add,
                                         accum_out=mem_sq[:, n:n + 1]).then_inc(mem_step, 1)
            dve.wait_ge(mem_step, 4)
            halves = mem_sq[:, :].rearrange("p (b h) -> p h b", h=2)
            dve.tensor_tensor(mem_sq[:, 0:2], halves[:, 0, :], halves[:, 1, :], ALU.add).then_inc(mem_step, 1)
            dve.wait_ge(mem_step, 6)
            dve.reciprocal(mem_rstd[:, :], mem_std[:, :]).then_inc(mem_step, 1)
            dve.wait_ge(mem_step, 7)
            for n in range(4):
                dve.tensor_scalar(mem_tok[:, n, :], mem_tok[:, n, :], mem_rstd[:, n // 2:n // 2 + 1], None,
                                  ALU.mult).then_inc(mem_scaled, 1)
            splits("chunk_v")
            for f in range(KT):
                dve.wait_ge(turns["mem"].hi, f + 1)
                dve.scalar_tensor_tensor(out=a_lo[:, f, 0:N_MEM], in0=ps[:, 4 + f % 4, 0:N_MEM],
                                         scalar=vcol("mem_kv_pre", f), in1=a_hi[:, f, 0:N_MEM].bitcast(F),
                                         op0=ALU.mult, op1=ALU.subtract).then_inc(turns["mem"].read, 1)
            dve.memset(q_pad_1, 0.0).then_inc(pad_cleared, 1)
            dve.wait_ge(pad_cleared, 4)
            dve.wait_ge(freed["act"], CREDIT + G["chunk_v"].freed_end)
            dve.wait_ge(rel_ready, 1)
            attention(FOX)
            attention(CHUNKED)

            splits("mem_k")
            dve.wait_ge(row_step, 9)
            dve.reciprocal(row_rstd[:, :], row_std[:, :]).then_inc(row_step, 1)
            dve.wait_ge(row_step, 10)
            for b in range(4):
                for half in range(2):
                    n = 2 * b + half
                    part = heads_1[:, b, half * HW:(half + 1) * HW]
                    dve.tensor_scalar(part, part, row_rstd[:, n:n + 1], None, ALU.mult).then_inc(heads_scaled, 1)
            splits("mem_v")
            turned_lo(turns["mix"], KT, lambda f: vcol("fox_out", f), straight)
            splits("mix_out")
            dve.wait_ge(mask_ready, 2)
            dve.tensor_reduce(mod4[:, :], ident[:, :].rearrange("p (a b) -> p b a", b=4), axis=AX.X, op=ALU.add)\
               .then_inc(mask_ready, 1)
            dve.wait_ge(mask_ready, 3)
            dve.tensor_scalar(mod4[:, :], mod4[:, :], -1.0, -NEG, ALU.add, ALU.mult).then_inc(mask_ready, 1)
            dve.wait_ge(mask_ready, 4)
            for b in range(4):
                part = stride_made[:, 128:256].rearrange("p (a b) -> p b a", b=4)[:, b, :]
                dve.tensor_scalar(part, part, mod4[:, b:b + 1], None, ALU.add).then_inc(mask_ready, 1)
            residual("mix_post", y_1, "mem_pre")
            invert_pre("mem_pre")

            def mem_q_out(ch):
                if ch.first_of_gemm:
                    dve.wait_ge(norms["mem_pre"].rstd, 1)
                split_lo(ch)
                for j in range(2):
                    dve.wait_ge(tile_done, ch.before + (j + 1))
                    dve.tensor_tensor(flat(ch.c * (2 * S) + (MEM_Q + j * S), S), ps[:, 2 * ch.slot_o + j, :], rstd[:, :],
                                      ALU.mult).then_inc(freed["dve"], 1)
            over_chunks(dve, G["mem_q"], mem_q_out, peel=1)
            dve.wait_ge(freed["dve"], CREDIT + G["mem_q"].freed_end)
            attention(MEMORY)
            turned_lo(turns["memo"], KT, None, straight)
            splits("mem_o")
            residual("mem_post", y_1, "ffn_pre")
            invert_pre("ffn_pre")

            def scaled(ch, j, signal):
                dve.wait_ge(tile_done, ch.before + (j + 1))
                dve.tensor_tensor(up[:, 2 * ch.slot_o + j, :], ps[:, 2 * ch.slot_o + j, :], rstd[:, :],
                                  ALU.mult).then_inc(signal, 1)

            def gated(ch):
                if ch.first_of_gemm:
                    dve.wait_ge(norms["ffn_pre"].rstd, 1)
                split_lo(ch)
                if ch.last_of_gemm:
                    first_rows_lo(0)
                dve.wait_ge(hidden_written, ch.c + (CREDIT - 1))
                scaled(ch, 0, gate_scaled)
                scaled(ch, 1, up_scaled)
                dve.wait_ge(gate_scaled, ch.c + 1)
                dve.wait_ge(up_scaled, ch.c + 1)
                dve.sem_inc(freed["dve"], 2)
                dve.wait_ge(silu_done, ch.c + 1)
                dve.tensor_tensor(arena[:, ds(ch.c * S, S)], gate_act[:, ch.slot_o, :],
                                  up[:, 2 * ch.slot_o + 1, :], ALU.mult).then_inc(hidden_written, 1)

            def rows_lo(ch, base):
                if not ch.last:
                    split_lo(ch)
                if not ch.last_of_gemm:
                    to = 2 * ((ch.o + 1) % 2)
                    dve.wait_ge(hidden_hi, ch.c + (base + 2))
                    dve.tensor_tensor(a_lo[:, to:to + 2, :], pair_of_hidden(ch.c + 1),
                                      a_hi[:, to:to + 2, :].bitcast(F), ALU.subtract).then_inc(hidden_split, 1)

            def first_rows_lo(base):
                dve.wait_ge(hidden_hi, base + 1)
                dve.tensor_tensor(a_lo[:, 0:2, :], hidden[:, 0:2, :], a_hi[:, 0:2, :].bitcast(F),
                                  ALU.subtract).then_inc(hidden_split, 1)

            over_chunks(dve, G["ffn_up"], gated, peel=1, tail=1)
            over_chunks(dve, G["ffn_down"], lambda ch: rows_lo(ch, 0))
            residual("ffn_post", y_ffn)
            invert(norms["mixer_2"])
            dve.wait_ge(norms["mixer_2"].rstd, 1)
            operand("mixer_2", x_t)

            def dil_tiles(grp, c):
                ch = Chunk(G["dil_in"], grp, 6, c)
                for j in range(2):
                    if c < 4:
                        t, n = 2 * c + j, 8 * grp + (2 * c + j)
                        dve.wait_ge(dil_std, n + 1)
                        dve.wait_ge(freed["dve"], ch.freed + (j + CREDIT))
                        dve.reciprocal(rstd[:, :], std[:, :]).then_inc(dil_rstd, 1)
                        dve.wait_ge(dil_rstd, n + 1 + CREDIT)
                        dve.scalar_tensor_tensor(
                            out=arena[:, ds(n * S, S)], in0=ps[:, t % 4, :],
                            scalar=vcol("q_gain" if c < 2 else "k_gain", grp), in1=rstd[:, :],
                            op0=ALU.mult, op1=ALU.mult).then_inc(freed["dve"], 1)
                    else:
                        t = 2 * c + j
                        dve.wait_ge(tile_done, ch.before + (j + 1))
                        dve.tensor_copy(v_2[:, ds(4 * grp + 2 * j, 2), (c - 4) * 256:(c - 3) * 256],
                                        ps[:, t % 4, :].rearrange("p (b n) -> p b n", b=2))\
                           .then_inc(freed["dve"], 1)
            dil_groups(dve, dil_tiles)
            dve.wait_ge(freed["dve"], CREDIT + G["dil_in"].freed_end)
            dve.memset(q_pad_2, 0.0).then_inc(pad_cleared, 1)
            dve.wait_ge(pad_cleared, 5)
            attention(DILATED)
            turned_lo(turns["dil"], 4, None, lambda a, f: a[:, f, :].rearrange("p (j r) -> p r j", r=4))

            def wide(ch):
                split_lo(ch)
                for j in range(4):
                    dve.wait_ge(tile_done, ch.before + (j + 1))
                    xt = x_flat[:, ds(ch.c * (4 * S) + j * S, S)]
                    dve.tensor_tensor(xt, xt, ps[:, j, :], ALU.add).then_inc(x_block2, 1)
                dve.wait_ge(x_block2, 4 * ch.c + 4)
                dve.sem_inc(freed["dve"], 4)
            over_chunks(dve, G["dil_out"], wide)
            for k in range(KT):
                gained_lo("ffn_2", k)
            invert_pre("ffn_2")

            def convolved(ch):
                if ch.first_of_gemm:
                    dve.wait_ge(norms["ffn_2"].rstd, 1)
                split_lo(ch)
                if ch.last_of_gemm:
                    first_rows_lo(11)
                for j in range(2):
                    dve.wait_ge(hidden_written, ch.c + (2 * CREDIT + FT - 1))
                    scaled(ch, j, up_scaled)
                dve.wait_ge(up_scaled, 2 * ch.c + (2 + FT))
                dve.sem_inc(freed["dve"], 2)
                for j in range(2):
                    u, src = conv[:, 2 * ch.slot_o + j, :], up[:, 2 * ch.slot_o + j, :]
                    for tap in (1, 2):
                        if tap == 1:
                            dve.wait_ge(conv_base, 2 * ch.c + (j + 1))
                        else:
                            dve.wait_ge(conv_tap, 4 * ch.c + (2 * j + 1))
                        dve.scalar_tensor_tensor(out=u[:, tap:S], in0=src[:, 0:S - tap],
                                                 scalar=vcol(f"tap{2 - tap}", ch.c + j * FT), in1=u[:, tap:S],
                                                 op0=ALU.mult, op1=ALU.add).then_inc(conv_tap, 1)
                dve.wait_ge(conv_tap, 4 * ch.c + 4)
                dve.wait_ge(silu_done, ch.c + (FT + 1))
                dve.tensor_tensor(arena[:, ds(ch.c * S, S)], gate_act[:, ch.slot_o, :],
                                  conv[:, 2 * ch.slot_o + 1, :], ALU.mult).then_inc(hidden_written, 1)

            dve.wait_ge(hidden_written, CREDIT + FT)
            dve.sem_inc(hidden_written, CREDIT)
            over_chunks(dve, G["conv_up"], convolved, peel=1, tail=1)
            over_chunks(dve, G["conv_down"], lambda ch: rows_lo(ch, 11))
            for k in range(KT):
                dve.wait_ge(down_done[1], k + 1)
                dve.tensor_tensor(x_t[:, k, :], x_t[:, k, :], ps[:, k, :], ALU.add).then_inc(x_final, 1)

        @block.tensor
        def _(pe):
            def three(dst, stationary, moving, start, stop, across=False):
                (s_hi, s_lo), (m_hi, m_lo) = stationary, moving
                pe.matmul(dst, s_hi, m_hi, start=start, stop=False, skip_group_check=across)
                pe.matmul(dst, s_hi, m_lo, start=False, stop=False, skip_group_check=across)
                return pe.matmul(dst, s_lo, m_hi, start=False, stop=stop, skip_group_check=across)

            def weights(slot, k_tiles):
                return tuple(w[:, slot, :].rearrange("p (k n) -> p k n", k=k_tiles) for w in (w_hi, w_lo))

            def enter(name, previous):
                if previous and G[previous].freed_by:
                    pe.wait_ge(freed[G[previous].freed_by], CREDIT + G[previous].freed_end)

            def chunk_ready(ch):
                pe.wait_ge(weights_split, ch.g + 1 + CREDIT)

            def feature_chunk(ch, bank0, tokens=S, tiles=2, k_tiles=KT):
                by = ch.gemm.freed_by
                chunk_ready(ch)
                whi, wlo = weights(ch.slot, k_tiles)
                for j in range(tiles):
                    pe.wait_ge(freed[by], ch.freed + (j + 1))
                    cols = slice(j * 128, j * 128 + 128)
                    for k in range(k_tiles):
                        last = three(ps[:, (bank0 + j) % 4, 0:tokens], (whi[:, k, cols], wlo[:, k, cols]),
                                     (a_hi[:, k, 0:tokens], a_lo[:, k, 0:tokens]), k == 0, k == k_tiles - 1)
                        if ch.second_of_gemm and ch.gemm.name in deferred and j == 1 and k == 3:
                            spread(norms[deferred[ch.gemm.name]])
                    last.then_inc(tile_done, 1)
                    if ch.second_of_gemm and ch.gemm.name in deferred and j == 0:
                        norm = norms[deferred[ch.gemm.name]]
                        pe.wait_ge(norm.added, 1)
                        by_token(square_sum, True, True).then_inc(norm.sum, 1)

            deferred = {"mem_q": "mem_pre", "ffn_up": "ffn_pre", "conv_up": "ffn_2"}

            def closing(ch):
                chunk_ready(ch)
                whi, wlo = weights(ch.slot, KT)
                for k in range(KT):
                    for j in range(2):
                        if k == 0:
                            pe.wait_ge(freed[ch.gemm.freed_by], ch.freed + (j + 1))
                        cols = slice(j * 128, j * 128 + 128)
                        last = three(ps[:, 2 * ch.slot_o + j, :], (whi[:, k, cols], wlo[:, k, cols]),
                                     (a_hi[:, k, :], a_lo[:, k, :]), k == 0, k == KT - 1, across=True)
                        if k == KT - 1:
                            last.then_inc(tile_done, 1)
                    if k == 1:
                        last.then_inc(rows_free[ch.gemm.name], 1)

            def opening(ch, ready, after=None, tiles=2, k_tiles=KT):
                chunk_ready(ch)
                whi, wlo = weights(ch.slot, k_tiles)
                for k in range(k_tiles):
                    pe.wait_ge(ready, k + 1)
                    for j in range(tiles):
                        cols = slice(j * 128, j * 128 + 128)
                        last = three(ps[:, j, :], (whi[:, k, cols], wlo[:, k, cols]), (a_hi[:, k, :], a_lo[:, k, :]),
                                     k == 0, k == k_tiles - 1, across=True)
                        if k == k_tiles - 1:
                            last.then_inc(tile_done, 1)
                    if after:
                        after(k)

            def feature_major(name, previous, tokens=S, tiles=2, k_tiles=KT, ready=None, after=None, tail=0):
                enter(name, previous)

                def body(ch):
                    if ch.first_of_gemm and ready is not None:
                        opening(ch, ready, after, tiles, k_tiles)
                    elif ch.last_of_gemm and tail:
                        closing(ch)
                    else:
                        feature_chunk(ch, ch.o * tiles, tokens, tiles, k_tiles)
                over_chunks(pe, G[name], body, int(ready is not None), tail)

            def token_chunk(ch, by, bank0, blocks):
                chunk_ready(ch)
                whi, wlo = weights(ch.slot, KT)
                for j in range(2):
                    pe.wait_ge(freed[by], ch.freed + (j + 1))
                    for h in range(blocks):
                        b = blocks * j + h
                        tok = slice(b * 128, b * 128 + 128)
                        for k in range(KT):
                            last = three(ps[:, (bank0 + j) % 4, h * 256:h * 256 + 256],
                                         (a_hi[:, k, tok], a_lo[:, k, tok]), (whi[:, k, :], wlo[:, k, :]),
                                         k == 0, k == KT - 1)
                    last.then_inc(tile_done, 1)

            def token_major(name, previous, blocks=2):
                enter(name, previous)
                over_chunks(pe, G[name], lambda ch: token_chunk(ch, G[name].freed_by, 2 * ch.o, blocks))

            def down(name, previous, base, after=None):

                def body(ch):
                    chunk_ready(ch)
                    pe.wait_ge(hidden_split, ch.c + (base + 1))
                    whi, wlo = weights(ch.slot, 2)
                    done = down_done[int(base > 0)]
                    for j in (4, 5, 6, 7, 0, 1, 2, 3) if ch.first_of_gemm else range(8):
                        if ch.first_of_gemm and j == 0:
                            enter(name, previous)
                        for k in range(2):
                            cols = slice(j * 128, j * 128 + 128)
                            at = 2 * (ch.o % 2) + k
                            last = three(ps[:, j, :], (whi[:, k, cols], wlo[:, k, cols]),
                                         (a_hi[:, at, :], a_lo[:, at, :]), ch.first_of_gemm and k == 0,
                                         k == 1, across=True)
                        if ch.last_of_gemm:
                            last.then_inc(done, 1)
                            if after:
                                after(j)
                    if ch.last_of_gemm:
                        pe.wait_ge(done, 8)
                        pe.sem_inc(tile_done, 1)
                    else:
                        last.then_inc(tile_done, 1)
                over_chunks(pe, G[name], body)

            def by_token(of, first, last):
                for b in range(4):
                    at = pe.matmul(ps[:, 4, b:b + 1], of[:, b * 128:(b + 1) * 128], ones[:, 0:1],
                                   start=first and b == 0, stop=last, skip_group_check=True)
                return at

            def summed(norm):
                pe.wait_ge(norm.added, CREDIT + KT)
                by_token(square_sum, True, True).then_inc(norm.sum, 1)
                spread(norm)

            def sums(norm):
                def after(k):
                    pe.wait_ge(norm.sq, k + 1)
                    at = by_token(squares[:, k % 4, :], k == 0, k == KT - 1)
                    at.then_inc(norm.added if k < KT - 1 else norm.sum, 1)
                return after

            def spread(norm):
                pe.wait_ge(norm.diagonal, 1)
                last = pe.matmul(ps[:, 5, :], ones[:, :], diagonal, start=True, stop=True)
                last.then_inc(norm.spread, 1)

            def turn(t, tiles, src, blocks=4):
                for f in range(tiles):
                    if f >= 4:
                        pe.wait_ge(t.read, f - 3)
                    for b in range(blocks):
                        last = pe.transpose(ps[:, 4 + f % 4, b * 128:(b + 1) * 128], src(f, b), ident[:, :])
                    last.then_inc(t.turned, 1)

            def lead(units):
                def f(p, u):
                    n = units.number(p, u)
                    if u % 4 == 0:
                        pe.wait_ge(q_padded, units.padded(p, u // 4))
                    pe.wait_ge(probs_done, n + 1 - units.deep)
                    units.score(pe, p, u).then_inc(scores_done, 1)
                return f

            def turn_probs(units):
                def f(p, u):
                    n = units.number(p, u)
                    pe.wait_ge(probs_done, n + 1)
                    pe.wait_ge(turned_read, units.turn_free(n))
                    for b in range(units.keys(u) // 128):
                        last = pe.transpose(units.turned(u)[:, b * 128:(b + 1) * 128],
                                            units.probs(u)[:, b * 128:(b + 1) * 128], ident[:, :])
                    last.then_inc(turned, 1)
                return f

            def values(units):
                def f(p, u):
                    n = units.number(p, u)
                    pe.wait_ge(turned_read, n + 1)
                    pe.wait_ge(heads_done, n - 1)
                    blocks = units.keys(u) // 128
                    for b in range(blocks):
                        last = pe.matmul(ps[:, 2 + u % 2, 0:units.width], units.probs_t(u)[:, b * 128:(b + 1) * 128],
                                         units.value(p, u, b), start=b == 0, stop=b == blocks - 1)
                    last.then_inc(values_done, 1)
                return f

            def attention(units):
                units.pipeline(pe, lead=lead(units), turn=turn_probs(units), values=values(units))

            for s in (scores_done, turned, values_done, dil_mean):
                pe.sem_inc(s, CREDIT)
            pe.wait_ge(const_ready, 6)
            pe.wait_ge(vec_loaded, 20 * 16)
            for t in range(3):
                pe.transpose(ps[:, 0, t * 128:(t + 1) * 128], vec_rows[:, t, :], ident[:, :]).then_inc(vec_turned, 1)
            pe.wait_ge(x_ready, 4)

            def turn_tile(t, f, src, blocks=4):
                if f >= 4:
                    pe.wait_ge(t.read, f - 3)
                for b in range(blocks):
                    last = pe.transpose(ps[:, 4 + f % 4, b * 128:(b + 1) * 128], src(f, b), ident[:, :])
                last.then_inc(t.turned, 1)

            def turning(t, src, tiles=KT):
                for f in range(4):
                    turn_tile(t, f, src)

                def after(k):
                    if k + 4 < tiles:
                        turn_tile(t, k + 4, src)
                return after

            after = turning(turns["xs"], lambda f, b: x_scaled[:, b, f * 128:(f + 1) * 128])
            first = Chunk(G["forget"], 0, 2, 0)
            chunk_ready(first)
            pe.wait_ge(vec_ready, 1)
            whi, wlo = (w[:, 0, 0:HEADS * KT].rearrange("p (k n) -> p k n", k=KT) for w in (w_hi, w_lo))
            for k in range(KT):
                pe.wait_ge(turns["xs"].read, k + 1)
                last = three(ps[0:HEADS, 0, :], (whi[:, k, :], wlo[:, k, :]), (a_hi[:, k, :], a_lo[:, k, :]),
                             k == 0, k == KT - 1, across=True)
                if k == KT - 1:
                    last.then_inc(tile_done, 1)
                after(k)
            x_src = lambda f, b: x_tok[:, b, f * 128:(f + 1) * 128]
            for f in range(4):
                turn_tile(turns["x"], f, x_src)
            feature_major("fox_qk", "forget")
            for f in range(4, KT):
                turn_tile(turns["x"], f, x_src)
            token_major("fox_v", "fox_qk")
            feature_major("chunk_qk", "fox_v")
            token_major("chunk_v", "chunk_qk")
            pe.wait_ge(mem_scaled, 4)
            turn(turns["mem"], KT, lambda f, b: mem_tok[:, 2 * b + f // 4, f % 4 * 128:(f % 4 + 1) * 128], 2)
            enter("", "chunk_v")
            pe.wait_ge(decay_ready, 4)
            pe.wait_ge(turns["mem"].read, KT)
            attention(FOX)
            attention(CHUNKED)

            pe.wait_ge(heads_done, CREDIT + 64)
            feature_major("mem_k", "chunk_v", N_MEM)
            token_major("mem_v", "mem_k", 1)
            pe.wait_ge(heads_scaled, 8)
            after = turning(turns["mix"], lambda f, b: heads_1[:, b, f * 128:(f + 1) * 128])
            feature_major("mix_out", "mem_v", ready=turns["mix"].read, after=after)
            summed(norms["mix_post"])
            feature_major("mem_q", "mix_out", ready=norms["mem_pre"].ready)
            enter("", "mem_q")
            attention(MEMORY)
            pe.wait_ge(heads_done, CREDIT + 80)
            after = turning(turns["memo"], lambda f, b: heads_1[:, b, f * 128:(f + 1) * 128])
            feature_major("mem_o", "mem_q", ready=turns["memo"].read, after=after)
            summed(norms["mem_post"])
            feature_major("ffn_up", "mem_o", ready=norms["ffn_pre"].ready, tail=1)
            down("ffn_down", "ffn_up", 0)
            pe.wait_ge(freed_down, KT)
            summed(norms["ffn_post"])
            after = sums(norms["mixer_2"])
            for k in range(KT):
                after(k)
            spread(norms["mixer_2"])

            def head_mean(n, t):
                pe.wait_ge(dil_sq, n + 1)
                pe.matmul(ps[:, 4 + t % 2, :], mean_head[:, :], squares[:, t % 2, :], start=True, stop=True)\
                  .then_inc(dil_mean, 1)

            def dil_tiles(grp, c):
                ch = Chunk(G["dil_in"], grp, 6, c)
                if c >= 4:
                    token_chunk(ch, "dve", 2 * c, 2)
                    return
                if ch.first_of_gemm:
                    opening(ch, norms["mixer_2"].ready)
                    head_mean(0, 0)
                    return
                chunk_ready(ch)
                whi, wlo = weights(ch.slot, KT)
                for j in range(2):
                    t = 2 * c + j
                    pe.wait_ge(freed["dve"], ch.freed + (j + 1))
                    cols = slice(j * 128, j * 128 + 128)
                    for k in range(KT):
                        last = three(ps[:, t % 4, :], (whi[:, k, cols], wlo[:, k, cols]),
                                     (a_hi[:, k, :], a_lo[:, k, :]), k == 0, k == KT - 1)
                    last.then_inc(tile_done, 1)
                    if t >= 1:
                        head_mean(8 * grp + (t - 1), t - 1)
                if c == 3:
                    head_mean(8 * grp + 7, 7)

            dil_groups(pe, dil_tiles)
            enter("", "dil_in")
            pe.wait_ge(mask_ready, 9)
            attention(DILATED)
            pe.wait_ge(heads_done, CREDIT + 112)
            turning(turns["dil"], lambda f, b: heads_2[:, f, b * 128:(b + 1) * 128], 4)
            feature_major("dil_out", "dil_in", tiles=4, k_tiles=4, ready=turns["dil"].read)
            feature_major("conv_up", "dil_out", ready=norms["ffn_2"].ready, tail=1)

            def out_tile(f):
                pe.wait_ge(x_final, f + 1)
                for b in range(4):
                    last = pe.transpose(ps[:, f, b * 128:(b + 1) * 128], x_t[:, f, b * 128:(b + 1) * 128], ident[:, :])
                last.then_inc(out_turned, 1)

            down("conv_down", "conv_up", 11, lambda j: out_tile(j - 2) if j >= 2 else None)
            for f in (KT - 2, KT - 1):
                out_tile(f)


_INS = ["x", "mem", "g_mix_pre", "w_in", "b_fgate", "rel_bias", "g_fox_out", "g_chunk_out", "w_out", "g_mix_post",
        "g_mem_pre", "g_mem_kv", "w_mem_q", "w_mem_kv", "w_mem_o", "g_mem_post", "g_ffn_pre", "w_gate_up", "w_down",
        "g_ffn_post", "mixer_norm_2", "ffn_norm_2", "attn_w_in_2", "attn_q_gain_2", "attn_k_gain_2",
        "attn_w_out_2", "ffn_w_up_2", "ffn_conv_w_2", "ffn_conv_b_2", "ffn_w_down_2"]


def kernel(**inputs):
    import numpy as _np
    import concourse.bacc as _bacc
    from concourse import mybir as _mybir
    from concourse.bass_utils import run_bass_kernel_spmd as _run

    nc = _bacc.Bacc("TRN2", target_bir_lowering=False, num_devices=1)
    arrays, aps = {}, {}
    for name in _INS:
        a = _np.ascontiguousarray(inputs[name])
        arrays[f"in_{name}"] = a
        aps[name] = nc.dram_tensor(f"in_{name}", a.shape, _mybir.dt.from_np(a.dtype), kind="ExternalInput").ap()
    out = nc.dram_tensor("out_x", (1, S, D), _mybir.dt.float32, kind="ExternalOutput").ap()
    two_blocks_kernel(nc, aps, out)
    r = _run(nc, [arrays], core_ids=[0])
    return r.results[0]["out_x"]
```

```python
import concourse.bass as bass
from concourse import mybir
from contextlib import ExitStack

S = 512
D = 1024
KT = D // 128
N_MEM = 256
HEADS = 8
HW = 512
N_REL = 192
D_FF = 2816
FT = D_FF // 128
IN_COLS = 3080
EPS = 1e-6
NEG = -1e30
CHUNK = 2048
CREDIT = 4

GEMMS = [
    ("forget", 1, 1, 1, "act"),
    ("fox_qk", 4, 2, 2, "act"), ("fox_v", 2, 2, 2, "act"),
    ("chunk_qk", 4, 2, 2, "act"), ("chunk_v", 2, 2, 2, "act"),
    ("mem_k", 4, 2, 2, "act"), ("mem_v", 4, 2, 2, "act"),
    ("mix_out", 4, 2, 2, "act"),
    ("mem_q", 4, 2, 2, "dve"), ("mem_o", 4, 2, 2, "act"),
    ("ffn_up", 22, 2, 2, "dve"), ("ffn_down", 11, 1, 0, ""),
    ("dil_in", 18, 2, 2, "dve"), ("dil_out", 2, 4, 4, "dve"),
    ("conv_up", 22, 2, 2, "dve"), ("conv_down", 11, 1, 0, ""),
]


class Gemm:

    def __init__(self, name, chunks, signals, tiles, freed_by, chunk0, signal0, freed0):
        self.name, self.chunks, self.signals, self.tiles = name, chunks, signals, tiles
        self.freed_by, self.chunk0, self.signal0, self.freed0 = freed_by, chunk0, signal0, freed0
        self.signal_end = signal0 + chunks * signals
        self.freed_end = freed0 + chunks * tiles


def plan():
    gemms, chunk, signal, freed = {}, 0, 0, {"act": 0, "dve": 0, "": 0}
    for name, n, signals, tiles, by in GEMMS:
        gemms[name] = Gemm(name, n, signals, tiles, by, chunk, signal, freed[by])
        chunk, signal, freed[by] = chunk + n, signal + n * signals, freed[by] + n * tiles
    return gemms, chunk


class Chunk:

    def __init__(self, gemm, i, per, o):
        at = gemm.chunk0 + o
        self.gemm, self.o, self.slot_o = gemm, o, o % 2
        self.c, self.g = i * per + o, i * per + at
        self.slot, self.next_slot = at % 2, (at + 1) % 2
        self.next_loads = i * (per // 2 * 32) + ((at + 1) // 2 * 32 + 32)
        self.before = i * (per * gemm.signals) + (gemm.signal0 + o * gemm.signals)
        self.freed = i * (per * gemm.tiles) + (gemm.freed0 + o * gemm.tiles)
        self.first = isinstance(i, int) and self.g == 0
        self.first_of_gemm = isinstance(i, int) and self.c == 0
        self.second_of_gemm = isinstance(i, int) and self.c == 1
        self.last_of_gemm = isinstance(i, int) and self.c == gemm.chunks - 1
        self.last = self.last_of_gemm and gemm.name == GEMMS[-1][0]


def over_chunks(eng, gemm, body, peel=0, tail=0):
    odd = gemm.chunks % 2
    tail = tail or (odd and gemm.chunks > 1)
    if odd:
        body(Chunk(gemm, 0, 2, 0))
    for t in range(peel):
        for s in range(2):
            body(Chunk(gemm, t, 2, s + odd))
    turns = gemm.chunks // 2 - peel - tail
    if turns > 0:
        with eng.Fori(0, turns) as i:
            for s in range(2):
                body(Chunk(gemm, i, 2, s + odd + 2 * peel))
    for t in range(tail):
        for s in range(2):
            body(Chunk(gemm, turns + peel + t, 2, s + odd))


def pool_splits(ch):
    return ch.gemm.name == "dil_in" or (
        ch.gemm.name in ("mem_q", "ffn_up", "conv_up") and (ch.first_of_gemm or ch.second_of_gemm))


def two_blocks_kernel(nc, A, out):
    F, R = mybir.dt.float32, mybir.dt.float32r
    ALU, ACT, AX = mybir.AluOpType, mybir.ActivationFunctionType, mybir.AxisListType
    ds = bass.ds
    G, TOTAL = plan()

    def by_columns(w, width=256):
        return w.rearrange("(k p) (c n) -> c p k n", p=128, n=width)

    def by_rows(w):
        return w.rearrange("(c k p) n -> c p k n", p=128, k=2)

    def gate_and_up(w):
        return w.rearrange("(k p) (h c n) -> c p k h n", p=128, h=2, n=128)

    w_in, w_kv = A["w_in"][0], A["w_mem_kv"][0]
    fox_end = 3 * HW
    views = {
        "forget": by_columns(w_in[:, fox_end:fox_end + HEADS], HEADS),
        "fox_qk": by_columns(w_in[:, 0:2 * HW]),
        "fox_v": by_columns(w_in[:, 2 * HW:3 * HW]),
        "chunk_qk": by_columns(w_in[:, fox_end + HEADS:fox_end + HEADS + 2 * HW]),
        "chunk_v": by_columns(w_in[:, fox_end + HEADS + 2 * HW:IN_COLS]),
        "mix_out": by_columns(A["w_out"][0]),
        "mem_k": by_columns(w_kv[:, 0:D]), "mem_v": by_columns(w_kv[:, D:2 * D]),
        "mem_q": by_columns(A["w_mem_q"][0]), "mem_o": by_columns(A["w_mem_o"][0]),
        "ffn_up": gate_and_up(A["w_gate_up"][0]), "ffn_down": by_rows(A["w_down"][0]),
        "dil_in": by_columns(A["attn_w_in_2"][0]), "dil_out": by_columns(A["attn_w_out_2"][0], 512),
        "conv_up": gate_and_up(A["ffn_w_up_2"][0]), "conv_down": by_rows(A["ffn_w_down_2"][0]),
    }

    ctx = ExitStack()
    with ctx:
        def sb(name, shape, dt=F):
            return ctx.enter_context(nc.sbuf_tensor(name, shape, dt))

        def sem(name):
            return ctx.enter_context(nc.semaphore(name))

        raw = sb("raw", [128, 2, CHUNK])
        w_hi = sb("w_hi", [128, 2, CHUNK], R)
        w_lo = sb("w_lo", [128, 2, CHUNK], R)
        a_hi = sb("a_hi", [128, KT, S], R)
        a_lo = sb("a_lo", [128, KT, S], R)
        x_t = sb("x_t", [128, KT, S])
        arena = sb("arena", [128, 21504])
        work = sb("work", [128, 3072])
        masks = sb("masks", [128, 1152], R)
        ident = sb("ident", [128, 128])
        ident_r = sb("ident_r", [128, 128], R)
        sel_col = sb("sel_col", [128, HEADS])
        ones = sb("ones", [128, 128])
        mean_head = sb("mean_head", [128, 128])
        std = sb("std", [128, S])
        tok_std = sb("tok_std", [128, 4])
        tok_rstd = sb("tok_rstd", [128, 4])
        tok_eps_mean = sb("tok_eps_mean", [128, 4])
        rstd = sb("rstd", [128, S])
        mix_gain = sb("mix_gain", [128, KT])
        vec = sb("vec", [128, 3 * 128])
        gate_bias = sb("gate_bias", [8, 1])
        eps = sb("eps", [128, 1])
        x_sq = sb("x_sq", [128, 4])
        x_std = sb("x_std", [128, 4])
        x_rstd = sb("x_rstd", [128, 4])
        mem_sq = sb("mem_sq", [128, 4])
        mem_std = sb("mem_std", [128, 2])
        mem_rstd = sb("mem_rstd", [128, 2])
        ahead_of_root = sb("ahead_of_root", [128, 2])
        row_sq = sb("row_sq", [128, 8])
        row_std = sb("row_std", [128, 8])
        row_rstd = sb("row_rstd", [128, 8])
        neg_max = sb("neg_max", [128, 4])
        row_sum = sb("row_sum", [128, 4])
        row_recip = sb("row_recip", [128, 4])
        mod4 = sb("mod4", [128, 4])
        ps = ctx.enter_context(nc.psum_tensor("ps", [128, 8, 512], F))
        rel_dram = nc.dram_tensor("rel_dram", [HEADS, 640], F, kind="Internal").ap()

        def region(start, *shape):
            n = 1
            for d in shape:
                n *= d
            ap = arena[:, start:start + n]
            if len(shape) == 2:
                ap = ap.rearrange("p (a b) -> p a b", b=shape[1])
            return ap

        def slots(start, n, width):
            return work[:, start:start + n * width].rearrange("p (a b) -> p a b", b=width)

        def flat(start, n):
            return arena[:, ds(start, n)]

        def pair_of_hidden(c):
            return flat(c * (2 * S), 2 * S).rearrange("p (a n) -> p a n", a=2)

        QK_1, V_1, REL, HEADS_1, Y_1, MEM_K, MEM_V, MEM_Q, V_2 = (
            0, 8192, 12288, 16384, 4096, 0, 2048, 8192, 12288)
        v_1 = region(8192, 8, HW)
        rel = region(12288, HEADS, S)
        rel_rows = arena[0:HEADS, 12288:12288 + 640]
        rel_back = region(16384, HEADS, S)
        rel_pad = region(0, 2, S)
        causal_made = region(20864, 128)
        heads_1 = region(16384, 4, D)
        q_pad_1 = region(20480, 2, S)
        x_tok = region(16384, 4, D)
        x_scaled = region(0, 4, D)
        mem_tok = heads_1[:, :, HW:D]
        y_1 = region(4096, KT, S)
        mem_k = region(0, KT, N_MEM)
        mem_v = region(2048, 2, D)
        mem_q_pad = region(12288, 4, S)
        hidden = region(0, FT, S)
        y_ffn = region(12288, KT, S)
        gate_act = region(16384, 2, S)
        conv = region(17408, 4, S)
        up = region(19456, 4, S)
        v_2 = region(12288, 12, HW)
        q_pad_2 = region(18432, 4, S)
        heads_2 = region(0, 4, S)
        out_tok = region(12288, KT, S)
        decay = masks[:, 0:512]
        causal = masks[:, 512:640]
        sel_pad = masks[:, 640:896].rearrange("p (a n) -> p a n", a=2)
        decay_made = work[0:8, 0:S]
        band = masks[:, 0:896]
        stride_masks = masks[:, 896:1152]
        masks_made = region(14336, 1152)
        band_made, stride_made = masks_made[:, 0:896], masks_made[:, 896:1152]
        squares = slots(0, 4, S)
        square_sum = slots(4 * S, 1, S)[:, 0, :]
        diagonal = slots(5 * S, 1, S)[:, 0, :]
        eps_mean = square_sum
        x_squares = {"mem_pre": y_1, "ffn_pre": y_1, "mixer_2": y_ffn, "ffn_2": y_ffn}
        vec_rows = region(20480, 3, 128)

        raw_loaded = [sem("raw_loaded_0"), sem("raw_loaded_1")]
        weights_hi = sem("weights_hi")
        weights_split = sem("weights_split")
        tile_done = sem("tile_done")
        freed = {"act": sem("freed_by_act"), "dve": sem("freed_by_dve")}
        x_loaded = [sem(f"x_loaded_{b}") for b in range(4)]
        gain_loaded = sem("gain_loaded")
        x_squared, x_rooted, x_inverted, x_ready = (
            sem(n) for n in ("x_squared", "x_rooted", "x_inverted", "x_ready"))
        mem_loaded, vec_loaded, mem_step, mem_scaled = (
            sem(n) for n in ("mem_loaded", "vec_loaded", "mem_step", "mem_scaled"))
        rel_loaded, rel_stored, rel_spread = sem("rel_loaded"), sem("rel_stored"), sem("rel_spread")
        out_stored = sem("out_stored")
        const_step, const_ready, mask_step, mask_ready = (
            sem("const_step"), sem("const_ready"), sem("mask_step"), sem("mask_ready"))
        vec_cleared, vec_turned, vec_ready = sem("vec_cleared"), sem("vec_turned"), sem("vec_ready")
        gate_step, decay_ready = sem("gate_step"), sem("decay_ready")
        rel_row, rel_ready, rel_padded = sem("rel_row"), sem("rel_ready"), sem("rel_padded")
        bias_open = sem("bias_open")
        scores_done, max_done, probs_done, turned, turned_read, values_done, recip_done, heads_done = (
            sem(n) for n in ("scores_done", "max_done", "probs_done", "turned", "turned_read",
                             "values_done", "recip_done", "heads_done"))
        q_padded = sem("q_padded")
        packed_hi, packed_lo = sem("packed_hi"), sem("packed_lo")
        pad_cleared, pad_1_cleared, pad_2_cleared = sem("pad_cleared"), sem("pad_1_cleared"), sem("pad_2_cleared")
        row_step, heads_scaled = sem("row_step"), sem("heads_scaled")
        silu_done, gate_scaled, up_scaled = sem("silu_done"), sem("gate_scaled"), sem("up_scaled")
        rows_free = {n: sem(f"rows_free_{n}") for n in ("ffn_up", "conv_up")}
        x_added = {n: sem(f"x_added_{n}") for n in ("mix_post", "mem_post", "ffn_post")}
        hidden_written, hidden_hi, hidden_split = sem("hidden_written"), sem("hidden_hi"), sem("hidden_split")
        conv_base, conv_tap = sem("conv_base"), sem("conv_tap")
        dil_added = sem("dil_added")
        dil_sq, dil_mean, dil_std, dil_rstd, dil_written = (
            sem(n) for n in ("dil_sq", "dil_mean", "dil_std", "dil_rstd", "dil_written"))
        x_block2, x_final = sem("x_block2"), sem("x_final")
        freed_down, down_done = sem("freed_down"), [sem("down_done_1"), sem("down_done_2")]
        out_turned, out_copied = sem("out_turned"), sem("out_copied")

        class Norm:

            def __init__(self, n, more):
                self.sq, self.added, self.sum, self.std, self.inverse, self.spread = (
                    sem(f"{n}_{s}") for s in ("sq", "added", "sum", "std", "inverse", "spread"))
                self.value, self.rstd, self.hi, self.ready = (
                    sem(f"{n}_{s}") if s in more else None for s in ("value", "rstd", "hi", "ready"))

        norms = {n: Norm(n, ("value",)) for n in ("mix_post", "mem_post", "ffn_post")}
        norms.update({n: Norm(n, ("rstd", "hi", "ready")) for n in ("mem_pre", "ffn_pre", "mixer_2", "ffn_2")})

        class Turn:

            def __init__(self, n):
                self.turned, self.hi, self.read = sem(f"{n}_turned"), sem(f"{n}_hi"), sem(f"{n}_read")

        turns = {n: Turn(n) for n in ("x", "xs", "mem", "mix", "memo", "dil")}

        VEC = {"mix_pre": 0, "mix_post": 8, "mem_pre": 16, "mem_kv_pre": 24, "mem_post": 32, "ffn_pre": 40,
               "ffn_post": 48, "mixer_2": 56, "ffn_2": 64, "fox_out": 72, "chunk_out": 76, "conv_b": 80,
               "tap0": 128, "tap1": 172, "tap2": 256, "q_gain": 300, "k_gain": 303}

        def operand_tile(a, name, k):
            tile = a[:, k, :]
            return tile.rearrange("p (r j) -> p j r", r=4) if name == "mixer_2" else tile

        def in_order_of(name, tile):
            return tile.rearrange("p (j r) -> p j r", r=4) if name == "mixer_2" else tile

        def vcol(name, k):
            return vec[:, ds(k + VEC[name], 1)]

        class Units:

            def __init__(self, base, pads0, pads, pairs, width):
                self.base, self.pads0, self.pads, self.pairs, self.width = base, pads0, pads, pairs, width

            def number(self, p, u):
                return p * 8 + (self.base + u)

            def last(self, p):
                return isinstance(p, int) and p == self.pairs - 1

            def padded(self, p, half):
                return p * (2 * self.pads) + (self.pads0 + (half + 1) * self.pads)

            def keys(self, u):
                return (u % 4 + 1) * 128

            ahead, deep = 2, 4

            def scores(self, u):
                return ps[:, (4, 5, 0, 1)[u % 4], 0:self.keys(u)]

            def probs(self, u):
                return slots(0, 4, S)[:, u % 4, 0:self.keys(u)]

            def turned(self, u):
                return ps[:, 6 + u % 2, 0:self.keys(u)]

            def probs_t(self, u):
                return slots(4 * S, 2, S)[:, u % 2, 0:self.keys(u)]

            def turn_free(self, n):
                return n - 1

            def pipeline(self, eng, lead, turn=None, values=None):
                ahead = self.ahead

                def step(p, t, leads=True):
                    if leads:
                        lead(p + (t + ahead) // 8, (t + ahead) % 8)
                    if turn:
                        turn(p + t // 8, t % 8)
                    if values and t:
                        values(p + (t - 1) // 8, (t - 1) % 8)

                for u in range(ahead):
                    lead(0, u)
                step(0, 0)
                with eng.Fori(0, self.pairs - 1) as p:
                    for t in range(1, 9):
                        step(p, t)
                for t in range(1, 8):
                    step(self.pairs - 1, t, t < 8 - ahead)
                if values:
                    values(self.pairs - 1, 7)

        class Heads64(Units):

            def __init__(self, base, pads0, pads, q, v, out):
                super().__init__(base, pads0, pads, 4, 64)
                self.q, self.v, self.to = q, v, out

            def pad(self, dve, p, half):
                rows = slice(64 * half, 64 * half + 64)
                dve.tensor_scalar(q_pad_1[rows, half, :], arena[rows, ds(p * S + (QK_1 + self.q * S), S)], 0.125, None,
                                  ALU.mult).then_inc(q_padded, 1)
                if self.pads == 2:
                    dve.tensor_copy(sel_pad[:, half, :], sel_col[:, ds(p * 2 + half, 1)].to_broadcast([128, 128]))\
                       .then_inc(q_padded, 1)

            def score(self, pe, p, u):
                half, i, n = u // 4, u % 4, self.keys(u)
                last = pe.matmul(self.scores(u), q_pad_1[:, half, i * 128:(i + 1) * 128],
                          flat(p * S + (QK_1 + (self.q + 4) * S), n), start=True, stop=self.pads == 1)
                if self.pads == 1:
                    return last
                pe.matmul(self.scores(u), sel_pad[:, half, :], decay[:, 0:n], start=False, stop=False)
                return pe.matmul(self.scores(u)[:, n - 128:n], ident_r[:, :], causal, start=False, stop=True)

            def bias(self, u):
                return rel_pad[:, u // 4, (3 - u % 4) * 128:S]

            def value(self, p, u, b):
                return flat(p * 128 + (V_1 + (self.v + b) * HW + u // 4 * 64), 64)

            def out(self, p, u):
                return flat(p * 128 + (HEADS_1 + u % 4 * D + self.to + u // 4 * 64), 64)

        class MemoryHeads(Units):

            def keys(self, u):
                return N_MEM

            def pad(self, dve, p, half):
                dve.tensor_scalar(mem_q_pad[:, 2 * half:2 * half + 2, :],
                                  flat(p * (4 * S) + (MEM_Q + half * 2 * S), 2 * S).rearrange("p (a n) -> p a n", a=2),
                                  0.0625, None, ALU.mult).then_inc(q_padded, 1)

            def score(self, pe, p, u):
                half, i = u // 4, u % 4
                for k in range(2):
                    last = pe.matmul(self.scores(u), mem_q_pad[:, 2 * half + k, i * 128:(i + 1) * 128],
                                     flat(p * (4 * N_MEM) + (MEM_K + (2 * half + k) * N_MEM), N_MEM),
                                     start=k == 0, stop=k == 1)
                return last

            def value(self, p, u, b):
                return flat(p * 512 + (MEM_V + b * D + u // 4 * 256), 256)

            def out(self, p, u):
                return flat(p * 512 + (HEADS_1 + u % 4 * D + u // 4 * 256), 256)

        class Packed:

            def __init__(self, half):
                self.half = half
                self.own = slice(64 * half, 64 * half + 64)
                self.other = slice(64 - 64 * half, 128 - 64 * half)
                self.q, self.k_hi, self.k_lo = (a_hi[:, 3 * half + n, :] for n in range(3))

            def source(self, start):
                return arena[self.own, ds(start, S)]

            def hi(self, act, p, step):
                if step < 2:
                    act.activation(self.k_hi[self.own if step == 0 else self.other, :], self.source(p * S + 4 * S),
                                   ACT.Copy).then_inc(packed_hi, 1)
                else:
                    act.activation(self.q[self.own, :], self.source(p * S), ACT.Copy, scale=0.125)\
                       .then_inc(packed_hi, 1)

            def lo(self, dve, p):
                done = p * 6 + 3 * self.half
                dve.wait_ge(packed_hi, done + 1)
                for rows in (self.own, self.other):
                    dve.tensor_tensor(self.k_lo[rows, :], self.source(p * S + 4 * S), self.k_hi[self.own, :].bitcast(F),
                                      ALU.subtract).then_inc(packed_lo, 1)
                dve.wait_ge(packed_hi, done + 3)
                dve.scalar_tensor_tensor(out=self.q[self.other, :], in0=self.source(p * S), scalar=0.125,
                                         in1=self.q[self.own, :].bitcast(F), op0=ALU.mult, op1=ALU.subtract)\
                   .then_inc(packed_lo, 1)

            def score(self, pe, out, columns):
                pe.matmul(out, self.q[:, columns], self.k_hi, start=True, stop=False)
                return pe.matmul(out, self.q[:, columns], self.k_lo, start=False, stop=False)

        packed = [Packed(half) for half in range(2)]

        class DilatedHeads(Units):

            ahead, deep = 1, 2

            def keys(self, u):
                return 768

            def probs(self, u):
                return slots(0, 2, 768)[:, u % 2, :]

            def probs_t(self, u):
                return slots(1536, 2, 768)[:, u % 2, :]

            def scores(self, u):
                b = 4 * (1 - u % 2)
                return ps[:, b:b + 2, :].rearrange("p b n -> p (b n)")[:, 0:768]

            def turned(self, u):
                return ps[:, 6:8, :].rearrange("p b n -> p (b n)")[:, 0:768]

            def turn_free(self, n):
                return n

            def pad(self, dve, p, half):
                rows = slice(64 * half, 64 * half + 64)
                for g in (1, 2):
                    dve.tensor_scalar(q_pad_2[rows, 2 * half + g - 1, :], arena[rows, ds(p * S + 8 * g * S, S)], 0.125, None,
                                      ALU.mult).then_inc(q_padded, 1)

            def score(self, pe, p, u):
                half, r = u // 4, u % 4
                out, own = self.scores(u), slice(r * 128, (r + 1) * 128)
                pe.matmul(out[:, S:768], ident_r[:, :], stride_masks, start=True, stop=False)
                for g in (1, 2):
                    at = S + (g - 1) * 128
                    pe.matmul(out[:, at:at + 128], q_pad_2[:, 2 * half + g - 1, own],
                              flat(p * S + ((8 * g + 4) * S + r * 128), 128), start=False, stop=g == 2)
                if r == 0:
                    pe.wait_ge(packed_lo, p * 6 + (3 * half + 3))
                packed[half].score(pe, out[:, 0:S], own)
                return pe.matmul(out[:, 0:S], ident_r[:, :], band[:, (3 - r) * 128:(7 - r) * 128], start=False, stop=True)

            def value(self, p, u, b):
                tile = b if b < 4 else 4 * (b - 3) + u % 4
                return flat(p * 128 + (V_2 + tile * HW + u // 4 * 64), 64)

            def out(self, p, u):
                return flat(p * S + (u % 4 * 128 + u // 4 * 64), 64)

        FOX = Heads64(CREDIT, 0, 2, 0, 0, 0)
        CHUNKED = Heads64(CREDIT + 32, 16, 1, 8, 4, HW)
        MEMORY = MemoryHeads(CREDIT + 64, 24, 1, 2, 256)
        DILATED = DilatedHeads(CREDIT + 80, 28, 2, 4, 64)

        def dil_groups(eng, body):
            for c in range(6):
                body(0, c)
            with eng.Fori(1, 3) as grp:
                for c in range(6):
                    body(grp, c)

        block = ctx.enter_context(nc.Block())

        @block.sync
        def _(sp):
            def load_chunk(ch):
                sp.wait_ge(weights_split, ch.g + (CREDIT - 1))
                src = views[ch.gemm.name][ch.c]
                dst = raw[:, ch.slot, 0:HEADS * KT if ch.first else CHUNK]
                if len(src.shape) == 4:
                    dst = dst.rearrange("p (k h n) -> p k h n", k=KT, h=2)
                    halves = [(dst[:, :, h, :], src[:, :, h, :]) for h in range(2)]
                else:
                    k = src.shape[1]
                    dst = dst.rearrange("p (k n) -> p k n", k=k)
                    halves = [(dst[:, h * k // 2:(h + 1) * k // 2, :], src[:, h * k // 2:(h + 1) * k // 2, :])
                              for h in range(2)]
                for to, of in halves:
                    sp.dma_start(to, of).then_inc(raw_loaded[ch.slot], 16)

            def load_vectors():
                def rows(name, v):
                    n, at = v.shape[0] // 128, VEC[name]
                    sp.dma_start(vec_rows[at % 128:at % 128 + n, at // 128, :],
                                 v.rearrange("(a n) -> a n", n=128)).then_inc(vec_loaded, 16)

                sp.wait_ge(vec_cleared, 1)
                for name, key in (("mix_post", "g_mix_post"), ("mem_pre", "g_mem_pre"),
                                  ("mem_kv_pre", "g_mem_kv"), ("mem_post", "g_mem_post"), ("ffn_pre", "g_ffn_pre"),
                                  ("ffn_post", "g_ffn_post"), ("mixer_2", "mixer_norm_2"), ("ffn_2", "ffn_norm_2"),
                                  ("fox_out", "g_fox_out"), ("chunk_out", "g_chunk_out"), ("conv_b", "ffn_conv_b_2")):
                    rows(name, A[key][0])
                for tap in range(3):
                    rows(f"tap{tap}", A["ffn_conv_w_2"][0, tap])
                for name, key in (("q_gain", "attn_q_gain_2"), ("k_gain", "attn_k_gain_2")):
                    for half in range(2):
                        at = VEC[name]
                        sp.dma_start(vec_rows[at % 128:at % 128 + 3, at // 128, half * 64:half * 64 + 64],
                                     A[key][0]).then_inc(vec_loaded, 16)

            for b in range(4):
                sp.dma_start(x_tok[:, b, :], A["x"][0, b * 128:(b + 1) * 128, :]).then_inc(x_loaded[b], 16)
            for name, *_ in GEMMS:
                over_chunks(sp, G[name], load_chunk)
                if name == "forget":
                    sp.dma_start(rel_rows[:, 64:256], A["rel_bias"][0]).then_inc(rel_loaded, 16)
                if name == "fox_qk":
                    load_vectors()
            by_tile = out[0].rearrange("(b p) n -> p b n", p=128)
            for f in range(KT):
                sp.wait_ge(out_copied, f + 1)
                sp.dma_start(by_tile[:, :, f * 128:(f + 1) * 128],
                             out_tok[:, f, :].rearrange("p (b n) -> p b n", b=4)).then_inc(out_stored, 16)
            sp.wait_ge(out_stored, KT * 16)

        @block.gpsimd
        def _(pool):
            pool.memset(ident[:, :], 0.0).then_inc(const_step, 1)
            pool.memset(causal_made, 0.0).then_inc(const_step, 1)
            pool.memset(sel_col[:, :], 0.0).then_inc(const_step, 1)
            pool.memset(ones[:, :], 1.0).then_inc(const_ready, 1)
            for n in ("mix_post", "mem_post", "ffn_post"):
                pool.sem_inc(norms[n].added, CREDIT)
            pool.memset(decay.bitcast(F), 0.0).then_inc(const_ready, 1)
            pool.wait_ge(const_step, 3)
            pool.affine_select(out=ident[:, :], in_=ident[:, :], compare_op=ALU.not_equal, fill=1.0,
                               base=0, pattern=[[-1, 128]], channel_multiplier=1).then_inc(const_ready, 1)
            pool.affine_select(out=causal_made, in_=causal_made, compare_op=ALU.is_ge, fill=NEG,
                               base=0, pattern=[[-1, 128]], channel_multiplier=1).then_inc(const_ready, 1)
            pool.affine_select(out=sel_col[:, :], in_=sel_col[:, :], compare_op=ALU.not_equal, fill=-1.0,
                               base=0, pattern=[[-1, HEADS]], channel_multiplier=1).then_inc(const_step, 1)
            pool.wait_ge(const_step, 4)
            pool.affine_select(out=sel_col[:, :], in_=sel_col[:, :], compare_op=ALU.not_equal, fill=-1.0,
                               base=-32, pattern=[[-1, HEADS]], channel_multiplier=1).then_inc(const_ready, 1)
            pool.wait_ge(rel_row, 2)
            pool.dma_start(rel_dram, rel_rows).then_inc(rel_stored, 16)
            pool.wait_ge(rel_stored, 16)
            pool.wait_ge(turns["x"].turned, KT)
            pool.dma_start(rel_back, bass.AP(rel_dram.tensor, 0, [[1, 128], [640, HEADS], [1, S]]))\
                .then_inc(rel_spread, 16)
            pool.wait_ge(rel_spread, 16)
            pool.tensor_copy(rel, rel_back[:, :, ::-1]).then_inc(rel_row, 1)
            pool.wait_ge(rel_row, 3)
            pool.memset(rel[0:64, :, S - 64:S], NEG).then_inc(rel_ready, 1)
            pool.wait_ge(rel_ready, 1)
            for b in range(2):
                pool.dma_start(mem_tok[:, 2 * b:2 * b + 2, :],
                               A["mem"][0, b * 128:(b + 1) * 128, :].rearrange("p (h n) -> p h n", h=2))\
                    .then_inc(mem_loaded, 16)
            pool.wait_ge(vec_turned, 1)
            pool.memset(q_pad_1, 0.0).then_inc(pad_1_cleared, 1)
            pool.wait_ge(scores_done, CREDIT + 32)
            with pool.Fori(0, HEADS // 2) as p:
                for half in range(2):
                    pool.wait_ge(max_done, p * 8 + (CHUNKED.base + 4 * half - 4))
                    pool.tensor_copy(rel_pad[:, half, :], flat(p * (2 * S) + (REL + half * S), S))\
                        .then_inc(rel_padded, 1)
            pool.wait_ge(max_done, CREDIT + 64)
            pool.memset(masks_made, 0.0).then_inc(mask_step, 1)
            pool.wait_ge(mask_step, 1)
            pool.affine_select(out=band_made, in_=band_made, compare_op=ALU.is_ge, fill=NEG, base=3,
                               pattern=[[-1, 7], [-4, 128]], channel_multiplier=4).then_inc(mask_step, 1)
            pool.wait_ge(mask_step, 2)
            pool.affine_select(out=band_made, in_=band_made, compare_op=ALU.is_ge, fill=NEG, base=125,
                               pattern=[[1, 7], [4, 128]], channel_multiplier=-4).then_inc(mask_ready, 1)
            pool.affine_select(out=stride_made, in_=stride_made, compare_op=ALU.is_ge, fill=NEG, base=0,
                               pattern=[[0, 2], [-1, 128]], channel_multiplier=1).then_inc(mask_ready, 1)

            def sum_squares(norm, tiles=KT - 1):
                for k in range(tiles):
                    pool.wait_ge(norm.sq, k + 1)
                    if k == 0:
                        pool.tensor_copy(square_sum, squares[:, 0, :]).then_inc(norm.added, 1)
                    else:
                        pool.wait_ge(norm.added, CREDIT + k)
                        pool.tensor_tensor(square_sum, square_sum, squares[:, k % 4, :], ALU.add)\
                            .then_inc(norm.added, 1)

            def add_residual(name, y):
                pool.wait_ge(x_added[name], 2)
                for k in range(2, KT):
                    pool.wait_ge(norms[name].value, k + 1)
                    pool.tensor_tensor(x_t[:, k, :], x_t[:, k, :], y[:, k, :], ALU.add).then_inc(x_added[name], 1)

            def split_lo(ch):
                pool.wait_ge(weights_split, ch.g + (1 + CREDIT))
                pool.wait_ge(weights_hi, ch.g + 2)
                pool.tensor_tensor(w_lo[:, ch.next_slot, :], raw[:, ch.next_slot, :],
                                   w_hi[:, ch.next_slot, :].bitcast(F), ALU.subtract).then_inc(weights_split, 1)

            pool.wait_ge(mask_ready, 2)
            for name, y, gemm in (("mix_post", y_1, "mem_q"), ("mem_post", y_1, "ffn_up")):
                sum_squares(norms[name])
                split_lo(Chunk(G[gemm], 0, 2, 0))
                add_residual(name, y)
                split_lo(Chunk(G[gemm], 0, 2, 1))
            sum_squares(norms["ffn_post"], KT - 2)
            split_lo(Chunk(G["dil_in"], 0, 6, 0))
            add_residual("ffn_post", y_ffn)
            pool.memset(q_pad_2, 0.0).then_inc(pad_2_cleared, 1)
            for c in range(1, 6):
                split_lo(Chunk(G["dil_in"], 0, 6, c))
            with pool.Fori(1, 3) as grp:
                for c in range(6):
                    split_lo(Chunk(G["dil_in"], grp, 6, c))
            for c in range(2):
                split_lo(Chunk(G["conv_up"], 0, 2, c))

        @block.scalar
        def _(act):
            def split_hi(ch):
                act.wait_ge(raw_loaded[ch.next_slot], ch.next_loads)
                if not ch.first:
                    act.wait_ge(tile_done, ch.before)
                act.activation(w_hi[:, ch.next_slot, :], raw[:, ch.next_slot, :], ACT.Copy).then_inc(weights_hi, 1)

            def load_root(n):
                act.activation(ahead_of_root[:, n:n + 1], eps[:, :], ACT.Sqrt)

            def root_of(norm, src, scale=1.0 / D):
                act.wait_ge(norm.sum, 1)
                act.activation(tok_std[:, :], src, ACT.Sqrt, bias=eps[:, :], scale=scale).then_inc(norm.std, 1)

            def keep_rstd(norm):
                act.wait_ge(norm.spread, 1)
                act.activation(rstd[:, :], ps[:, 5, :], ACT.Copy).then_inc(norm.rstd, 1)

            def gained_hi(name, ready, tiles=range(KT)):
                norm = norms[name]
                for k in tiles:
                    act.wait_ge(ready, k + 1)
                    act.activation(operand_tile(a_hi, name, k), in_order_of(name, x_t[:, k, :]), ACT.Identity,
                                   scale=vcol(name, k)).then_inc(norm.hi, 1)
                    act.activation(x_squares[name][:, k, :], x_t[:, k, :], ACT.Square).then_inc(norm.sq, 1)

            def rstd_out(name, gemm):
                split_hi(Chunk(G[gemm], 0, 2, 1))
                root_of(norms[name], ps[:, 4, 0:4])
                keep_rstd(norms[name])

            def later_split_hi(ch):
                if not (ch.first_of_gemm or ch.second_of_gemm):
                    split_hi(ch)

            def turned_hi(turn, tiles, gain, columns):
                for f in range(tiles):
                    act.wait_ge(turn.turned, f + 1)
                    act.activation(columns(a_hi, f), ps[:, 4 + f % 4, :].rearrange("p (r j) -> p r j", r=4),
                                   ACT.Identity, scale=1.0 if gain is None else gain(f)).then_inc(turn.hi, 1)

            def gained_tiles(name):
                return lambda ch, j, src: act.activation(flat(ch.c * (2 * S) + (Y_1 + j * S), S), src, ACT.Identity,
                                                         scale=vcol(name, ch.c * 2 + j))

            def tiles_out(name, write, norm=None, split_ahead=False):
                def body(ch):
                    if not (split_ahead and ch.first_of_gemm) and not (split_ahead == 2 and ch.second_of_gemm):
                        split_hi(ch)
                    for j in range(2):
                        act.wait_ge(tile_done, ch.before + (j + 1))
                        if norm is not None:
                            tile = 2 * ch.c + j
                            act.wait_ge(norm.added, tile + (CREDIT - 3))
                            act.activation(squares[:, 2 * ch.o + j, :], ps[:, 2 * ch.o + j, :], ACT.Square)\
                               .then_inc(norm.sq, 1)
                        write(ch, j, ps[:, (ch.o * 2 + j) % 4, :]).then_inc(freed["act"], 1)
                over_chunks(act, G[name], body, peel=int(bool(split_ahead)))

            def feature_tiles(dst, first=0, tokens=S):
                return lambda ch, j, src: act.activation(
                    arena[:, ds(ch.c * (2 * tokens) + (dst + (first + j) * tokens), tokens)], src[:, 0:tokens], ACT.Copy)

            def token_tiles(dst, first):
                return lambda ch, j, src: act.activation(
                    dst[:, first + 2 * j:first + 2 * j + 2, ds(ch.c * 256, 256)],
                    src.rearrange("p (b n) -> p b n", b=2), ACT.Copy)

            def exps(units, p, u):
                n = units.number(p, u)
                act.wait_ge(max_done, n + 1)
                if units is CHUNKED:
                    act.wait_ge(recip_done, n - 3)
                    act.activation(units.probs(u), units.probs(u), ACT.Exp, scale=-1.0,
                                   bias=neg_max[:, u % 4:u % 4 + 1],
                                   accum_out=row_sum[:, u % 4:u % 4 + 1]).then_inc(probs_done, 1)
                    return
                act.wait_ge(turned, n + 1 - units.deep)
                act.wait_ge(recip_done, n - 3)
                act.activation(units.probs(u), units.scores(u), ACT.Exp, bias=neg_max[:, u % 4:u % 4 + 1],
                               accum_out=row_sum[:, u % 4:u % 4 + 1]).then_inc(probs_done, 1)

            def attention(units):
                def lead(p, u):
                    ahead = units is DILATED and u in (3, 7) and not units.last(p)
                    if ahead:
                        act.wait_ge(scores_done, units.number(p, u) + 1)
                        packed[u // 4].hi(act, p + 1, 0)
                    exps(units, p, u)
                    if ahead:
                        packed[u // 4].hi(act, p + 1, 1)
                        packed[u // 4].hi(act, p + 1, 2)

                if units is DILATED:
                    for half in range(2):
                        for step in range(3):
                            packed[half].hi(act, 0, step)
                units.pipeline(act, lead=lead)

            act.sem_inc(freed["act"], CREDIT)
            act.sem_inc(probs_done, CREDIT)
            act.dma_start(mix_gain[:, :], A["g_mix_pre"][0].rearrange("(k p) -> p k", p=128),
                          allow_slow_non_contiguous=True).then_inc(gain_loaded, 16)
            act.dma_start(gate_bias[:, :], A["b_fgate"][0].rearrange("(h a) -> h a", a=1),
                          allow_slow_non_contiguous=True).then_inc(gain_loaded, 16)

            for b in range(4):
                act.wait_ge(x_squared, b + 1)
                act.activation(x_std[:, b:b + 1], x_sq[:, b:b + 1], ACT.Sqrt, scale=1.0 / D, bias=eps[:, :])\
                   .then_inc(x_rooted, 1)
                act.wait_ge(x_inverted, b + 1)
                act.activation(x_scaled[:, b, :], x_tok[:, b, :], ACT.Copy, scale=x_rstd[:, b:b + 1]).then_inc(x_ready, 1)
            act.wait_ge(raw_loaded[0], 32)
            act.activation(w_hi[:, 0, 0:HEADS * KT], raw[:, 0, 0:HEADS * KT], ACT.Copy).then_inc(weights_hi, 1)
            straight = lambda a, f: a[:, f, :].rearrange("p (r j) -> p r j", r=4)
            act.wait_ge(gain_loaded, 32)
            turned_hi(turns["xs"], KT, lambda f: mix_gain[:, f:f + 1], straight)

            z, e, u_, ln = (work[0:8, a * S:(a + 1) * S] for a in range(4))
            first = Chunk(G["forget"], 0, 2, 0)
            split_hi(first)
            act.wait_ge(tile_done, 1)
            split_hi(Chunk(G["fox_qk"], 0, 2, 0))
            act.wait_ge(const_ready, 6)
            act.activation(ident_r[:, :], ident[:, :], ACT.Copy).then_inc(decay_ready, 1)
            act.activation(causal, causal_made, ACT.Copy).then_inc(decay_ready, 1)
            act.activation(z, ps[0:8, 0, :], ACT.Identity, bias=gate_bias[:, :]).then_inc(freed["act"], 1)
            act.wait_ge(freed["act"], CREDIT + 1)
            act.activation(e, z, ACT.Abs).then_inc(gate_step, 1)
            act.wait_ge(gate_step, 1)
            act.activation(e, e, ACT.Exp, scale=-1.0).then_inc(gate_step, 1)
            act.wait_ge(gate_step, 3)
            act.activation(ln, u_, ACT.Ln).then_inc(gate_step, 1)

            def x_out(tiles):
                for f in tiles:
                    act.wait_ge(turns["x"].turned, f + 1)
                    act.activation(x_t[:, f, :], ps[:, 4 + f % 4, :], ACT.Copy).then_inc(turns["x"].read, 1)

            x_out(range(4))
            tiles_out("fox_qk", feature_tiles(QK_1), split_ahead=True)
            act.wait_ge(gate_step, 12)
            act.activation(decay[0:8, :], decay_made, ACT.Copy).then_inc(decay_ready, 1)
            x_out(range(4, KT))
            act.wait_ge(vec_turned, 1)
            act.activation(vec[:, :], ps[:, 4, 0:384], ACT.Copy).then_inc(vec_ready, 1)
            tiles_out("fox_v", token_tiles(v_1, 0))
            tiles_out("chunk_qk", feature_tiles(QK_1, 8))
            act.wait_ge(mem_step, 5)
            act.activation(mem_std[:, :], mem_sq[:, 0:2], ACT.Sqrt, scale=1.0 / D, bias=eps[:, :]).then_inc(mem_step, 1)
            tiles_out("chunk_v", token_tiles(v_1, 4))
            for f in range(KT):
                act.wait_ge(turns["mem"].turned, f + 1)
                act.activation(a_hi[:, f, 0:N_MEM], ps[:, 4 + f % 4, 0:N_MEM], ACT.Identity,
                               scale=vcol("mem_kv_pre", f)).then_inc(turns["mem"].hi, 1)
            attention(FOX)
            attention(CHUNKED)

            tiles_out("mem_k", feature_tiles(MEM_K, tokens=N_MEM))
            split_hi(Chunk(G["mem_v"], 0, 2, 0))
            act.wait_ge(heads_done, CREDIT + 64)
            for b in range(4):
                for half in range(2):
                    n = 2 * b + half
                    if n >= 4:
                        act.wait_ge(row_step, n - 3)
                    act.activation(squares[:, n % 4, :], heads_1[:, b, half * HW:(half + 1) * HW], ACT.Square,
                                   accum_out=row_sq[:, n:n + 1]).then_inc(row_step, 1)
                    if n == 5:
                        split_hi(Chunk(G["mem_v"], 0, 2, 1))
            act.wait_ge(row_step, 8)
            act.activation(row_std[:, :], row_sq[:, :], ACT.Sqrt, scale=1.0 / HW, bias=eps[:, :]).then_inc(row_step, 1)
            tiles_out("mem_v", lambda ch, j, src: act.activation(mem_v[:, j, ds(ch.c * 256, 256)],
                                                                 src[:, 0:256], ACT.Copy), split_ahead=2)
            turned_hi(turns["mix"], KT, lambda f: vcol("fox_out", f), straight)
            tiles_out("mix_out", gained_tiles("mix_post"), norms["mix_post"])
            root_of(norms["mix_post"], ps[:, 4, 0:4])
            split_hi(Chunk(G["mem_q"], 0, 2, 0))
            gained_hi("mem_pre", x_added["mix_post"])
            rstd_out("mem_pre", "mem_q")
            over_chunks(act, G["mem_q"], later_split_hi, peel=1)
            attention(MEMORY)
            load_root(0)
            turned_hi(turns["memo"], KT, None, straight)
            tiles_out("mem_o", gained_tiles("mem_post"), norms["mem_post"])
            root_of(norms["mem_post"], ps[:, 4, 0:4])
            split_hi(Chunk(G["ffn_up"], 0, 2, 0))
            gained_hi("ffn_pre", x_added["mem_post"])
            rstd_out("ffn_pre", "ffn_up")

            def gate(ch):
                later_split_hi(ch)
                if ch.last_of_gemm:
                    first_rows_hi("ffn_up", CREDIT)
                act.wait_ge(gate_scaled, ch.c + 1)
                act.wait_ge(hidden_written, ch.c + (CREDIT - 1))
                act.activation(gate_act[:, ch.slot_o, :], up[:, 2 * ch.slot_o, :], ACT.Silu).then_inc(silu_done, 1)

            def rows_hi(ch):
                if not ch.last:
                    split_hi(ch)
                if not ch.last_of_gemm:
                    to = 2 * ((ch.o + 1) % 2)
                    act.activation(a_hi[:, to:to + 2, :], pair_of_hidden(ch.c + 1), ACT.Copy).then_inc(hidden_hi, 1)

            def first_rows_hi(gemm, written):
                act.wait_ge(hidden_written, written + 2)
                act.wait_ge(rows_free[gemm], 1)
                act.activation(a_hi[:, 0:2, :], hidden[:, 0:2, :], ACT.Copy).then_inc(hidden_hi, 1)

            act.wait_ge(mask_ready, 8)
            act.activation(masks[:, :], masks_made, ACT.Copy).then_inc(mask_ready, 1)
            over_chunks(act, G["ffn_up"], gate, peel=1, tail=1)
            load_root(1)
            act.wait_ge(hidden_written, CREDIT + FT)
            over_chunks(act, G["ffn_down"], rows_hi)
            act.wait_ge(mask_ready, 9)
            for k in range(KT):
                norm = norms["ffn_post"]
                act.wait_ge(down_done[0], k + 1)
                if k >= 4:
                    act.wait_ge(norm.added, CREDIT + k - 3)
                act.activation(squares[:, k % 4, :], ps[:, k, :], ACT.Square).then_inc(norm.sq, 1)
                act.activation(y_ffn[:, k, :], ps[:, k, :], ACT.Identity, scale=vcol("ffn_post", k)).then_inc(freed_down, 1)
            root_of(norms["ffn_post"], ps[:, 4, 0:4])
            split_hi(Chunk(G["dil_in"], 0, 6, 0))

            gained_hi("mixer_2", x_added["ffn_post"])
            split_hi(Chunk(G["dil_in"], 0, 6, 1))

            def mixer_norm_out():
                root_of(norms["mixer_2"], ps[:, 4, 0:4])
                act.wait_ge(norms["mixer_2"].spread, 1)
                act.activation(eps_mean, ps[:, 5, :], ACT.Copy).then_inc(norms["mixer_2"].rstd, 1)

            def dil_tiles(grp, c):
                def square(t):
                    n = 8 * grp + t
                    act.wait_ge(tile_done, ch.before + (t % 2 + 1))
                    act.wait_ge(dil_mean, n - 1 + CREDIT)
                    act.activation(squares[:, t % 2, :], ps[:, t % 4, :], ACT.Square).then_inc(dil_sq, 1)

                def root(t):
                    n = 8 * grp + t
                    act.wait_ge(dil_added, n + 1)
                    act.activation(std[:, :], std[:, :], ACT.Sqrt).then_inc(dil_std, 1)

                ch = Chunk(G["dil_in"], grp, 6, c)
                if not (ch.first_of_gemm or ch.second_of_gemm):
                    split_hi(ch)
                if ch.first_of_gemm:
                    square(0), square(1)
                    mixer_norm_out()
                elif ch.second_of_gemm:
                    square(2), root(0), square(3), root(1), root(2)
                elif c == 0:
                    square(0), square(1), root(0)
                elif c < 4:
                    square(2 * c), root(2 * c - 1), square(2 * c + 1), root(2 * c)
                elif c == 4:
                    root(7)

            dil_groups(act, dil_tiles)
            act.wait_ge(freed["dve"], CREDIT + G["dil_in"].freed0 + 8)
            act.wait_ge(tile_done, G["dil_in"].signal_end)
            attention(DILATED)
            strided = lambda a, f: a[:, 4 + f, :].rearrange("p (j r) -> p r j", r=4)
            turned_hi(turns["dil"], 4, None, strided)

            def wide(ch):
                split_hi(ch)
                if ch.c == 1:
                    gained_hi("ffn_2", x_block2, range(4))
            over_chunks(act, G["dil_out"], wide, peel=1)
            split_hi(Chunk(G["conv_up"], 0, 2, 0))
            gained_hi("ffn_2", x_block2, range(4, KT))
            rstd_out("ffn_2", "conv_up")

            def conv_gate(ch):
                later_split_hi(ch)
                if ch.last_of_gemm:
                    first_rows_hi("conv_up", 2 * CREDIT + FT)
                for j in range(2):
                    act.wait_ge(up_scaled, 2 * ch.c + (j + 1 + FT))
                    act.wait_ge(hidden_written, ch.c + (2 * CREDIT + FT - 1))
                    act.activation(conv[:, 2 * ch.slot_o + j, :], up[:, 2 * ch.slot_o + j, :], ACT.Identity,
                                   bias=vcol("conv_b", ch.c + j * FT), scale=vcol("tap2", ch.c + j * FT))\
                       .then_inc(conv_base, 1)
                act.wait_ge(conv_tap, 4 * ch.c + 2)
                act.activation(gate_act[:, ch.slot_o, :], conv[:, 2 * ch.slot_o, :], ACT.Silu).then_inc(silu_done, 1)

            over_chunks(act, G["conv_up"], conv_gate, peel=1, tail=1)
            act.wait_ge(hidden_written, 2 * CREDIT + 2 * FT)
            over_chunks(act, G["conv_down"], rows_hi)
            for f in range(KT):
                act.wait_ge(out_turned, f + 1)
                act.activation(out_tok[:, f, :], ps[:, f, :], ACT.Copy).then_inc(out_copied, 1)

        @block.vector
        def _(dve):
            def split_lo(ch):
                if pool_splits(ch):
                    return
                if ch.gemm.name in ("mem_q", "ffn_up", "dil_out", "conv_up"):
                    dve.wait_ge(weights_split, ch.g + (1 + CREDIT))
                dve.wait_ge(weights_hi, ch.g + 2)
                dve.tensor_tensor(w_lo[:, ch.next_slot, :], raw[:, ch.next_slot, :],
                                  w_hi[:, ch.next_slot, :].bitcast(F), ALU.subtract).then_inc(weights_split, 1)

            def invert(norm):
                dve.wait_ge(norm.std, 1)
                dve.reciprocal(tok_rstd[:, :], tok_std[:, :]).then_inc(norm.inverse, 1)
                dve.wait_ge(norm.inverse, 1)
                dve.tensor_tensor(diagonal.rearrange("p (b n) -> p b n", b=4),
                                  ident[:, :].rearrange("p (b n) -> p b n", b=1).to_broadcast([128, 4, 128]),
                                  tok_rstd[:, :].rearrange("p (b n) -> p b n", n=1).to_broadcast([128, 4, 128]),
                                  ALU.mult).then_inc(norm.inverse, 1)

            def invert_pre(name):
                dve.wait_ge(norms[name].sq, KT)
                dve.tensor_reduce(square_sum, x_squares[name].rearrange("p k n -> p n k"), axis=AX.X, op=ALU.add)\
                   .then_inc(norms[name].added, 1)
                if name != "mixer_2":
                    invert(norms[name])

            def invert_mixer(norm):
                dve.wait_ge(norm.std, 1)
                dve.tensor_scalar(tok_eps_mean[:, :], ps[:, 4, 0:4], EPS / D, EPS * EPS, ALU.mult, ALU.add)\
                   .then_inc(norm.inverse, 1)
                dve.wait_ge(norm.inverse, 1)
                dve.tensor_tensor(diagonal.rearrange("p (b n) -> p b n", b=4),
                                  ident[:, :].rearrange("p (b n) -> p b n", b=1).to_broadcast([128, 4, 128]),
                                  tok_eps_mean[:, :].rearrange("p (b n) -> p b n", n=1).to_broadcast([128, 4, 128]),
                                  ALU.mult).then_inc(norm.inverse, 1)
                dve.wait_ge(norm.std, 1)
                dve.reciprocal(tok_rstd[:, :], tok_std[:, :]).then_inc(norm.inverse, 1)

            def gained_lo(name, k):
                dve.wait_ge(norms[name].hi, k + 1)
                dve.scalar_tensor_tensor(out=operand_tile(a_lo, name, k), in0=in_order_of(name, x_t[:, k, :]),
                                         scalar=vcol(name, k), in1=operand_tile(a_hi, name, k).bitcast(F),
                                         op0=ALU.mult, op1=ALU.subtract)\
                   .then_inc(norms[name].ready, 1)

            def residual(name, y, after):
                norm = norms[name]
                invert(norm)
                dve.wait_ge(norm.spread, 1)

                def scale(k):
                    dve.tensor_tensor(y[:, k, :], y[:, k, :], ps[:, 5, :], ALU.mult).then_inc(norm.value, 1)

                def add(k):
                    dve.wait_ge(norm.value, k + 1)
                    dve.tensor_tensor(x_t[:, k, :], x_t[:, k, :], y[:, k, :], ALU.add).then_inc(x_added[name], 1)

                scale(0), add(0)
                scale(1), add(1)
                gained_lo(after, 0)
                scale(2)
                for k in range(1, KT):
                    if k + 2 < KT:
                        scale(k + 2)
                    gained_lo(after, k)

            def turned_lo(turn, tiles, gain, columns):
                for f in range(tiles):
                    dve.wait_ge(turn.hi, f + 1)
                    src = ps[:, 4 + f % 4, :].rearrange("p (r j) -> p r j", r=4)
                    hi = columns(a_hi, f).bitcast(F)
                    if gain is None:
                        dve.tensor_tensor(columns(a_lo, f), src, hi, ALU.subtract).then_inc(turn.read, 1)
                    else:
                        dve.scalar_tensor_tensor(out=columns(a_lo, f), in0=src, scalar=gain(f), in1=hi,
                                                 op0=ALU.mult, op1=ALU.subtract).then_inc(turn.read, 1)

            def splits(name, split_ahead=False):
                done = lambda ch: (split_ahead and ch.first_of_gemm) or (split_ahead == 2 and ch.second_of_gemm)
                over_chunks(dve, G[name], lambda ch: None if done(ch) else split_lo(ch), peel=int(bool(split_ahead)))

            def pad(units, p, half):
                units.pad(dve, p, half)

            def lead(units):
                def f(p, u):
                    n = units.number(p, u)
                    dve.wait_ge(scores_done, n + 1)
                    dve.wait_ge(probs_done, n - 3)
                    if units is CHUNKED:
                        dve.wait_ge(turned, n + 1 - units.deep)
                        if u % 4 == 0:
                            dve.wait_ge(rel_padded, p * 2 + (u // 4 + 1))
                        dve.sem_inc(bias_open, 1)
                        dve.tensor_tensor_reduce(out=units.probs(u), in0=units.scores(u),
                                                 in1=units.bias(u), scale=-1.0, scalar=3e38, op0=ALU.add,
                                                 op1=ALU.min, accum_out=neg_max[:, u % 4:u % 4 + 1])\
                           .then_inc(max_done, 1)
                        return
                    dve.tensor_reduce(neg_max[:, u % 4:u % 4 + 1], units.scores(u), axis=AX.X, op=ALU.max,
                                      negate=True).then_inc(max_done, 1)
                return f

            def turned_out(units):
                def f(p, u):
                    n = units.number(p, u)
                    dve.wait_ge(turned, n + 1)
                    dve.wait_ge(values_done, n - 1)
                    dve.tensor_copy(units.probs_t(u), units.turned(u)).then_inc(turned_read, 1)
                    if units is DILATED and isinstance(p, int) and p == 0:
                        pad(units, 0, 1)
                        packed[1].lo(dve, 0)
                return f

            def heads_out(units):
                def f(p, u):
                    n = units.number(p, u)
                    dve.wait_ge(probs_done, n + 1)
                    dve.reciprocal(row_recip[:, u % 4:u % 4 + 1], row_sum[:, u % 4:u % 4 + 1]).then_inc(recip_done, 1)
                    dve.wait_ge(recip_done, n + 1)
                    dve.wait_ge(values_done, n + 1)
                    dve.tensor_scalar(units.out(p, u), ps[:, 2 + u % 2, 0:units.width], row_recip[:, u % 4:u % 4 + 1],
                                      None, ALU.mult).then_inc(heads_done, 1)
                    if u % 4 == 2 - units.ahead and not units.last(p):
                        pad(units, p + 1, u // 4)
                    elif u % 4 == 2 - units.ahead and units is FOX:
                        pad(CHUNKED, 0, u // 4)
                    if units is DILATED and u % 4 == 2 and not units.last(p):
                        packed[u // 4].lo(dve, p + 1)
                return f

            def attention(units):
                if units is DILATED:
                    pad(units, 0, 0)
                    packed[0].lo(dve, 0)
                units.pipeline(dve, lead=lead(units), turn=turned_out(units), values=heads_out(units))

            dve.memset(vec_rows, 0.0).then_inc(vec_cleared, 1)
            dve.memset(eps[:, :], EPS).then_inc(const_ready, 1)
            dve.memset(mean_head[:, :], 0.0).then_inc(pad_cleared, 1)
            dve.wait_ge(pad_cleared, 1)
            dve.memset(mean_head[0:64, 0:64], 1.0 / 64).then_inc(pad_cleared, 1)
            dve.memset(mean_head[64:128, 64:128], 1.0 / 64).then_inc(pad_cleared, 1)
            dve.sem_inc(weights_split, CREDIT)
            dve.sem_inc(freed["dve"], CREDIT)
            dve.sem_inc(hidden_written, CREDIT)
            dve.sem_inc(dil_rstd, CREDIT)
            for s in (max_done, turned_read, recip_done, heads_done):
                dve.sem_inc(s, CREDIT)

            for b in range(4):
                dve.wait_ge(x_loaded[b], 16)
                dve.tensor_tensor_reduce(out=work[:, (b % 2) * D:(b % 2 + 1) * D], in0=x_tok[:, b, :], in1=x_tok[:, b, :],
                                         scale=1.0, scalar=0.0, op0=ALU.mult, op1=ALU.add,
                                         accum_out=x_sq[:, b:b + 1]).then_inc(x_squared, 1)
                dve.wait_ge(x_rooted, b + 1)
                dve.reciprocal(x_rstd[:, b:b + 1], x_std[:, b:b + 1]).then_inc(x_inverted, 1)
            dve.wait_ge(weights_hi, 1)
            dve.tensor_tensor(w_lo[:, 0, 0:HEADS * KT], raw[:, 0, 0:HEADS * KT], w_hi[:, 0, 0:HEADS * KT].bitcast(F),
                              ALU.subtract).then_inc(weights_split, 1)
            straight = lambda a, f: a[:, f, :].rearrange("p (r j) -> p r j", r=4)
            dve.wait_ge(gain_loaded, 32)
            turned_lo(turns["xs"], KT, lambda f: mix_gain[:, f:f + 1], straight)
            split_lo(Chunk(G["forget"], 0, 2, 0))

            split_lo(Chunk(G["fox_qk"], 0, 2, 0))

            z, e, u_, ln = (work[0:8, a * S:(a + 1) * S] for a in range(4))
            r, w = std[0:8, :], rstd[0:8, :]
            dve.wait_ge(gate_step, 2)
            dve.tensor_scalar(u_, e, 1.0, None, ALU.add).then_inc(gate_step, 1)
            dve.wait_ge(gate_step, 4)
            dve.tensor_scalar(r, u_, -1.0, None, ALU.add).then_inc(gate_step, 1)
            dve.wait_ge(gate_step, 5)
            dve.tensor_tensor(r, e, r, ALU.subtract).then_inc(gate_step, 1)
            dve.reciprocal(w, u_).then_inc(gate_step, 1)
            dve.wait_ge(gate_step, 7)
            dve.tensor_tensor(r, r, w, ALU.mult).then_inc(gate_step, 1)
            dve.wait_ge(gate_step, 8)
            dve.tensor_tensor(r, r, ln, ALU.add).then_inc(gate_step, 1)
            dve.wait_ge(gate_step, 9)
            dve.scalar_tensor_tensor(out=r, in0=z, scalar=0.0, in1=r, op0=ALU.min, op1=ALU.subtract)\
               .then_inc(gate_step, 1)
            dve.memset(w, 1.0).then_inc(gate_step, 1)
            dve.wait_ge(gate_step, 11)
            dve.tensor_tensor_scan(decay_made, w, r, 0.0, ALU.mult, ALU.add).then_inc(gate_step, 1)
            dve.wait_ge(rel_loaded, 16)
            dve.tensor_copy(rel_rows[:, 0:64], rel_rows[:, 64:65].to_broadcast([HEADS, 64])).then_inc(rel_row, 1)
            dve.tensor_copy(rel_rows[:, 256:640], rel_rows[:, 255:256].to_broadcast([HEADS, 384])).then_inc(rel_row, 1)

            splits("fox_qk", split_ahead=True)
            dve.wait_ge(decay_ready, 3)
            dve.tensor_tensor(decay[32:40, :], decay_made, decay[0:8, :].bitcast(F), ALU.subtract)\
               .then_inc(decay_ready, 1)
            splits("fox_v")
            splits("chunk_qk")
            dve.wait_ge(vec_ready, 1)
            dve.wait_ge(mem_loaded, 32)
            for n in range(4):
                dve.tensor_tensor_reduce(out=slots(0, 4, S)[:, n, :], in0=mem_tok[:, n, :], in1=mem_tok[:, n, :],
                                         scale=1.0, scalar=0.0, op0=ALU.mult, op1=ALU.add,
                                         accum_out=mem_sq[:, n:n + 1]).then_inc(mem_step, 1)
            dve.wait_ge(mem_step, 4)
            halves = mem_sq[:, :].rearrange("p (b h) -> p h b", h=2)
            dve.tensor_tensor(mem_sq[:, 0:2], halves[:, 0, :], halves[:, 1, :], ALU.add).then_inc(mem_step, 1)
            dve.wait_ge(mem_step, 6)
            dve.reciprocal(mem_rstd[:, :], mem_std[:, :]).then_inc(mem_step, 1)
            dve.wait_ge(mem_step, 7)
            for n in range(4):
                dve.tensor_scalar(mem_tok[:, n, :], mem_tok[:, n, :], mem_rstd[:, n // 2:n // 2 + 1], None,
                                  ALU.mult).then_inc(mem_scaled, 1)
            splits("chunk_v")
            dve.wait_ge(pad_1_cleared, 1)
            dve.wait_ge(freed["act"], CREDIT + G["fox_qk"].freed_end)
            for half in range(2):
                pad(FOX, 0, half)
            for f in range(KT):
                dve.wait_ge(turns["mem"].hi, f + 1)
                dve.scalar_tensor_tensor(out=a_lo[:, f, 0:N_MEM], in0=ps[:, 4 + f % 4, 0:N_MEM],
                                         scalar=vcol("mem_kv_pre", f), in1=a_hi[:, f, 0:N_MEM].bitcast(F),
                                         op0=ALU.mult, op1=ALU.subtract).then_inc(turns["mem"].read, 1)
            dve.wait_ge(freed["act"], CREDIT + G["chunk_v"].freed_end)
            dve.wait_ge(rel_ready, 1)
            attention(FOX)
            attention(CHUNKED)

            splits("mem_k")
            split_lo(Chunk(G["mem_v"], 0, 2, 0))
            split_lo(Chunk(G["mem_v"], 0, 2, 1))
            dve.wait_ge(row_step, 9)
            dve.reciprocal(row_rstd[:, :], row_std[:, :]).then_inc(row_step, 1)
            dve.wait_ge(row_step, 10)
            for b in range(4):
                for half in range(2):
                    n = 2 * b + half
                    part = heads_1[:, b, half * HW:(half + 1) * HW]
                    dve.tensor_scalar(part, part, row_rstd[:, n:n + 1], None, ALU.mult).then_inc(heads_scaled, 1)
            splits("mem_v", split_ahead=2)
            turned_lo(turns["mix"], KT, lambda f: vcol("fox_out", f), straight)
            splits("mix_out")
            dve.wait_ge(mask_ready, 2)
            dve.tensor_reduce(mod4[:, :], ident[:, :].rearrange("p (a b) -> p b a", b=4), axis=AX.X, op=ALU.add)\
               .then_inc(mask_ready, 1)
            dve.wait_ge(mask_ready, 3)
            dve.tensor_scalar(mod4[:, :], mod4[:, :], -1.0, -NEG, ALU.add, ALU.mult).then_inc(mask_ready, 1)
            dve.wait_ge(mask_ready, 4)
            for b in range(4):
                part = stride_made[:, 128:256].rearrange("p (a b) -> p b a", b=4)[:, b, :]
                dve.tensor_scalar(part, part, mod4[:, b:b + 1], None, ALU.add).then_inc(mask_ready, 1)
            residual("mix_post", y_1, "mem_pre")
            invert_pre("mem_pre")

            def mem_q_out(ch):
                if ch.first_of_gemm:
                    dve.wait_ge(norms["mem_pre"].rstd, 1)
                split_lo(ch)
                for j in range(2):
                    dve.wait_ge(tile_done, ch.before + (j + 1))
                    dve.tensor_tensor(flat(ch.c * (2 * S) + (MEM_Q + j * S), S), ps[:, 2 * ch.slot_o + j, :], rstd[:, :],
                                      ALU.mult).then_inc(freed["dve"], 1)
                if ch.second_of_gemm:
                    dve.wait_ge(freed["dve"], CREDIT + G["mem_q"].freed0 + 4)
                    for half in range(2):
                        pad(MEMORY, 0, half)
            over_chunks(dve, G["mem_q"], mem_q_out, peel=1)
            dve.wait_ge(freed["dve"], CREDIT + G["mem_q"].freed_end)
            attention(MEMORY)
            turned_lo(turns["memo"], KT, None, straight)
            splits("mem_o")
            residual("mem_post", y_1, "ffn_pre")
            invert_pre("ffn_pre")

            def scaled(ch, j, signal):
                dve.wait_ge(tile_done, ch.before + (j + 1))
                dve.tensor_tensor(up[:, 2 * ch.slot_o + j, :], ps[:, 2 * ch.slot_o + j, :], rstd[:, :],
                                  ALU.mult).then_inc(signal, 1)

            def gated(ch):
                if ch.first_of_gemm:
                    dve.wait_ge(norms["ffn_pre"].rstd, 1)
                split_lo(ch)
                if ch.last_of_gemm:
                    first_rows_lo(0)
                dve.wait_ge(hidden_written, ch.c + (CREDIT - 1))
                scaled(ch, 0, gate_scaled)
                scaled(ch, 1, up_scaled)
                dve.wait_ge(gate_scaled, ch.c + 1)
                dve.wait_ge(up_scaled, ch.c + 1)
                dve.sem_inc(freed["dve"], 2)
                dve.wait_ge(silu_done, ch.c + 1)
                dve.tensor_tensor(arena[:, ds(ch.c * S, S)], gate_act[:, ch.slot_o, :],
                                  up[:, 2 * ch.slot_o + 1, :], ALU.mult).then_inc(hidden_written, 1)

            def rows_lo(ch, base):
                if not ch.last:
                    split_lo(ch)
                if not ch.last_of_gemm:
                    to = 2 * ((ch.o + 1) % 2)
                    dve.wait_ge(hidden_hi, ch.c + (base + 2))
                    dve.tensor_tensor(a_lo[:, to:to + 2, :], pair_of_hidden(ch.c + 1),
                                      a_hi[:, to:to + 2, :].bitcast(F), ALU.subtract).then_inc(hidden_split, 1)

            def first_rows_lo(base):
                dve.wait_ge(hidden_hi, base + 1)
                dve.tensor_tensor(a_lo[:, 0:2, :], hidden[:, 0:2, :], a_hi[:, 0:2, :].bitcast(F),
                                  ALU.subtract).then_inc(hidden_split, 1)

            over_chunks(dve, G["ffn_up"], gated, peel=1, tail=1)
            over_chunks(dve, G["ffn_down"], lambda ch: rows_lo(ch, 0))
            residual("ffn_post", y_ffn, "mixer_2")
            invert_pre("mixer_2")
            invert_mixer(norms["mixer_2"])
            dve.wait_ge(norms["mixer_2"].rstd, 1)

            def dil_tiles(grp, c):
                ch = Chunk(G["dil_in"], grp, 6, c)
                for j in range(2):
                    if c < 4:
                        t, n = 2 * c + j, 8 * grp + (2 * c + j)
                        dve.wait_ge(dil_mean, n + 1 + CREDIT)
                        dve.wait_ge(dil_rstd, n + CREDIT)
                        dve.tensor_tensor(std[:, :], ps[:, 4 + t % 2, :], eps_mean, ALU.add).then_inc(dil_added, 1)
                        dve.wait_ge(dil_std, n + 1)
                        dve.wait_ge(freed["dve"], ch.freed + (j + CREDIT))
                        dve.reciprocal(rstd[:, :], std[:, :]).then_inc(dil_rstd, 1)
                        dve.wait_ge(dil_rstd, n + 1 + CREDIT)
                        dve.scalar_tensor_tensor(
                            out=arena[:, ds(n * S, S)], in0=ps[:, t % 4, :],
                            scalar=vcol("q_gain" if c < 2 else "k_gain", grp), in1=rstd[:, :],
                            op0=ALU.mult, op1=ALU.mult).then_inc(freed["dve"], 1)
                    else:
                        t = 2 * c + j
                        dve.wait_ge(tile_done, ch.before + (j + 1))
                        for b in range(2):
                            last = dve.tensor_scalar(v_2[:, 4 * grp + (2 * j + b), (c - 4) * 256:(c - 3) * 256],
                                                     ps[:, t % 4, b * 256:(b + 1) * 256],
                                                     tok_rstd[:, 2 * j + b:2 * j + b + 1], None, ALU.mult)
                        last.then_inc(freed["dve"], 1)
            dil_groups(dve, dil_tiles)
            dve.wait_ge(freed["dve"], CREDIT + G["dil_in"].freed_end)
            dve.wait_ge(pad_2_cleared, 1)
            attention(DILATED)
            turned_lo(turns["dil"], 4, None, lambda a, f: a[:, 4 + f, :].rearrange("p (j r) -> p r j", r=4))

            def wide(ch):
                split_lo(ch)
                if ch.c == 1:
                    for k in range(4):
                        gained_lo("ffn_2", k)
                for j in range(4):
                    dve.wait_ge(tile_done, ch.before + (j + 1))
                    xt = x_t[:, 4 * ch.c + j, :]
                    dve.tensor_tensor(xt, xt, ps[:, j, :], ALU.add).then_inc(x_block2, 1)
                    dve.wait_ge(x_block2, 4 * ch.c + (j + 1))
                    dve.sem_inc(freed["dve"], 1)
            over_chunks(dve, G["dil_out"], wide, peel=1)
            for k in range(4, KT):
                gained_lo("ffn_2", k)
            invert_pre("ffn_2")

            def convolved(ch):
                if ch.first_of_gemm:
                    dve.wait_ge(norms["ffn_2"].rstd, 1)
                split_lo(ch)
                if ch.last_of_gemm:
                    first_rows_lo(11)
                for j in range(2):
                    dve.wait_ge(hidden_written, ch.c + (2 * CREDIT + FT - 1))
                    scaled(ch, j, up_scaled)
                dve.wait_ge(up_scaled, 2 * ch.c + (2 + FT))
                dve.sem_inc(freed["dve"], 2)
                for j in range(2):
                    u, src = conv[:, 2 * ch.slot_o + j, :], up[:, 2 * ch.slot_o + j, :]
                    for tap in (1, 2):
                        if tap == 1:
                            dve.wait_ge(conv_base, 2 * ch.c + (j + 1))
                        else:
                            dve.wait_ge(conv_tap, 4 * ch.c + (2 * j + 1))
                        dve.scalar_tensor_tensor(out=u[:, tap:S], in0=src[:, 0:S - tap],
                                                 scalar=vcol(f"tap{2 - tap}", ch.c + j * FT), in1=u[:, tap:S],
                                                 op0=ALU.mult, op1=ALU.add).then_inc(conv_tap, 1)
                dve.wait_ge(conv_tap, 4 * ch.c + 4)
                dve.wait_ge(silu_done, ch.c + (FT + 1))
                dve.tensor_tensor(arena[:, ds(ch.c * S, S)], gate_act[:, ch.slot_o, :],
                                  conv[:, 2 * ch.slot_o + 1, :], ALU.mult).then_inc(hidden_written, 1)

            dve.wait_ge(hidden_written, CREDIT + FT)
            dve.sem_inc(hidden_written, CREDIT)
            over_chunks(dve, G["conv_up"], convolved, peel=1, tail=1)
            over_chunks(dve, G["conv_down"], lambda ch: rows_lo(ch, 11))
            for k in range(KT):
                dve.wait_ge(down_done[1], k + 1)
                dve.tensor_tensor(x_t[:, k, :], x_t[:, k, :], ps[:, k, :], ALU.add).then_inc(x_final, 1)

        @block.tensor
        def _(pe):
            def three(dst, stationary, moving, start, stop, across=False):
                (s_hi, s_lo), (m_hi, m_lo) = stationary, moving
                pe.matmul(dst, s_hi, m_hi, start=start, stop=False, skip_group_check=across)
                pe.matmul(dst, s_hi, m_lo, start=False, stop=False, skip_group_check=across)
                return pe.matmul(dst, s_lo, m_hi, start=False, stop=stop, skip_group_check=across)

            def weights(slot, k_tiles):
                return tuple(w[:, slot, :].rearrange("p (k n) -> p k n", k=k_tiles) for w in (w_hi, w_lo))

            def enter(name, previous):
                if previous and G[previous].freed_by:
                    pe.wait_ge(freed[G[previous].freed_by], CREDIT + G[previous].freed_end)

            def chunk_ready(ch):
                pe.wait_ge(weights_split, ch.g + 1 + CREDIT)

            def feature_chunk(ch, bank0, tokens=S, tiles=2, k_tiles=KT):
                first = KT - k_tiles
                by = ch.gemm.freed_by
                chunk_ready(ch)
                whi, wlo = weights(ch.slot, k_tiles)
                for j in range(tiles):
                    pe.wait_ge(freed[by], ch.freed + (j + 1))
                    cols = slice(j * 128, j * 128 + 128)
                    for k in range(k_tiles):
                        last = three(ps[:, (bank0 + j) % 4, 0:tokens], (whi[:, k, cols], wlo[:, k, cols]),
                                     (a_hi[:, first + k, 0:tokens], a_lo[:, first + k, 0:tokens]), k == 0, k == k_tiles - 1)
                        if ch.second_of_gemm and ch.gemm.name in deferred and j == 1 and k == 3:
                            spread(norms[deferred[ch.gemm.name]])
                    last.then_inc(tile_done, 1)
                    if ch.second_of_gemm and ch.gemm.name in deferred and j == 0:
                        norm = norms[deferred[ch.gemm.name]]
                        pe.wait_ge(norm.added, 1)
                        by_token(square_sum, True, True).then_inc(norm.sum, 1)

            deferred = {"mem_q": "mem_pre", "ffn_up": "ffn_pre", "conv_up": "ffn_2"}

            def closing(ch):
                chunk_ready(ch)
                whi, wlo = weights(ch.slot, KT)
                for k in range(KT):
                    for j in range(2):
                        if k == 0:
                            pe.wait_ge(freed[ch.gemm.freed_by], ch.freed + (j + 1))
                        cols = slice(j * 128, j * 128 + 128)
                        last = three(ps[:, 2 * ch.slot_o + j, :], (whi[:, k, cols], wlo[:, k, cols]),
                                     (a_hi[:, k, :], a_lo[:, k, :]), k == 0, k == KT - 1, across=True)
                        if k == KT - 1:
                            last.then_inc(tile_done, 1)
                    if k == 1:
                        last.then_inc(rows_free[ch.gemm.name], 1)

            def opening(ch, ready, after=None, tiles=2, k_tiles=KT):
                chunk_ready(ch)
                whi, wlo = weights(ch.slot, k_tiles)
                for k in range(k_tiles):
                    pe.wait_ge(ready, k + 1)
                    for j in range(tiles):
                        if k == 0:
                            pe.wait_ge(freed[ch.gemm.freed_by], ch.freed + (j + 1))
                        cols = slice(j * 128, j * 128 + 128)
                        at = KT - k_tiles + k
                        last = three(ps[:, j, :], (whi[:, k, cols], wlo[:, k, cols]), (a_hi[:, at, :], a_lo[:, at, :]),
                                     k == 0, k == k_tiles - 1, across=True)
                        if k == k_tiles - 1:
                            last.then_inc(tile_done, 1)
                    if after:
                        after(k)

            def feature_major(name, previous, tokens=S, tiles=2, k_tiles=KT, ready=None, after=None, tail=0):
                enter(name, previous)

                def body(ch):
                    if ch.first_of_gemm and ready is not None:
                        opening(ch, ready, after, tiles, k_tiles)
                    elif ch.last_of_gemm and tail:
                        closing(ch)
                    else:
                        feature_chunk(ch, ch.o * tiles, tokens, tiles, k_tiles)
                over_chunks(pe, G[name], body, int(ready is not None), tail)

            def token_chunk(ch, by, bank0, blocks, between=None):
                chunk_ready(ch)
                whi, wlo = weights(ch.slot, KT)
                for j in range(2):
                    pe.wait_ge(freed[by], ch.freed + (j + 1))
                    for h in range(blocks):
                        b = blocks * j + h
                        tok = slice(b * 128, b * 128 + 128)
                        for k in range(KT):
                            last = three(ps[:, (bank0 + j) % 4, h * 256:h * 256 + 256],
                                         (a_hi[:, k, tok], a_lo[:, k, tok]), (whi[:, k, :], wlo[:, k, :]),
                                         k == 0, k == KT - 1)
                    last.then_inc(tile_done, 1)
                    if between and j == 0:
                        between()

            def token_major(name, previous, blocks=2):
                enter(name, previous)
                over_chunks(pe, G[name], lambda ch: token_chunk(ch, G[name].freed_by, 2 * ch.o, blocks))

            def down(name, previous, base, after=None):

                def body(ch):
                    chunk_ready(ch)
                    pe.wait_ge(hidden_split, ch.c + (base + 1))
                    whi, wlo = weights(ch.slot, 2)
                    done = down_done[int(base > 0)]
                    for j in (4, 5, 6, 7, 0, 1, 2, 3) if ch.first_of_gemm else range(8):
                        if ch.first_of_gemm and j == 0:
                            enter(name, previous)
                        for k in range(2):
                            cols = slice(j * 128, j * 128 + 128)
                            at = 2 * (ch.o % 2) + k
                            last = three(ps[:, j, :], (whi[:, k, cols], wlo[:, k, cols]),
                                         (a_hi[:, at, :], a_lo[:, at, :]), ch.first_of_gemm and k == 0,
                                         k == 1, across=True)
                        if ch.last_of_gemm:
                            last.then_inc(done, 1)
                            if after:
                                after(j)
                    if ch.last_of_gemm:
                        pe.wait_ge(done, 8)
                        pe.sem_inc(tile_done, 1)
                    else:
                        last.then_inc(tile_done, 1)
                over_chunks(pe, G[name], body)

            def by_token(of, first, last, by_residue=False):
                for b in range(4):
                    part = of.rearrange("p (j r) -> p r j", r=4)[:, b, :] if by_residue else of[:, b * 128:(b + 1) * 128]
                    at = pe.matmul(ps[:, 4, b:b + 1], part, ones[:, 0:1],
                                   start=first and b == 0, stop=last, skip_group_check=True)
                return at

            def summed(norm):
                pe.wait_ge(norm.added, CREDIT + KT - 1)
                by_token(square_sum, True, False)
                pe.wait_ge(norm.sq, KT)
                by_token(squares[:, 3, :], False, True).then_inc(norm.sum, 1)
                spread(norm)

            def summed_late(norm):
                for k in (KT - 2, KT - 1):
                    pe.wait_ge(norm.sq, k + 1)
                    by_token(squares[:, k % 4, :], k == KT - 2, False)
                pe.wait_ge(norm.added, CREDIT + KT - 2)
                by_token(square_sum, False, True).then_inc(norm.sum, 1)
                spread(norm)

            def spread(norm):
                pe.wait_ge(norm.inverse, 2)
                last = pe.matmul(ps[:, 5, :], ones[:, :], diagonal, start=True, stop=True)
                last.then_inc(norm.spread, 1)

            def turn(t, tiles, src, blocks=4):
                for f in range(tiles):
                    if f >= 4:
                        pe.wait_ge(t.read, f - 3)
                    for b in range(blocks):
                        last = pe.transpose(ps[:, 4 + f % 4, b * 128:(b + 1) * 128], src(f, b), ident[:, :])
                    last.then_inc(t.turned, 1)

            def lead(units):
                def f(p, u):
                    n = units.number(p, u)
                    if u % 4 == 0:
                        pe.wait_ge(q_padded, units.padded(p, u // 4))
                    pe.wait_ge(probs_done, n + 1 - units.deep)
                    units.score(pe, p, u).then_inc(scores_done, 1)
                return f

            def turn_probs(units):
                def f(p, u):
                    n = units.number(p, u)
                    if units is FOX and isinstance(p, int) and p == 0:
                        pe.wait_ge(turns["mem"].read, KT)
                    pe.wait_ge(probs_done, n + 1)
                    pe.wait_ge(turned_read, units.turn_free(n))
                    for b in range(units.keys(u) // 128):
                        last = pe.transpose(units.turned(u)[:, b * 128:(b + 1) * 128],
                                            units.probs(u)[:, b * 128:(b + 1) * 128], ident[:, :])
                    last.then_inc(turned, 1)
                return f

            def values(units):
                def f(p, u):
                    n = units.number(p, u)
                    pe.wait_ge(turned_read, n + 1)
                    pe.wait_ge(heads_done, n - 1)
                    blocks = units.keys(u) // 128
                    for b in range(blocks):
                        last = pe.matmul(ps[:, 2 + u % 2, 0:units.width], units.probs_t(u)[:, b * 128:(b + 1) * 128],
                                         units.value(p, u, b), start=b == 0, stop=b == blocks - 1)
                    last.then_inc(values_done, 1)
                return f

            def attention(units):
                units.pipeline(pe, lead=lead(units), turn=turn_probs(units), values=values(units))

            for s in (scores_done, turned, values_done, dil_mean):
                pe.sem_inc(s, CREDIT)
            pe.wait_ge(const_ready, 6)
            pe.wait_ge(x_ready, 4)

            def turn_tile(t, f, src, blocks=4):
                if f >= 4:
                    pe.wait_ge(t.read, f - 3)
                for b in range(blocks):
                    last = pe.transpose(ps[:, 4 + f % 4, b * 128:(b + 1) * 128], src(f, b), ident[:, :])
                last.then_inc(t.turned, 1)

            def turning(t, src, tiles=KT):
                for f in range(4):
                    turn_tile(t, f, src)

                def after(k):
                    if k + 4 < tiles:
                        turn_tile(t, k + 4, src)
                return after

            after = turning(turns["xs"], lambda f, b: x_scaled[:, b, f * 128:(f + 1) * 128])
            first = Chunk(G["forget"], 0, 2, 0)
            chunk_ready(first)
            whi, wlo = (w[:, 0, 0:HEADS * KT].rearrange("p (k n) -> p k n", k=KT) for w in (w_hi, w_lo))
            for k in range(KT):
                pe.wait_ge(turns["xs"].read, k + 1)
                last = three(ps[0:HEADS, 0, :], (whi[:, k, :], wlo[:, k, :]), (a_hi[:, k, :], a_lo[:, k, :]),
                             k == 0, k == KT - 1, across=True)
                if k == KT - 1:
                    last.then_inc(tile_done, 1)
                after(k)
            x_src = lambda f, b: x_tok[:, b, f * 128:(f + 1) * 128]
            for f in range(4):
                turn_tile(turns["x"], f, x_src)
            feature_major("fox_qk", "forget")
            for f in range(4, KT):
                turn_tile(turns["x"], f, x_src)
            pe.wait_ge(vec_loaded, 18 * 16)
            pe.wait_ge(turns["x"].read, 5)
            for t in range(3):
                last = pe.transpose(ps[:, 4, t * 128:(t + 1) * 128], vec_rows[:, t, :], ident[:, :])
            last.then_inc(vec_turned, 1)
            token_major("fox_v", "")
            feature_major("chunk_qk", "")
            token_major("chunk_v", "")
            pe.wait_ge(mem_scaled, 4)
            turn(turns["mem"], KT, lambda f, b: mem_tok[:, 2 * b + f // 4, f % 4 * 128:(f % 4 + 1) * 128], 2)
            enter("", "chunk_v")
            pe.wait_ge(decay_ready, 4)
            pe.wait_ge(turns["mem"].read, 6)
            attention(FOX)
            attention(CHUNKED)

            pe.wait_ge(heads_done, CREDIT + 64)
            feature_major("mem_k", "chunk_v", N_MEM)
            token_major("mem_v", "", 1)
            pe.wait_ge(heads_scaled, 8)
            after = turning(turns["mix"], lambda f, b: heads_1[:, b, f * 128:(f + 1) * 128])
            feature_major("mix_out", "", ready=turns["mix"].read, after=after)
            summed(norms["mix_post"])
            feature_major("mem_q", "mix_out", ready=norms["mem_pre"].ready)
            enter("", "mem_q")
            attention(MEMORY)
            pe.wait_ge(heads_done, CREDIT + 80)
            after = turning(turns["memo"], lambda f, b: heads_1[:, b, f * 128:(f + 1) * 128])
            feature_major("mem_o", "mem_q", ready=turns["memo"].read, after=after)
            summed(norms["mem_post"])
            feature_major("ffn_up", "mem_o", ready=norms["ffn_pre"].ready, tail=1)
            down("ffn_down", "ffn_up", 0)
            pe.wait_ge(freed_down, 6)
            summed_late(norms["ffn_post"])
            def head_mean(n, t):
                pe.wait_ge(dil_sq, n + 1)
                if not (isinstance(n, int) and n < 2):
                    pe.wait_ge(dil_added, n - 1)
                pe.matmul(ps[:, 4 + t % 2, :], mean_head[:, :], squares[:, t % 2, :], start=True, stop=True)\
                  .then_inc(dil_mean, 1)

            def dil_tiles(grp, c):
                ch = Chunk(G["dil_in"], grp, 6, c)
                if c >= 4:
                    token_chunk(ch, "dve", 2 * c, 2, lambda: head_mean(8 * grp + 7, 7) if c == 4 else None)
                    return
                if ch.first_of_gemm:
                    opening(ch, norms["mixer_2"].ready)
                    return
                chunk_ready(ch)
                whi, wlo = weights(ch.slot, KT)
                for j in range(2):
                    t = 2 * c + j
                    pe.wait_ge(freed["dve"], ch.freed + (j + 1))
                    cols = slice(j * 128, j * 128 + 128)
                    for k in range(KT):
                        last = three(ps[:, t % 4, :], (whi[:, k, cols], wlo[:, k, cols]),
                                     (a_hi[:, k, :], a_lo[:, k, :]), k == 0, k == KT - 1)
                        if ch.second_of_gemm and j == 0 and k == 5:
                            pe.wait_ge(norms["mixer_2"].added, 1)
                            by_token(square_sum, True, True, by_residue=True).then_inc(norms["mixer_2"].sum, 1)
                    last.then_inc(tile_done, 1)
                    if ch.second_of_gemm and j == 0:
                        spread(norms["mixer_2"])
                        head_mean(0, 0)
                        continue
                    if ch.second_of_gemm:
                        pe.wait_ge(norms["mixer_2"].rstd, 1)
                        head_mean(1, 1)
                    if t >= 1:
                        head_mean(8 * grp + (t - 1), t - 1)

            dil_groups(pe, dil_tiles)
            enter("", "dil_in")
            pe.wait_ge(mask_ready, 9)
            attention(DILATED)
            pe.wait_ge(heads_done, CREDIT + 112)
            turning(turns["dil"], lambda f, b: heads_2[:, f, b * 128:(b + 1) * 128], 4)
            feature_major("dil_out", "dil_in", tiles=4, k_tiles=4, ready=turns["dil"].read)
            feature_major("conv_up", "dil_out", ready=norms["ffn_2"].ready, tail=1)

            def out_tile(f):
                pe.wait_ge(x_final, f + 1)
                for b in range(4):
                    last = pe.transpose(ps[:, f, b * 128:(b + 1) * 128], x_t[:, f, b * 128:(b + 1) * 128], ident[:, :])
                last.then_inc(out_turned, 1)

            down("conv_down", "conv_up", 11, lambda j: out_tile(j - 2) if j >= 2 else None)
            for f in (KT - 2, KT - 1):
                out_tile(f)


_INS = ["x", "mem", "g_mix_pre", "w_in", "b_fgate", "rel_bias", "g_fox_out", "g_chunk_out", "w_out", "g_mix_post",
        "g_mem_pre", "g_mem_kv", "w_mem_q", "w_mem_kv", "w_mem_o", "g_mem_post", "g_ffn_pre", "w_gate_up", "w_down",
        "g_ffn_post", "mixer_norm_2", "ffn_norm_2", "attn_w_in_2", "attn_q_gain_2", "attn_k_gain_2",
        "attn_w_out_2", "ffn_w_up_2", "ffn_conv_w_2", "ffn_conv_b_2", "ffn_w_down_2"]


def kernel(**inputs):
    import numpy as _np
    import concourse.bacc as _bacc
    from concourse import mybir as _mybir
    from concourse.bass_utils import run_bass_kernel_spmd as _run

    nc = _bacc.Bacc("TRN2", target_bir_lowering=False, num_devices=1)
    arrays, aps = {}, {}
    for name in _INS:
        a = _np.ascontiguousarray(inputs[name])
        arrays[f"in_{name}"] = a
        aps[name] = nc.dram_tensor(f"in_{name}", a.shape, _mybir.dt.from_np(a.dtype), kind="ExternalInput").ap()
    out = nc.dram_tensor("out_x", (1, S, D), _mybir.dt.float32, kind="ExternalOutput").ap()
    two_blocks_kernel(nc, aps, out)
    r = _run(nc, [arrays], core_ids=[0])
    return r.results[0]["out_x"]
```
